# Optimizing a Trainium2 kernel written in Bass

```python
import math
import jax, jax.numpy as jnp
from jax import lax
import numpy as np

D_MODEL = 1024
BATCH = 1
SEQ = 512
DEPTH = 2
DEC_BATCH = 8
DEC_SEQ = 16
PAST_LEN = 512

CHUNK = 64
Q_BLOCK = 128
ROPE_THETA = 10000.0
N_DIFF_HEADS = 8
DIFF_HEAD_DIM = 64
N_SWA_HEADS = 16
N_SWA_KV_HEADS = 2
SWA_GROUP = N_SWA_HEADS // N_SWA_KV_HEADS
SWA_HEAD_DIM = 64
SWA_WINDOW = 128
SWA_BAND = SWA_WINDOW // CHUNK
D_FF = 4 * D_MODEL
DIFF_Q = N_DIFF_HEADS * 2 * DIFF_HEAD_DIM
DIFF_K = N_DIFF_HEADS * 2 * DIFF_HEAD_DIM
DIFF_V = N_DIFF_HEADS * 2 * DIFF_HEAD_DIM
SWA_Q = N_SWA_HEADS * SWA_HEAD_DIM
SWA_KV = N_SWA_KV_HEADS * SWA_HEAD_DIM
SPLIT_POINTS = (DIFF_Q, DIFF_Q + DIFF_K, DIFF_Q + DIFF_K + DIFF_V,
                DIFF_Q + DIFF_K + DIFF_V + SWA_Q,
                DIFF_Q + DIFF_K + DIFF_V + SWA_Q + SWA_KV,
                DIFF_Q + DIFF_K + DIFF_V + SWA_Q + 2 * SWA_KV,
                DIFF_Q + DIFF_K + DIFF_V + SWA_Q + 2 * SWA_KV + D_MODEL)
D_IN = DIFF_Q + DIFF_K + DIFF_V + SWA_Q + 2 * SWA_KV + 2 * D_MODEL
ALPHA = (2 * DEPTH) ** 0.25
BETA = (8 * DEPTH) ** -0.25
LN_EPS = 1e-5
NEG = -1e30

kernel_name = 'hybrid_diffattn_swa_sink_streaming_step'

def rope(x, pos):
    half = x.shape[-1] // 2
    inv = ROPE_THETA ** (-jnp.arange(half, dtype=jnp.float32) / half)
    ang = pos.astype(jnp.float32)[:, None] * inv[None, :]
    shape = (1, pos.shape[0]) + (1,) * (x.ndim - 3) + (half,)
    cos = jnp.cos(ang).reshape(shape).astype(x.dtype)
    sin = jnp.sin(ang).reshape(shape).astype(x.dtype)
    x1, x2 = x[..., :half], x[..., half:]
    return jnp.concatenate([x1 * cos - x2 * sin, x2 * cos + x1 * sin], axis=-1)

def layer_norm(x, g, b):
    xf = x.astype(jnp.float32)
    mu = jnp.mean(xf, axis=-1, keepdims=True)
    var = jnp.mean(jnp.square(xf - mu), axis=-1, keepdims=True)
    return ((xf - mu) * lax.rsqrt(var + LN_EPS) * g + b).astype(x.dtype)

def sink_softmax(s, sink):
    sink_col = jnp.broadcast_to(sink.astype(jnp.float32), s.shape[:-1] + (1,))
    return jax.nn.softmax(jnp.concatenate([s, sink_col], axis=-1), axis=-1)[..., :-1]

def project_in(x, w, pos):
    B, T, _ = x.shape
    h = x @ w
    qd, kd, vd, qs, ks, vs, ga, gb = jnp.split(h, SPLIT_POINTS, axis=-1)
    qd = rope(qd.reshape(B, T, N_DIFF_HEADS, 2, DIFF_HEAD_DIM), pos)
    kd = rope(kd.reshape(B, T, N_DIFF_HEADS, 2, DIFF_HEAD_DIM), pos)
    vd = vd.reshape(B, T, N_DIFF_HEADS, 2 * DIFF_HEAD_DIM)
    qs = rope(qs.reshape(B, T, N_SWA_KV_HEADS, SWA_GROUP, SWA_HEAD_DIM), pos)
    ks = rope(ks.reshape(B, T, N_SWA_KV_HEADS, SWA_HEAD_DIM), pos)
    vs = vs.reshape(B, T, N_SWA_KV_HEADS, SWA_HEAD_DIM)
    return qd, kd, vd, qs, ks, vs, jax.nn.sigmoid(ga), jax.nn.sigmoid(gb)

def diff_attn_core(q, k, v, q_pos, k_pos, lam):
    s = jnp.einsum('bqhmd,bkhmd->bhmqk', q, k).astype(jnp.float32) * (DIFF_HEAD_DIM ** -0.5)
    visible = (k_pos[None, :] // CHUNK) <= (q_pos[:, None] // CHUNK)
    p = jax.nn.softmax(jnp.where(visible, s, NEG), axis=-1)
    a = p[:, :, 0] - lam * p[:, :, 1]
    return jnp.einsum('bhqk,bkhe->bqhe', a.astype(v.dtype), v)

def diff_post(o, g, lam_init):
    B, T = o.shape[:2]
    of = o.astype(jnp.float32)
    of = of * lax.rsqrt(jnp.mean(jnp.square(of), axis=-1, keepdims=True) + LN_EPS) * g * (1.0 - lam_init)
    return of.astype(o.dtype).reshape(B, T, DIFF_V)

def diff_attention_prompt(q, k, v, pos, lam):
    B, S = q.shape[:2]
    nblk = S // Q_BLOCK
    qb = q.reshape(B, nblk, Q_BLOCK, N_DIFF_HEADS, 2, DIFF_HEAD_DIM).swapaxes(0, 1)
    pb = pos.reshape(nblk, Q_BLOCK)
    o = lax.map(lambda a: diff_attn_core(a[0], k, v, a[1], pos, lam), (qb, pb))
    return o.swapaxes(0, 1).reshape(B, S, N_DIFF_HEADS, 2 * DIFF_HEAD_DIM)

def swa_attention_prompt(q, k, v, sinks):
    B, S = q.shape[:2]
    nc = S // CHUNK
    qc = q.reshape(B, nc, CHUNK, N_SWA_KV_HEADS, SWA_GROUP, SWA_HEAD_DIM)
    kc = k.reshape(B, nc, CHUNK, N_SWA_KV_HEADS, SWA_HEAD_DIM)
    vc = v.reshape(B, nc, CHUNK, N_SWA_KV_HEADS, SWA_HEAD_DIM)

    def shift(t, j):
        return jnp.pad(t, ((0, 0), (j, 0)) + ((0, 0),) * (t.ndim - 2))[:, :nc]

    shifts = range(SWA_BAND - 1, -1, -1)
    kb = jnp.concatenate([shift(kc, j) for j in shifts], axis=2)
    vb = jnp.concatenate([shift(vc, j) for j in shifts], axis=2)
    cidx = jnp.arange(nc)
    valid = jnp.concatenate([jnp.broadcast_to((cidx >= j)[:, None], (nc, CHUNK)) for j in shifts], axis=1)
    s = jnp.einsum('bcqhgd,bckhd->bchgqk', qc, kb).astype(jnp.float32) * (SWA_HEAD_DIM ** -0.5)
    s = jnp.where(valid[None, :, None, None, None, :], s, NEG)
    p = sink_softmax(s, sinks.reshape(N_SWA_KV_HEADS, SWA_GROUP)[None, None, :, :, None, None])
    o = jnp.einsum('bchgqk,bckhd->bcqhgd', p.astype(v.dtype), vb)
    return o.reshape(B, S, SWA_Q)

def swa_attention_sample(q, k, v, q_pos, k_pos, sinks):
    B, T = q.shape[:2]
    s = jnp.einsum('bqhgd,bkhd->bhgqk', q, k).astype(jnp.float32) * (SWA_HEAD_DIM ** -0.5)
    qc = q_pos[:, None] // CHUNK
    kc = k_pos[None, :] // CHUNK
    visible = (kc <= qc) & (kc > qc - SWA_BAND)
    s = jnp.where(visible, s, NEG)
    p = sink_softmax(s, sinks.reshape(N_SWA_KV_HEADS, SWA_GROUP)[None, :, :, None, None])
    o = jnp.einsum('bhgqk,bkhd->bqhgd', p.astype(v.dtype), v)
    return o.reshape(B, T, SWA_Q)

def finish_layer(x, a, b, ga, gb, w_a, w_b, w_o, g1, b1, w_up, w_down, g2, b2):
    mix = (ga * (a @ w_a) + gb * (b @ w_b)) @ w_o
    x = layer_norm(ALPHA * x + mix, g1, b1)
    h = jnp.square(jax.nn.relu(x @ w_up)) @ w_down
    return layer_norm(ALPHA * x + h, g2, b2)

def setup_inputs(seed: int = 0) -> dict:
    key = jax.random.key(seed)
    ks = jax.random.split(key, 24)

    def nrm(k, shape, scale):
        return jax.random.normal(k, shape, jnp.float32) * scale

    return {
        'x_prompt': nrm(ks[0], (BATCH, SEQ, D_MODEL), 1.0),
        'x_sample': nrm(ks[1], (DEC_BATCH, DEC_SEQ, D_MODEL), 1.0),
        'cache_diff_k': nrm(ks[2], (DEPTH, DEC_BATCH, PAST_LEN, N_DIFF_HEADS, 2, DIFF_HEAD_DIM), 1.0),
        'cache_diff_v': nrm(ks[3], (DEPTH, DEC_BATCH, PAST_LEN, N_DIFF_HEADS, 2 * DIFF_HEAD_DIM), 1.0),
        'cache_swa_k': nrm(ks[4], (DEPTH, DEC_BATCH, SWA_WINDOW, N_SWA_KV_HEADS, SWA_HEAD_DIM), 1.0),
        'cache_swa_v': nrm(ks[5], (DEPTH, DEC_BATCH, SWA_WINDOW, N_SWA_KV_HEADS, SWA_HEAD_DIM), 1.0),
        'w_in': nrm(ks[6], (DEPTH, D_MODEL, D_IN), D_MODEL ** -0.5),
        'diff_lambda_q1': nrm(ks[7], (DEPTH, DIFF_HEAD_DIM), 0.1),
        'diff_lambda_k1': nrm(ks[8], (DEPTH, DIFF_HEAD_DIM), 0.1),
        'diff_lambda_q2': nrm(ks[9], (DEPTH, DIFF_HEAD_DIM), 0.1),
        'diff_lambda_k2': nrm(ks[10], (DEPTH, DIFF_HEAD_DIM), 0.1),
        'diff_subln_g': 1.0 + nrm(ks[11], (DEPTH, 2 * DIFF_HEAD_DIM), 0.02),
        'swa_sinks': nrm(ks[12], (DEPTH, N_SWA_HEADS), 0.5),
        'w_branch_a': nrm(ks[13], (DEPTH, DIFF_V, D_MODEL), DIFF_V ** -0.5),
        'w_branch_b': nrm(ks[14], (DEPTH, SWA_Q, D_MODEL), SWA_Q ** -0.5),
        'w_o': nrm(ks[15], (DEPTH, D_MODEL, D_MODEL), BETA * D_MODEL ** -0.5),
        'ln1_g': 1.0 + nrm(ks[16], (DEPTH, D_MODEL), 0.02),
        'ln1_b': nrm(ks[17], (DEPTH, D_MODEL), 0.02),
        'w_up': nrm(ks[18], (DEPTH, D_MODEL, D_FF), D_MODEL ** -0.5),
        'w_down': nrm(ks[19], (DEPTH, D_FF, D_MODEL), BETA * D_FF ** -0.5),
        'ln2_g': 1.0 + nrm(ks[20], (DEPTH, D_MODEL), 0.02),
        'ln2_b': nrm(ks[21], (DEPTH, D_MODEL), 0.02),
    }

def reference(x_prompt, x_sample, cache_diff_k, cache_diff_v, cache_swa_k, cache_swa_v,
              w_in, diff_lambda_q1, diff_lambda_k1, diff_lambda_q2, diff_lambda_k2, diff_subln_g,
              swa_sinks, w_branch_a, w_branch_b, w_o, ln1_g, ln1_b, w_up, w_down, ln2_g, ln2_b):
    S = x_prompt.shape[1]
    T = x_sample.shape[1]
    past = cache_diff_k.shape[2]
    win = cache_swa_k.shape[2]
    pos_p = jnp.arange(S)
    pos_s = past + jnp.arange(T)
    diff_k_pos_s = jnp.concatenate([jnp.arange(past), pos_s])
    swa_k_pos_s = jnp.concatenate([jnp.arange(past - win, past), pos_s])
    xp, xs = x_prompt, x_sample
    dk_p, dv_p, sk_p, sv_p = [], [], [], []
    dk_s, dv_s, sk_s, sv_s = [], [], [], []
    for l in range(DEPTH):
        lam_init = 0.8 - 0.6 * math.exp(-0.3 * l)
        lam = (jnp.exp(jnp.sum(diff_lambda_q1[l].astype(jnp.float32) * diff_lambda_k1[l].astype(jnp.float32)))
               - jnp.exp(jnp.sum(diff_lambda_q2[l].astype(jnp.float32) * diff_lambda_k2[l].astype(jnp.float32)))
               + lam_init)
        g_sub = diff_subln_g[l].astype(jnp.float32)
        layer_w = (w_branch_a[l], w_branch_b[l], w_o[l], ln1_g[l], ln1_b[l], w_up[l], w_down[l], ln2_g[l], ln2_b[l])

        qd, kd, vd, qs, ks_, vs, ga, gb = project_in(xp, w_in[l], pos_p)
        a = diff_post(diff_attention_prompt(qd, kd, vd, pos_p, lam), g_sub, lam_init)
        b = swa_attention_prompt(qs, ks_, vs, swa_sinks[l])
        xp = finish_layer(xp, a, b, ga, gb, *layer_w)
        dk_p.append(kd)
        dv_p.append(vd)
        sk_p.append(ks_[:, S - SWA_WINDOW:])
        sv_p.append(vs[:, S - SWA_WINDOW:])

        qd, kd, vd, qs, ks_, vs, ga, gb = project_in(xs, w_in[l], pos_s)
        kfull = jnp.concatenate([cache_diff_k[l], kd], axis=1)
        vfull = jnp.concatenate([cache_diff_v[l], vd], axis=1)
        a = diff_post(diff_attn_core(qd, kfull, vfull, pos_s, diff_k_pos_s, lam), g_sub, lam_init)
        kwin = jnp.concatenate([cache_swa_k[l], ks_], axis=1)
        vwin = jnp.concatenate([cache_swa_v[l], vs], axis=1)
        b = swa_attention_sample(qs, kwin, vwin, pos_s, swa_k_pos_s, swa_sinks[l])
        xs = finish_layer(xs, a, b, ga, gb, *layer_w)
        dk_s.append(kd)
        dv_s.append(vd)
        sk_s.append(kwin[:, T:])
        sv_s.append(vwin[:, T:])

    return (xp, xs,
            jnp.stack(dk_p), jnp.stack(dv_p), jnp.stack(sk_p), jnp.stack(sv_p),
            jnp.stack(dk_s), jnp.stack(dv_s), jnp.stack(sk_s), jnp.stack(sv_s))


_drawn_inputs = setup_inputs


def setup_inputs(seed=0):
    import zlib

    import numpy as np

    out = dict(_drawn_inputs(seed))
    spreads = {}
    factors = {'diff_lambda_q1': 2.87,
     'diff_lambda_k1': 24.814,
     'diff_lambda_q2': 8.0,
     'diff_lambda_k2': 5.448,
     'diff_subln_g': 8.0,
     'swa_sinks': 27.413}
    for name, (base, spread) in spreads.items():
        noise = np.random.default_rng([zlib.crc32(name.encode()), seed]).standard_normal(out[name].shape)
        drawn = base * np.exp(spread * noise) if base else spread * noise
        out[name] = __import__('jax').numpy.asarray(drawn.astype(out[name].dtype))
    for name, factor in factors.items():
        out[name] = (out[name] * factor).astype(out[name].dtype)
    return out
```

```python
from contextlib import ExitStack

import concourse.bass as bass
from concourse import mybir

F32 = mybir.dt.float32
F32R = mybir.dt.float32r
BF16 = mybir.dt.bfloat16
ALU = mybir.AluOpType
ACT = mybir.ActivationFunctionType
AX_X = mybir.AxisListType.X

P = 128
D = 1024
KT = D // P
SEQ = 512
DEC_B = 8
DEC_T = 16
ROWS = SEQ + DEC_B * DEC_T
RT = ROWS // P
DEPTH = 2
CHUNK = 64
PAST = 512
HEADS = 8
DH = 64
PAIRS = 8
HALF = ROWS // 2
BANK = 512
FF_PARTS = 4
ALPHA = (2 * DEPTH) ** 0.25
EPS = 1e-5
QK_SCALE = DH ** -0.5
NEG = -1e30

V_CHUNKS, HEAD_CHUNKS, BRANCH_CHUNKS, O_CHUNKS = 8, 2 * HEADS, 2 * KT, 8
SWA_CHUNKS = 2 + PAIRS
FF_CHUNKS = FF_PARTS * 16
AT_V = 0
AT_HEADS = AT_V + V_CHUNKS
AT_BRANCH_A = AT_HEADS + HEAD_CHUNKS
AT_SWA = AT_BRANCH_A + BRANCH_CHUNKS
AT_BRANCH_B = AT_SWA + SWA_CHUNKS
AT_O = AT_BRANCH_B + BRANCH_CHUNKS
AT_FF = AT_O + O_CHUNKS
CHUNKS = AT_FF + FF_CHUNKS
RAW_SLOTS = 4

ROPES = 2 * HEADS + 1 + PAIRS
GROUPS = 2 + 2 + 2 * FF_PARTS

C_LAM_INIT = 0
C_ONE_MINUS = C_LAM_INIT + DEPTH
C_SUBLN = C_ONE_MINUS + DEPTH
C_ZERO = C_SUBLN + DEPTH
C_EPS = C_ZERO + 1
C_SINK = C_EPS + 1
C_END = C_SINK + DEPTH * PAIRS
MASK_COLS = 4 * P + 64 + P + 512


def build(nc, x_t, x_rows, k_cache, v_cache, swa_kc, swa_vc, swa_k_keep, swa_v_keep, weights, cols,
          lam_vec, ln_par, cos_t, sin_t, ident_d, ones_d, masks, x_all, k_out, v_out, swk_out,
          swv_out, swk_keep_out, swv_keep_out):
    ctx = ExitStack()
    with ctx:
        def sem(name):
            return ctx.enter_context(nc.semaphore(name))

        base = -(-nc.sbuf_base // 32) * 32
        total = 212480
        ctx.enter_context(nc.sbuf_tensor("arena", [P, (total + 32) // 4], F32))
        top = [base]

        def region(nbytes):
            at = top[0]
            top[0] += nbytes
            assert top[0] <= base + total
            return [at, at + nbytes]

        def at(where, name, shape, dt):
            t = nc.alloc_sbuf_tensor_at(name, [P, *shape], dt, offset=where[0])
            size = 2 if dt == BF16 else 4
            for n in shape:
                size *= n
            where[0] += -(-size // 32) * 32
            assert where[0] <= where[1], name
            return t

        WIDE = KT * ROWS * 4
        r_xt, r_a, r_b = region(2 * WIDE), region(2 * WIDE), region(2 * WIDE)
        r_rows, r_mix, r_w = region(WIDE), region(WIDE), region(32768)
        r_keep = region(base + total - top[0])

        xt_hi = at(r_xt, "xt_hi", [KT, ROWS], F32R)
        xt_lo = at(r_xt, "xt_lo", [KT, ROWS], F32R)
        rows = at(list(r_rows), "rows", [RT, D], F32)
        mix_a = at(list(r_mix), "mix_a", [KT, ROWS], F32)
        raw = at(r_w, "w_raw", [RAW_SLOTS, D], F32)
        w_hi = [at(r_w, f"w_hi{s}", [D], F32R) for s in range(2)]
        w_lo = [at(r_w, f"w_lo{s}", [D], F32R) for s in range(2)]
        cos = at(r_keep, "cos", [ROWS], F32)
        sin = at(r_keep, "sin", [ROWS], F32)
        rope_c = at(r_keep, "rope_c", [ROWS], F32)
        rope_s = at(r_keep, "rope_s", [ROWS], F32)
        ident = at(r_keep, "ident", [P], F32)
        ones = at(r_keep, "ones", [P], F32)
        mask_cols = at(r_keep, "mask_cols", [MASK_COLS], BF16)
        m_first, m_all = mask_cols[:, 0:P], mask_cols[:, P:2 * P]
        m_own = mask_cols[:, 2 * P:4 * P].rearrange("p (g n) -> p g n", g=2)
        m_neg64 = mask_cols[:, 4 * P:4 * P + 64]
        m_negnew = mask_cols[:, 4 * P + 64:5 * P + 64]
        m_negold = mask_cols[:, 5 * P + 64:MASK_COLS].rearrange("p (g n) -> p g n", g=2)
        col = at(r_keep, "col", [C_END], F32)
        neg_lam = at(r_keep, "neg_lam", [DEPTH], F32)
        g_sub = at(r_keep, "g_sub", [DEPTH], F32)
        small = at(r_keep, "small", [64], F32)
        tmp1, tmp2 = rope_c, rope_s

        ra = list(r_a)
        a_t = at(ra, "a_t", [KT, ROWS], F32)
        z_map = [[at(ra, f"z_map{p}{m}", [SEQ], F32) for m in range(2)] for p in range(2)]
        k_t = [at(ra, f"k_t{p}", [ROWS], F32) for p in range(2)]
        z_dec = at(ra, "z_dec", [DEC_B * P + 64 * 2], F32)
        d_a = at(list(ra), "d_a", [ROWS], F32)
        o_n = at(ra, "o_n", [4, P], F32)
        ra = list(r_a)
        sk_t = at(ra, "sk_t", [ROWS], F32)
        sk_dup = at(ra, "sk_dup", [2, ROWS], F32)
        sv_t = at(ra, "sv_t", [ROWS], F32)
        sv_rows = at(ra, "sv_rows", [8, P], F32)
        zq = [at(ra, f"zq{p}", [8, 2, 64], F32) for p in range(2)]
        zs = [at(ra, f"zs{p}", [2, P], F32) for p in range(2)]
        s_o = at(ra, "s_o", [10, DH], F32)
        ra = list(r_a)
        act_a = [at(ra, "act_a_hi", [KT, ROWS], F32R), at(ra, "act_a_lo", [KT, ROWS], F32R)]
        rb = list(r_b)
        kc = at(rb, "kc", [DEC_B, PAST], F32)
        vc = at(rb, "vc", [4, D], F32)
        d_o = at(rb, "d_o", [DEC_B, P], F32)
        d_at = at(rb, "d_at", [5, P], F32)
        d_on = at(rb, "d_on", [P], F32)
        d_out = at(rb, "d_out", [P], F32)
        d_rs = at(rb, "d_rs", [P], F32)
        rb = list(r_b)
        act_b = [at(rb, "act_b_hi", [KT, ROWS], F32R), at(rb, "act_b_lo", [KT, ROWS], F32R)]
        rm = list(r_mix)
        u_p = [at(rm, f"u_p{p}", [2, BANK], F32) for p in range(2)]
        u_a = [at(rm, f"u_a{p}", [BANK], F32) for p in range(2)]
        u_at = [at(rm, f"u_at{p}", [BANK], F32) for p in range(2)]
        d_t = at(list(rm), "d_t", [ROWS], F32)
        o_sq = at(list(rm), "o_sq", [4, P], F32)
        rm[0] += ROWS * 4
        z_all = at(rm, "z_all", [2, P], F32)
        d_sq = at(rm, "d_sq", [P], F32)
        d_p = at(list(r_mix), "d_p", [2, ROWS], F32)
        rm = list(r_mix)
        ln_g = at(rm, "ln_g", [D], F32)
        ln_b = at(rm, "ln_b", [D], F32)
        ln_x = [at(rm, f"ln_x{p}", [D], F32) for p in range(2)]
        rr = list(r_rows)
        s_p = at(rr, "s_p", [8 * P + 2 * 384], F32)
        s_pt = at(rr, "s_pt", [14, P], F32)
        s_kc = at(rr, "s_kc", [2, DEC_B, 64], F32)
        s_vc = at(rr, "s_vc", [4, P], F32)
        x_f = at(list(r_mix), "x_f", [KT, ROWS], F32)
        rr = list(r_rows)
        lam_v = at(rr, "lam_v", [DEPTH, 4, DH], F32)
        mask_f = at(rr, "mask_f", [MASK_COLS], F32)
        ln_st = at(r_keep, "ln_st", [RT, 2, 6], F32)
        ln_mv = at(r_keep, "ln_mv", [RT, 4], F32)
        d_nm, d_l, d_r = small[:, 0:2], small[:, 2:4], small[:, 4:6]
        u_nm = [small[:, 6:8], small[:, 8:10]]
        u_l = [small[:, 10:12], small[:, 12:14]]
        u_r = small[:, 14:16]
        o_ms, o_rs = small[:, 16:20], small[:, 20:24]
        s_nm, s_l, s_e = small[:, 24:34], small[:, 34:44], small[:, 44:54]
        lam2 = small[:, 54:58]

        PS = ctx.enter_context(nc.psum_tensor("PS", [P, 8, BANK], F32))
        flat = PS[:].rearrange("p b n -> p (b n)")

        def pair(which):
            return PS[:, 4 + 2 * which:6 + 2 * which, 0:HALF]

        def bank_of(which, half):
            return 4 + 2 * which + half

        def halves(t):
            return t.rearrange("p (a n) -> p a n", a=2)

        raw_loaded = [sem(f"raw_loaded{j}") for j in range(RAW_SLOTS)]
        w_hi_made = sem("w_hi_made")
        w_ready = [sem(f"w_ready{s}") for s in range(2)]
        chunk_done = [sem(f"chunk_done{s}") for s in range(2)]
        consts_loaded, x0_loaded, x0_copied = sem("consts_loaded"), sem("x0_loaded"), sem("x0_copied")
        lam_sum, lam_exp, lam_link = sem("lam_sum"), sem("lam_exp"), sem("lam_link")
        masks_ready = sem("masks_ready")
        x_hi_ready, x_lo_ready = sem("x_hi_ready"), sem("x_lo_ready")
        row_acc_ready = sem("row_acc_ready")
        row_evacuated = [sem(f"row_evacuated{r}") for r in range(RT)]
        v_stored = sem("v_stored")
        z_zeroed = sem("z_zeroed")
        rope_swapped, rope_cos_done = sem("rope_swapped"), sem("rope_cos_done")
        rope_sin_done, rope_added = sem("rope_sin_done"), sem("rope_added")
        k_stored = [sem(f"k_stored{p}") for p in range(2)]
        kc_loaded, vc_loaded = sem("kc_loaded"), sem("vc_loaded")
        dec_scores, dec_max, dec_exp = sem("dec_scores"), sem("dec_max"), sem("dec_exp")
        dec_recip, dec_r_ready = sem("dec_recip"), sem("dec_r_ready")
        dec_shifted, dec_probs = sem("dec_shifted"), sem("dec_probs")
        dec_t_ready, dec_t_copied = sem("dec_t_ready"), sem("dec_t_copied")
        dec_pv, dec_new_copied, dec_o_summed = sem("dec_pv"), sem("dec_new_copied"), sem("dec_o_summed")
        dec_ot_ready, dec_out_copied = sem("dec_ot_ready"), sem("dec_out_copied")
        dec_sq_ready, dec_ms_ready = sem("dec_sq_ready"), sem("dec_ms_ready")
        dec_ln_done, dec_rs_ready, dec_done = sem("dec_ln_done"), sem("dec_rs_ready"), sem("dec_done")
        unit_scores, unit_max, unit_exp = sem("unit_scores"), sem("unit_max"), sem("unit_exp")
        unit_recip, unit_r_ready = sem("unit_recip"), sem("unit_r_ready")
        unit_second, unit_probs = sem("unit_second"), sem("unit_probs")
        unit_t_ready, unit_t_copied, unit_pv = sem("unit_t_ready"), sem("unit_t_copied"), sem("unit_pv")
        o_sq_ready, o_ms_ready, o_ln_done = sem("o_sq_ready"), sem("o_ms_ready"), sem("o_ln_done")
        o_rs_ready, o_n_ready, o_t_ready = sem("o_rs_ready"), sem("o_n_ready"), sem("o_t_ready")
        a_done, a_hi_ready, a_lo_ready = sem("a_done"), sem("a_hi_ready"), sem("a_lo_ready")
        gate_ready, branch_taken = sem("gate_ready"), sem("branch_taken")
        mix_sum, mix_hi_ready, mix_ready = sem("mix_sum"), sem("mix_hi_ready"), sem("mix_ready")
        swa_cache_loaded, swa_k_dup = sem("swa_cache_loaded"), sem("swa_k_dup")
        swa_v_copied, swa_vt_ready, swa_v_ready = sem("swa_v_copied"), sem("swa_vt_ready"), sem("swa_v_ready")
        swa_stored, swa_zeroed = sem("swa_stored"), sem("swa_zeroed")
        swa_scores, swa_row_max, swa_max = sem("swa_scores"), sem("swa_row_max"), sem("swa_max")
        swa_exp, swa_sink_exp = sem("swa_exp"), sem("swa_sink_exp")
        swa_pt_ready, swa_pt_copied, swa_pv = sem("swa_pt_ready"), sem("swa_pt_copied"), sem("swa_pv")
        swa_sum, swa_recip, swa_o_ready = sem("swa_sum"), sem("swa_recip"), sem("swa_o_ready")
        swa_ot_ready, b_hi_ready, b_lo_ready = sem("swa_ot_ready"), sem("b_hi_ready"), sem("b_lo_ready")
        x_rows_loaded, ln_par_loaded = sem("x_rows_loaded"), sem("ln_par_loaded")
        ln_stats, ln_aggr, ln_log, ln_rstd = sem("ln_stats"), sem("ln_aggr"), sem("ln_log"), sem("ln_rstd")
        ln_normed, ln_scaled, ln_rows = sem("ln_normed"), sem("ln_scaled"), sem("ln_rows")
        ln_t_ready, resid_scaled = sem("ln_t_ready"), sem("resid_scaled")
        relu_done = [sem(f"relu_done{s}") for s in range(2)]
        sq_done, h_hi_ready, h_ready = sem("sq_done"), sem("h_hi_ready"), sem("h_ready")
        y_stored, keep_stored = sem("y_stored"), sem("keep_stored")
        waits_passed = sem("waits_passed")
        X0 = 1
        CONST_LOADS = 7

        block = ctx.enter_context(nc.Block())

        def nth(l, at_chunk, i=0):
            return l * (CHUNKS // 2) + (at_chunk // 2 + i)

        def norms_before(l, which):
            return l * (2 * RT) + (which * RT + X0)

        def transposed_outputs(dst, j):
            out = dst[:, j, :].rearrange("p (t u q) -> p t u q", t=RT, u=2)
            psum = flat[:, 1024:1024 + ROWS].rearrange("p (t g q) -> p t g q", t=RT, g=2)
            return [(out[g * DH:(g + 1) * DH, :, u, :], psum[u * DH:(u + 1) * DH, :, g, :])
                    for g in range(2) for u in range(2)]

        def all_heads(eng, l, head):
            with eng.Fori(0, HEADS // 2 - 1) as i:
                for p in range(2):
                    head(l, 2 * i + p, p, True)
            head(l, HEADS - 2, 0, True)
            head(l, HEADS - 1, 1, False)

        def all_pairs(eng, l, pair):
            with eng.Fori(0, PAIRS // 4) as i:
                for p in range(2):
                    pair(l, 0, i, p, True)
            for i in range(PAIRS // 4, PAIRS // 2):
                for p in range(2):
                    pair(l, 1, i, p, 2 * i + p < PAIRS - 1)

        def wait_apart(eng, semaphore, value):
            eng.wait_ge(semaphore, value)
            eng.sem_inc(waits_passed, 1)

        @block.sync
        def _(sp):
            sp.dma_start(x_f[:], x_t.rearrange("k p r -> p k r")).then_inc(x0_loaded, 16)
            loads = [(cos[:], cos_t), (sin[:], sin_t), (ident[:], ident_d), (ones[:], ones_d),
                     (col[:], cols), (lam_v[:].rearrange("p a b c -> p (a b c)"), lam_vec),
                     (mask_f[:], masks)]
            assert len(loads) == CONST_LOADS
            for dst, src in loads:
                sp.dma_start(dst, src).then_inc(consts_loaded, 16)

            def load(g, j):
                sp.dma_start(raw[:, j, :], weights[g * RAW_SLOTS + j]).then_inc(raw_loaded[j], 16)

            for j in range(RAW_SLOTS):
                load(0, j)
            sp.dma_start(x_all[0], x_rows).then_inc(x0_copied, 16)
            sp.dma_start(swk_keep_out, swa_k_keep).then_inc(keep_stored, 16)
            sp.dma_start(swv_keep_out, swa_v_keep).then_inc(keep_stored, 16)
            with sp.Fori(1, DEPTH * CHUNKS // RAW_SLOTS) as g:
                for j in range(RAW_SLOTS):
                    sp.wait_ge(w_ready[j % 2], 2 * g + (j // 2 - 1))
                    load(g, j)
            sp.wait_ge(keep_stored, 32)

        @block.gpsimd
        def _(pool):
            pool.wait_ge(consts_loaded, 16 * CONST_LOADS)
            with pool.Fori(0, DEPTH * CHUNKS // RAW_SLOTS) as g:
                for j in range(RAW_SLOTS):
                    s = j % 2
                    pool.wait_ge(raw_loaded[j], 16 * (g + 1))
                    pool.wait_ge(chunk_done[s], 2 * g + j // 2)
                    nc.gpsimd.tensor_tensor(w_hi[s][:], raw[:, j, :],
                                            col[:, C_ZERO:C_ZERO + 1].to_broadcast([P, D]),
                                            ALU.add).then_inc(w_hi_made, 1)
                    pool.wait_ge(w_hi_made, 4 * g + (j + 1))
                    nc.gpsimd.tensor_tensor(w_lo[s][:], raw[:, j, :], w_hi[s][:].bitcast(F32),
                                            ALU.subtract).then_inc(w_ready[s], 1)

        @block.tensor
        def _(pe):
            mm = nc.tensor.matmul

            def feature_tile(s, n, hi, lo, which, part=None, before_half=None):
                for half in (0, 1) if part is None else (part,):
                    if half == 0:
                        pe.wait_ge(w_ready[s], n + 1)
                    if before_half:
                        before_half(half)
                    out = PS[:, bank_of(which, half), 0:HALF]
                    c = slice(half * HALF, (half + 1) * HALF)
                    for k in range(KT):
                        wh, wl = w_hi[s][:, k * P:(k + 1) * P], w_lo[s][:, k * P:(k + 1) * P]
                        mm(out, wh, hi[:, k, c], start=(k == 0), stop=False)
                        mm(out, wh, lo[:, k, c], start=False, stop=False)
                        last = mm(out, wl, hi[:, k, c], start=False, stop=(k == KT - 1))
                    if half == 1:
                        last.then_inc(chunk_done[s], 1)

            def row_group(n, group, hi, lo, before_k=None):
                for k in range(KT):
                    s, k2 = (k // 2) % 2, k % 2
                    if k2 == 0:
                        pe.wait_ge(w_ready[s], n + (k // 4 + 1))
                    if before_k:
                        before_k(k)
                    wh = w_hi[s][:, k2 * BANK:(k2 + 1) * BANK]
                    wl = w_lo[s][:, k2 * BANK:(k2 + 1) * BANK]
                    for r in range(RT):
                        if k == 0:
                            pe.wait_ge(row_evacuated[r], group)
                        xh, xl = hi[:, k, r * P:(r + 1) * P], lo[:, k, r * P:(r + 1) * P]
                        mm(PS[:, r, :], xh, wh, start=(k == 0), stop=False)
                        mm(PS[:, r, :], xh, wl, start=False, stop=False)
                        last = mm(PS[:, r, :], xl, wh, start=False, stop=(k == KT - 1))
                        if r == RT - 1:
                            if k2 == 1:
                                last.then_inc(chunk_done[s], 1)
                        elif k == KT - 1:
                            last.then_inc(row_acc_ready, 1)

            def rope_pair_free(u):
                pe.wait_ge(rope_swapped, u)
                pe.wait_ge(rope_cos_done, u)

            def head_tile(l, h, is_k, part=None):
                if part in (None, 0):
                    rope_pair_free(l * ROPES + 2 * h + is_k)
                feature_tile(is_k, nth(l, AT_HEADS) + h, xt_hi, xt_lo, 0, part)

            def dec_scores_of(l, h, p):
                n = l * HEADS + h
                pe.wait_ge(rope_added, l * ROPES + 2 * h + 2)
                pe.wait_ge(kc_loaded, 16 * (n + 1))
                pe.wait_ge(dec_out_copied, n)
                pe.wait_ge(dec_ln_done, n)
                pe.wait_ge(a_done, n)
                for g in range(2):
                    old, new = PS[:, 2 * g, :], PS[:, 2 * g + 1, 0:P]
                    for b in range(4):
                        zb = z_dec[:, (4 * g + b) * P:(4 * g + b + 1) * P]
                        mm(old, zb, kc[:, 4 * g + b, :], start=(b == 0), stop=(b == 3))
                    mm(new, z_all[:, g, :], k_t[p][:, SEQ:ROWS], start=True, stop=False)
                    mm(new, m_own[:, g, :], m_negnew, start=False, stop=True).then_inc(dec_scores, 1)

            def dec_outputs(l, h):
                n = l * HEADS + h
                pe.wait_ge(dec_probs, 2 * n + 2)
                pe.wait_ge(unit_t_copied, 4 * n)
                pe.wait_ge(o_n_ready, n)
                for t in range(4):
                    last = nc.tensor.transpose(PS[:, 6, t * P:(t + 1) * P], d_a[:, t * P:(t + 1) * P],
                                               ident[:])
                last.then_inc(dec_t_ready, 1)
                nc.tensor.transpose(PS[:, 7, 0:P], d_a[:, SEQ:ROWS], ident[:]).then_inc(dec_t_ready, 1)
                pe.wait_ge(dec_t_copied, 2 * n + 2)
                pe.wait_ge(vc_loaded, 16 * (n + 1))
                for half in range(2):
                    for t in range(4):
                        mm(PS[:, 2 + half, :], d_at[:, t, :], vc[:, t, half * BANK:(half + 1) * BANK],
                           start=(t == 0), stop=(t == 3))
                mm(PS[:, 7, 2 * P:3 * P], d_at[:, 4, :], rows[:, RT - 1, bass.ts(h, P)],
                   start=True, stop=True).then_inc(dec_pv, 1)

            def unit_score(l, h, p, i):
                n, w = l * HEADS + h, (i + 1) * P
                if i == 1:
                    pe.wait_ge(dec_o_summed, n + 1)
                if i >= 2:
                    pe.wait_ge(unit_exp, 4 * n + (i - 1))
                for m in range(2):
                    out = PS[:, 2 * (i % 2) + m, :]
                    mm(out[:, 0:w], z_map[p][m][:, i * P:(i + 1) * P], k_t[p][:, 0:w],
                       start=True, stop=False)
                    last = mm(out[:, w - CHUNK:w], m_first, m_neg64, start=False, stop=True)
                last.then_inc(unit_scores, 1)

            def unit_transpose(l, h, i):
                n = 4 * (l * HEADS + h) + i
                pe.wait_ge(unit_probs, n + 1)
                pe.wait_ge(unit_t_copied, n)
                for j in range(i + 1):
                    last = nc.tensor.transpose(PS[:, 6, j * P:(j + 1) * P],
                                               u_a[i % 2][:, j * P:(j + 1) * P], ident[:])
                last.then_inc(unit_t_ready, 1)

            def unit_product(l, h, i):
                n = 4 * (l * HEADS + h) + i
                pe.wait_ge(unit_t_copied, n + 1)
                if i == 0:
                    pe.wait_ge(dec_new_copied, l * HEADS + h + 1)
                for j in range(i + 1):
                    last = mm(PS[:, 7, i * P:(i + 1) * P], u_at[i % 2][:, j * P:(j + 1) * P],
                              rows[:, j, bass.ts(h, P)], start=(j == 0), stop=(j == i))
                last.then_inc(unit_pv, 1)

            def head(l, h, p, more):
                n = l * HEADS + h
                dec_scores_of(l, h, p)
                if more:
                    head_tile(l, h + 1, 0)
                dec_outputs(l, h)
                unit_score(l, h, p, 0)
                unit_score(l, h, p, 1)
                if more:
                    head_tile(l, h + 1, 1, 0)
                for i in range(2):
                    unit_transpose(l, h, i)
                    unit_score(l, h, p, i + 2)
                    unit_product(l, h, i)
                pe.wait_ge(unit_exp, 4 * n + 3)
                pe.wait_ge(dec_o_summed, n + 1)
                for b in range(DEC_B):
                    last = nc.tensor.transpose(flat[:, b * P:(b + 1) * P], d_o[:, b, :], ident[:])
                last.then_inc(dec_ot_ready, 1)
                if more:
                    head_tile(l, h + 1, 1, 1)
                for i in range(2, 4):
                    unit_transpose(l, h, i)
                    unit_product(l, h, i)
                pe.wait_ge(dec_sq_ready, n + 1)
                mm(PS[:, 2, 0:P], ones[:], d_sq[:], start=True, stop=True).then_inc(dec_ms_ready, 1)
                pe.wait_ge(o_n_ready, n + 1)
                for i in range(4):
                    last = nc.tensor.transpose(PS[:, 3, i * P:(i + 1) * P], o_n[:, i, :], ident[:])
                last.then_inc(o_t_ready, 1)

            def pair_scores(l, kv, j, p):
                n = l * PAIRS + j
                pe.wait_ge(rope_added, l * ROPES + (2 * HEADS + 2) + j)
                pe.wait_ge(b_lo_ready, n)
                for c in range(SEQ // CHUNK):
                    ws = max(0, c - 1) * CHUNK
                    out = PS[:, c // 4, (c % 4) * P:(c % 4 + 1) * P]
                    zc = zq[p][:, c].rearrange("p g q -> p (g q)")
                    mm(out, zc, sk_dup[:, kv, ws:ws + P], start=True, stop=(c > 0))
                    if c == 0:
                        mm(out[:, CHUNK:P], m_all, m_neg64, start=False, stop=True)
                for g in range(2):
                    old, new = PS[:, 2 + g, 0:256], PS[:, 2 + g, 256:384]
                    keys = s_kc[:, kv, 4 * g:4 * g + 4, :].rearrange("p b k -> p (b k)")
                    mm(old, zs[p][:, g, :], keys, start=True, stop=False)
                    mm(old, m_own[:, g, :], m_negold[:, g, :], start=False, stop=True)
                    mm(new, zs[p][:, g, :], sk_dup[:, kv, SEQ:ROWS], start=True, stop=False)
                    last = mm(new, m_own[:, g, :], m_negnew, start=False, stop=True)
                last.then_inc(swa_scores, 1)

            def pair_output(l, kv, j):
                n = l * PAIRS + j
                pe.wait_ge(swa_exp, n + 1)
                for q in range(4):
                    bank = 6 + q % 2
                    if q >= 2:
                        pe.wait_ge(swa_pt_copied, 4 * n + (q - 1))
                    for t in range(4 * q, min(4 * q + 4, 14)):
                        last = nc.tensor.transpose(PS[:, bank, (t % 4) * P:(t % 4 + 1) * P],
                                                   s_p[:, t * P:(t + 1) * P], ident[:])
                    last.then_inc(swa_pt_ready, 1)
                pe.wait_ge(swa_pt_copied, 4 * n + 4)
                d = bass.ts(kv, DH)
                for c in range(SEQ // CHUNK):
                    window = 0 if c == 0 else c // 2 if c % 2 else 4 + c // 2 - 1
                    mm(flat[:, c * DH:(c + 1) * DH], s_pt[:, c, :], sv_rows[:, window, d],
                       start=True, stop=True)
                for g in range(2):
                    out = flat[:, (8 + g) * DH:(9 + g) * DH]
                    mm(out, s_pt[:, 8 + 3 * g, :], s_vc[:, 2 * g, d], start=True, stop=False)
                    mm(out, s_pt[:, 9 + 3 * g, :], s_vc[:, 2 * g + 1, d], start=False, stop=False)
                    last = mm(out, s_pt[:, 10 + 3 * g, :], sv_rows[:, 7, d], start=False, stop=True)
                last.then_inc(swa_pv, 1)
                pe.wait_ge(swa_o_ready, n + 1)
                for t in range(RT):
                    pair_o = s_o[:, 2 * t:2 * t + 2, :].rearrange("p u d -> p (u d)")
                    last = nc.tensor.transpose(flat[:, 1024 + t * P:1024 + (t + 1) * P], pair_o, ident[:])
                last.then_inc(swa_ot_ready, 1)

            def pair_tile(l, i, s):
                rope_pair_free(l * ROPES + (2 * HEADS + 1) + 2 * i + s)
                feature_tile(s, nth(l, AT_SWA, 1) + i, xt_hi, xt_lo, 0)

            def window_pair(l, kv, i, p, more):
                pair_scores(l, kv, 2 * i + p, p)
                if more:
                    pair_tile(l, i + p, 1 - p)
                pair_output(l, kv, 2 * i + p)

            def norm_transposes(l, which):
                for r in range(RT):
                    n = l * (2 * RT) + (which * RT + r)
                    pe.wait_ge(ln_rows, n + 1)
                    if r >= 2:
                        pe.wait_ge(x_lo_ready, n - 2 + X0 + 1)
                    for k in range(KT):
                        at_col = (r % 2) * 1024 + k * P
                        last = nc.tensor.transpose(flat[:, at_col:at_col + P],
                                                   rows[:, r, k * P:(k + 1) * P], ident[:])
                    last.then_inc(ln_t_ready, 1)

            pe.wait_ge(consts_loaded, 16 * CONST_LOADS)
            pe.wait_ge(masks_ready, 1)
            with pe.Fori(0, DEPTH) as l:
                pe.wait_ge(x_hi_ready, l * (2 * RT) + X0)
                wait_apart(pe, x_lo_ready, l * (2 * RT) + X0)
                with pe.Fori(0, 2) as v:
                    row_group(nth(l, AT_V) + 2 * v, l * GROUPS + v, xt_hi, xt_lo)
                pe.wait_ge(row_evacuated[RT - 1], l * GROUPS + 2)
                head_tile(l, 0, 0)
                head_tile(l, 0, 1)
                for r in range(RT):
                    wait_apart(pe, row_evacuated[r], l * GROUPS + 2)
                all_heads(pe, l, head)
                pe.wait_ge(rope_swapped, l * ROPES + 2 * HEADS)
                wait_apart(pe, rope_cos_done, l * ROPES + 2 * HEADS)
                with pe.Fori(0, KT) as f:
                    pe.wait_ge(gate_ready, l * 16 + f)
                    feature_tile(0, nth(l, AT_BRANCH_A) + f, xt_hi, xt_lo, 0)
                    pe.wait_ge(branch_taken, l * 16 + f)
                    pe.wait_ge(a_done, l * HEADS + HEADS)
                    pe.wait_ge(a_hi_ready, l * KT + KT)
                    pe.wait_ge(a_lo_ready, l * KT + KT)
                    feature_tile(1, nth(l, AT_BRANCH_A) + f, act_b[0], act_b[1], 1)
                pe.wait_ge(gate_ready, l * 16 + 8)
                feature_tile(0, nth(l, AT_SWA), xt_hi, xt_lo, 0)
                pe.wait_ge(branch_taken, l * 16 + 8)
                feature_tile(1, nth(l, AT_SWA), xt_hi, xt_lo, 1)
                pair_tile(l, 0, 0)
                pe.wait_ge(swa_v_copied, l + 1)
                for t in range(8):
                    first = t * P if t < 4 else (t - 4) * P + CHUNK if t < 7 else SEQ
                    last = nc.tensor.transpose(flat[:, t * P:(t + 1) * P], sv_t[:, first:first + P],
                                               ident[:])
                last.then_inc(swa_vt_ready, 1)
                pe.wait_ge(swa_v_ready, l + 1)
                pe.wait_ge(swa_k_dup, l + 1)
                wait_apart(pe, swa_cache_loaded, 32 * (l + 1))
                all_pairs(pe, l, window_pair)
                with pe.Fori(0, KT) as f:
                    pe.wait_ge(gate_ready, l * 16 + 8 + f)
                    rope_pair_free(l * ROPES + ROPES)
                    feature_tile(0, nth(l, AT_BRANCH_B) + f, xt_hi, xt_lo, 0)
                    pe.wait_ge(branch_taken, l * 16 + 8 + f)
                    pe.wait_ge(b_hi_ready, l * PAIRS + PAIRS)
                    pe.wait_ge(b_lo_ready, l * PAIRS + PAIRS)
                    pe.wait_ge(swa_pt_copied, 4 * PAIRS * (l + 1))
                    feature_tile(1, nth(l, AT_BRANCH_B) + f, act_b[0], act_b[1], 1)
                pe.wait_ge(gate_ready, l * 16 + 16)
                wait_apart(pe, branch_taken, l * 16 + 16)
                with pe.Fori(0, 2) as v:
                    row_group(nth(l, AT_O) + 2 * v, l * GROUPS + 2 + v, act_a[0], act_a[1],
                              lambda k: pe.wait_ge(mix_ready, l * KT + k + 1))
                norm_transposes(l, 0)
                with pe.Fori(0, FF_PARTS // 2) as i:
                    for p in range(2):
                        hidden = act_b if p == 0 else act_a
                        part = 2 * i + p
                        with pe.Fori(0, KT // 2) as u:
                            for s in range(2):
                                pe.wait_ge(relu_done[s], l * 16 + 4 * part + u)
                                if s == 0:
                                    pe.wait_ge(row_evacuated[RT - 1], l * GROUPS + 4 + 2 * part)
                                feature_tile(s, nth(l, AT_FF) + 8 * part + u, xt_hi, xt_lo, s,
                                             before_half=lambda half: (
                                                 pe.wait_ge(x_hi_ready, norms_before(l, 0) + (3, 5)[half]),
                                                 pe.wait_ge(x_lo_ready, norms_before(l, 0) + (3, 5)[half])))
                        wait_apart(pe, relu_done[0], l * 16 + 4 * part + 4)
                        with pe.Fori(0, 2) as v:
                            row_group(nth(l, AT_FF) + 8 * part + 4 + 2 * v, l * GROUPS + 4 + 2 * part + v,
                                      hidden[0], hidden[1],
                                      lambda k: pe.wait_ge(h_ready, l * 32 + 8 * part + k + 1))
                norm_transposes(l, 1)

        @block.scalar
        def _(act):
            fn = nc.scalar.activation

            def swap(l, u, acc_sem, n, scale):
                act.wait_ge(acc_sem, n + 1)
                act.wait_ge(rope_added, u)
                for a in range(0, P, DH):
                    for dst, src in ((a, a + DH // 2), (a + DH // 2, a)):
                        last = fn(halves(rope_s[dst:dst + 32, :]), pair(0)[src:src + 32], ACT.Copy,
                                  scale=scale)
                last.then_inc(rope_swapped, 1)

            def head_swap(l, h, is_k):
                swap(l, l * ROPES + 2 * h + is_k, chunk_done[is_k], nth(l, AT_HEADS) + h,
                     1.0 if is_k else QK_SCALE)

            def load_cache(kind, l, h):
                if kind == 0:
                    act.dma_start(kc[:].rearrange("p b k -> p (b k)"), k_cache[l, h]).then_inc(kc_loaded, 16)
                else:
                    act.dma_start(vc[:].rearrange("p t n -> p (t n)"), v_cache[l, h]).then_inc(vc_loaded, 16)

            def unit_exps(l, h, i):
                n, w = 4 * (l * HEADS + h) + i, (i + 1) * P
                act.wait_ge(unit_max, n + 1)
                for m in range(2):
                    last = fn(u_p[i % 2][:, m, 0:w], PS[:, 2 * (i % 2) + m, 0:w], ACT.Exp,
                              bias=u_nm[i % 2][:, m:m + 1], accum_out=u_l[i % 2][:, m:m + 1])
                last.then_inc(unit_exp, 1)

            def unit_copy(l, h, i):
                n, w = 4 * (l * HEADS + h) + i, (i + 1) * P
                act.wait_ge(unit_t_ready, n + 1)
                act.wait_ge(unit_pv, 4 * (l * HEADS + h) + max(0, i - 1))
                fn(u_at[i % 2][:, 0:w], PS[:, 6, 0:w], ACT.Copy).then_inc(unit_t_copied, 1)

            def head(l, h, p, more):
                n = l * HEADS + h
                for g in range(2):
                    act.wait_ge(dec_max, 2 * n + g + 1)
                    fn(d_p[:, g, :], flat[:, 1024 * g:1024 * g + ROWS], ACT.Exp,
                       bias=d_nm[:, g:g + 1], accum_out=d_l[:, g:g + 1]).then_inc(dec_exp, 1)
                act.dma_start(k_out[l, h], k_t[p][:]).then_inc(k_stored[p], 16)
                if more:
                    load_cache(0, l, h + 1)
                act.wait_ge(dec_r_ready, n + 1)
                fn(d_t[0:64], d_p[64:128, 0, :], ACT.Copy, scale=d_r[64:128, 0:1])
                fn(d_t[64:128], d_p[0:64, 1, :], ACT.Copy, scale=d_r[0:64, 1:2]).then_inc(dec_shifted, 1)
                if more:
                    head_swap(l, h + 1, 0)
                act.wait_ge(dec_t_ready, 2 * n + 1)
                fn(d_at[:, 0:4, :].rearrange("p t n -> p (t n)"), PS[:, 6, :], ACT.Copy)\
                    .then_inc(dec_t_copied, 1)
                act.wait_ge(dec_t_ready, 2 * n + 2)
                fn(d_at[:, 4, :], PS[:, 7, 0:P], ACT.Copy).then_inc(dec_t_copied, 1)
                act.wait_ge(dec_pv, n + 1)
                fn(d_on[:], PS[:, 7, 2 * P:3 * P], ACT.Copy).then_inc(dec_new_copied, 1)
                if more:
                    load_cache(1, l, h + 1)
                unit_exps(l, h, 0)
                unit_exps(l, h, 1)
                unit_copy(l, h, 0)
                unit_exps(l, h, 2)
                unit_copy(l, h, 1)
                unit_exps(l, h, 3)
                act.wait_ge(dec_ot_ready, n + 1)
                own = flat[:, 0:1024].rearrange("p (b c) -> p b c", b=DEC_B)
                for b in range(DEC_B):
                    last = fn(d_out[:, b * DEC_T:(b + 1) * DEC_T], own[:, b, b * DEC_T:(b + 1) * DEC_T],
                              ACT.Copy)
                last.then_inc(dec_out_copied, 1)
                act.wait_ge(dec_out_copied, n + 1)
                fn(d_sq[:], d_out[:], ACT.Square).then_inc(dec_sq_ready, 1)
                if more:
                    head_swap(l, h + 1, 1)
                unit_copy(l, h, 2)
                unit_copy(l, h, 3)
                act.wait_ge(unit_pv, 4 * n + 4)
                fn(o_sq[:].rearrange("p t n -> p (t n)"), PS[:, 7, :], ACT.Square).then_inc(o_sq_ready, 1)
                act.wait_ge(dec_ms_ready, n + 1)
                fn(d_rs[:], PS[:, 2, 0:P], ACT.Ln, bias=eps).then_inc(dec_ln_done, 1)
                act.wait_ge(dec_ln_done, n + 1)
                fn(d_rs[:], d_rs[:], ACT.Exp, scale=-0.5).then_inc(dec_rs_ready, 1)
                act.wait_ge(o_ms_ready, n + 1)
                fn(o_rs, o_ms, ACT.Ln, bias=eps, scale=1.0 / P).then_inc(o_ln_done, 1)
                act.wait_ge(o_ln_done, n + 1)
                fn(o_rs, o_rs, ACT.Exp, scale=-0.5).then_inc(o_rs_ready, 1)
                wait_apart(act, o_t_ready, n + 1)
                fn(a_t[:, h, 0:SEQ], PS[:, 3, :], ACT.Copy, scale=g_sub[:, bass.ds(l, 1)])\
                    .then_inc(a_done, 1)

            def gate_tile(l, n, f, x):
                act.wait_ge(chunk_done[0], n + 1)
                act.wait_ge(branch_taken, x)
                fn(halves(tmp1[:]), pair(0), ACT.Sigmoid).then_inc(gate_ready, 1)

            def window_pair(l, kv, i, p, more):
                n = l * PAIRS + 2 * i + p
                act.wait_ge(swa_max, n + 1)
                for c in range(8):
                    fn(s_p[:, c * P:(c + 1) * P], flat[:, c * P:(c + 1) * P], ACT.Exp,
                       bias=s_nm[:, c:c + 1], accum_out=s_l[:, c:c + 1])
                for g in range(2):
                    last = fn(s_p[:, 1024 + g * 384:1024 + (g + 1) * 384], PS[:, 2 + g, 0:384], ACT.Exp,
                              bias=s_nm[:, 8 + g:9 + g], accum_out=s_l[:, 8 + g:9 + g])
                last.then_inc(swa_exp, 1)
                fn(s_e, s_nm, ACT.Exp, bias=col[:, bass.ds(C_SINK + l * PAIRS + 2 * i + p, 1)])\
                    .then_inc(swa_sink_exp, 1)
                if more:
                    swap(l, l * ROPES + (2 * HEADS + 1) + 2 * i + p + 1, chunk_done[1 - p],
                         nth(l, AT_SWA, 1) + i + p, QK_SCALE)
                for q in range(4):
                    act.wait_ge(swa_pt_ready, 4 * n + q + 1)
                    if q == 0:
                        act.wait_ge(swa_pv, n)
                    k = min(4 * q + 4, 14) - 4 * q
                    fn(s_pt[:, 4 * q:4 * q + k, :].rearrange("p t n -> p (t n)"),
                       PS[:, 6 + q % 2, 0:k * P], ACT.Copy).then_inc(swa_pt_copied, 1)
                wait_apart(act, swa_ot_ready, n + 1)
                for dst, src in transposed_outputs(act_b[0], 2 * i + p):
                    last = fn(dst, src, ACT.Copy)
                last.then_inc(b_hi_ready, 1)

            eps = col[:, C_EPS:C_EPS + 1]
            act.wait_ge(consts_loaded, 16 * CONST_LOADS)
            act.wait_ge(lam_sum, 1)
            fn(lam2, lam2, ACT.Exp).then_inc(lam_exp, 1)
            act.wait_ge(x0_loaded, 16)
            fn(xt_hi[:], x_f[:], ACT.Copy).then_inc(x_hi_ready, 1)
            with act.Fori(0, DEPTH) as l:
                act.wait_ge(x_lo_ready, l * (2 * RT) + X0)
                load_cache(0, l, 0)
                load_cache(1, l, 0)
                for r in range(RT):
                    act.wait_ge(row_evacuated[r], l * GROUPS + 2)
                act.dma_start(v_out[l], rows[:]).then_inc(v_stored, 16)
                head_swap(l, 0, 0)
                head_swap(l, 0, 1)
                all_heads(act, l, head)
                act.wait_ge(v_stored, 16 * (l + 1))
                act.dma_start(s_kc[:].rearrange("p a b k -> p (a b k)"), swa_kc[l])\
                    .then_inc(swa_cache_loaded, 16)
                act.dma_start(s_vc[:].rearrange("p t n -> p (t n)"), swa_vc[l])\
                    .then_inc(swa_cache_loaded, 16)
                act.wait_ge(dec_done, HEADS * (l + 1))
                act.wait_ge(a_done, HEADS * (l + 1))
                with act.Fori(0, KT) as k:
                    fn(act_b[0][:, k, :], a_t[:, k, :], ACT.Copy).then_inc(a_hi_ready, 1)
                with act.Fori(0, KT) as f:
                    gate_tile(l, nth(l, AT_BRANCH_A) + f, f, l * 16 + f)
                act.wait_ge(branch_taken, l * 16 + 8)
                swap(l, l * ROPES + 2 * HEADS, chunk_done[0], nth(l, AT_SWA), 1.0)
                act.wait_ge(chunk_done[1], nth(l, AT_SWA) + 1)
                act.wait_ge(a_lo_ready, KT * (l + 1))
                fn(halves(sv_t[:]), pair(1), ACT.Copy).then_inc(swa_v_copied, 1)
                act.wait_ge(rope_added, l * ROPES + 2 * HEADS + 1)
                for kv in range(2):
                    for half in range(2):
                        last = fn(sk_dup[half * DH:(half + 1) * DH, kv, :], sk_t[kv * DH:(kv + 1) * DH, :],
                                  ACT.Copy)
                last.then_inc(swa_k_dup, 1)
                act.wait_ge(swa_v_copied, l + 1)
                for dst, src in ((swk_out, sk_t), (swv_out, sv_t)):
                    act.dma_start(dst[l], src[:, SEQ - 2 * CHUNK:ROWS]).then_inc(swa_stored, 16)
                act.wait_ge(swa_vt_ready, l + 1)
                fn(sv_rows[:].rearrange("p t n -> p (t n)"), flat[:, 0:1024], ACT.Copy)\
                    .then_inc(swa_v_ready, 1)
                swap(l, l * ROPES + (2 * HEADS + 1), chunk_done[0], nth(l, AT_SWA, 1), QK_SCALE)
                all_pairs(act, l, window_pair)
                act.wait_ge(swa_pv, PAIRS * (l + 1))
                act.wait_ge(x0_copied, 16)
                act.wait_ge(y_stored, 16 * l)
                act.dma_start(rows[:], x_all[l].rearrange("(r p) d -> p r d", p=P))\
                    .then_inc(x_rows_loaded, 16)
                act.wait_ge(swa_stored, 32 * (l + 1))
                with act.Fori(0, KT) as f:
                    gate_tile(l, nth(l, AT_BRANCH_B) + f, f, l * 16 + 8 + f)
                    wait_apart(act, mix_sum, l * KT + f + 1)
                    fn(act_a[0][:, f, :], tmp2[:], ACT.Copy).then_inc(mix_hi_ready, 1)

                def load_norm(which):
                    act.dma_start(ln_g[:], ln_par[l, which, 0]).then_inc(ln_par_loaded, 16)
                    act.dma_start(ln_b[:], ln_par[l, which, 1]).then_inc(ln_par_loaded, 16)

                def norm(which):
                    for r in range(RT + 1):
                        if r < RT:
                            n = l * (2 * RT) + (which * RT + r)
                            act.wait_ge(ln_aggr, n + 1)
                            fn(ln_mv[:, r, 2:3], ln_mv[:, r, 1:2], ACT.Ln, bias=eps).then_inc(ln_log, 1)
                            act.wait_ge(ln_log, n + 1)
                            fn(ln_mv[:, r, 3:4], ln_mv[:, r, 2:3], ACT.Exp, scale=-0.5)\
                                .then_inc(ln_rstd, 1)
                        if r > 0:
                            n = l * (2 * RT) + (which * RT + r - 1)
                            act.wait_ge(ln_t_ready, n + 1)
                            at_col = ((r - 1) % 2) * 1024
                            fn(xt_hi[:, :, (r - 1) * P:r * P],
                               flat[:, at_col:at_col + 1024].rearrange("p (k n) -> p k n", k=KT),
                               ACT.Copy).then_inc(x_hi_ready, 1)

                act.wait_ge(mix_ready, KT * (l + 1))
                load_norm(0)
                norm(0)
                load_norm(1)
                with act.Fori(0, FF_PARTS // 2) as i:
                    for p in range(2):
                        hidden = act_b if p == 0 else act_a
                        with act.Fori(0, KT // 2) as u:
                            for s in range(2):
                                t = l * 32 + (2 * i + p) * 8 + 2 * u + s
                                act.wait_ge(chunk_done[s], nth(l, AT_FF) + (2 * i + p) * 8 + u + 1)
                                act.wait_ge(sq_done, t)
                                fn(halves(tmp1[:]), pair(s), ACT.Relu).then_inc(relu_done[s], 1)
                                wait_apart(act, sq_done, t + 1)
                                fn(hidden[0][:, 2 * u + s, :], tmp2[:], ACT.Copy).then_inc(h_hi_ready, 1)
                norm(1)
                act.wait_ge(ln_rows, 2 * RT * (l + 1))
                act.dma_start(x_all[l + 1].rearrange("(r p) d -> p r d", p=P), rows[:])\
                    .then_inc(y_stored, 16)
            act.wait_ge(y_stored, 16 * DEPTH)
            act.wait_ge(v_stored, 16 * DEPTH)
            act.wait_ge(swa_stored, 32 * DEPTH)
            for p in range(2):
                act.wait_ge(k_stored[p], 16 * DEPTH * HEADS // 2)

        @block.vector
        def _(dve):
            v = nc.vector

            def rotate(l, u, acc_sem, n, scale, adds, before_adds=None):
                dve.wait_ge(acc_sem, n + 1)
                dve.wait_ge(rope_swapped, u + 1)
                dve.wait_ge(rope_added, u)
                v.scalar_tensor_tensor(halves(rope_c[:]), pair(0), scale, halves(cos[:]), ALU.mult,
                                       ALU.mult).then_inc(rope_cos_done, 1)
                v.tensor_tensor(rope_s[:], rope_s[:], sin[:], ALU.mult).then_inc(rope_sin_done, 1)
                dve.wait_ge(rope_cos_done, u + 1)
                dve.wait_ge(rope_sin_done, u + 1)
                if before_adds:
                    before_adds()
                for out, parts, shape_cols in adds:
                    last = v.tensor_tensor(out, shape_cols(rope_c[parts]), shape_cols(rope_s[parts]),
                                           ALU.add)
                last.then_inc(rope_added, 1)

            LOW, HIGH = slice(0, DH), slice(DH, P)

            def rotate_q(l, h, p):
                def samples(g, split):
                    cs = slice(SEQ + g * DH, SEQ + (g + 1) * DH)
                    if split:
                        return lambda t: t[:, cs].rearrange("p (b q) -> p b q", b=4)
                    return lambda t: t[:, cs]

                adds = [(z_map[p][0][LOW, :], LOW, lambda t: t[:, 0:SEQ]),
                        (z_map[p][1][HIGH, :], HIGH, lambda t: t[:, 0:SEQ])]
                for g in range(2):
                    for m, parts in ((0, LOW), (1, HIGH)):
                        side = (m ^ g) * DH
                        adds.append((z_all[parts, g, side:side + DH], parts, samples(g, False)))
                        first = g * 4 * P + side
                        own = z_dec[parts, first:first + 4 * (P + DEC_T)]\
                            .rearrange("p (b c) -> p b c", b=4)[:, :, 0:DEC_T]
                        adds.append((own, parts, samples(g, True)))
                rotate(l, l * ROPES + 2 * h, chunk_done[0], nth(l, AT_HEADS) + h, QK_SCALE, adds,
                       lambda: dve.wait_ge(dec_scores, 2 * (l * HEADS + h)))

            def rotate_k(l, h, p, nth_use):
                rotate(l, l * ROPES + 2 * h + 1, chunk_done[1], nth(l, AT_HEADS) + h, 1.0,
                       [(k_t[p][:], slice(0, P), lambda t: t[:])],
                       lambda: dve.wait_ge(k_stored[p], 16 * nth_use))

            def unit_maxes(l, h, i):
                n, w = 4 * (l * HEADS + h) + i, (i + 1) * P
                dve.wait_ge(unit_scores, n + 1)
                two = PS[:, 2 * (i % 2):2 * (i % 2) + 2, 0:w]
                v.tensor_reduce(u_nm[i % 2], two, AX_X, ALU.max, negate=True).then_inc(unit_max, 1)

            def unit_combine(l, h, i):
                n, w = 4 * (l * HEADS + h) + i, (i + 1) * P
                dve.wait_ge(unit_exp, n + 1)
                dve.wait_ge(unit_probs, n)
                v.reciprocal(u_r, u_l[i % 2]).then_inc(unit_recip, 1)
                dve.wait_ge(unit_recip, n + 1)
                v.tensor_tensor(u_r[:, 1:2], u_r[:, 1:2], neg_lam[:, bass.ds(l, 1)], ALU.mult)\
                    .then_inc(unit_r_ready, 1)
                dve.wait_ge(unit_r_ready, n + 1)
                v.tensor_scalar(u_p[i % 2][:, 1, 0:w], u_p[i % 2][:, 1, 0:w], u_r[:, 1:2], None, ALU.mult)\
                    .then_inc(unit_second, 1)
                dve.wait_ge(unit_second, n + 1)
                dve.wait_ge(unit_t_ready, 4 * (l * HEADS + h) + max(0, i - 1))
                v.scalar_tensor_tensor(u_a[i % 2][:, 0:w], u_p[i % 2][:, 0, 0:w], u_r[:, 0:1],
                                       u_p[i % 2][:, 1, 0:w], ALU.mult, ALU.add).then_inc(unit_probs, 1)

            def head(l, h, p, more, next_uses):
                n = l * HEADS + h
                for g in range(2):
                    dve.wait_ge(dec_scores, 2 * n + g + 1)
                    v.tensor_reduce(d_nm[:, g:g + 1], flat[:, 1024 * g:1024 * g + ROWS], AX_X, ALU.max,
                                    negate=True).then_inc(dec_max, 1)
                dve.wait_ge(dec_exp, 2 * n + 2)
                v.reciprocal(d_r, d_l).then_inc(dec_recip, 1)
                dve.wait_ge(dec_recip, n + 1)
                for g, parts in ((0, HIGH), (1, LOW)):
                    last = v.tensor_tensor(d_r[parts, g:g + 1], d_r[parts, g:g + 1],
                                           neg_lam[parts, bass.ds(l, 1)], ALU.mult)
                last.then_inc(dec_r_ready, 1)
                dve.wait_ge(dec_shifted, n + 1)
                dve.wait_ge(o_t_ready, n)
                for g, parts in ((0, LOW), (1, HIGH)):
                    v.scalar_tensor_tensor(d_a[parts], d_p[parts, g, :], d_r[parts, g:g + 1], d_t[parts],
                                           ALU.mult, ALU.add).then_inc(dec_probs, 1)
                if more:
                    rotate_q(l, h + 1, 1 - p)
                dve.wait_ge(dec_new_copied, n + 1)
                dve.wait_ge(dec_ot_ready, n)
                v.tensor_tensor(d_o[:], PS[:, 2:4, :].rearrange("p a (b n) -> p (a b) n", b=4),
                                d_on[:].unsqueeze(1).to_broadcast([P, DEC_B, P]), ALU.add)\
                    .then_inc(dec_o_summed, 1)
                unit_maxes(l, h, 0)
                unit_maxes(l, h, 1)
                unit_combine(l, h, 0)
                unit_maxes(l, h, 2)
                unit_combine(l, h, 1)
                unit_maxes(l, h, 3)
                unit_combine(l, h, 2)
                unit_combine(l, h, 3)
                if more:
                    rotate_k(l, h + 1, 1 - p, next_uses)
                dve.wait_ge(o_sq_ready, n + 1)
                v.tensor_reduce(o_ms, o_sq[:], AX_X, ALU.add).then_inc(o_ms_ready, 1)
                dve.wait_ge(dec_rs_ready, n + 1)
                v.scalar_tensor_tensor(a_t[:, h, SEQ:ROWS], d_out[:], g_sub[:, bass.ds(l, 1)], d_rs[:],
                                       ALU.mult, ALU.mult).then_inc(dec_done, 1)
                dve.wait_ge(o_rs_ready, n + 1)
                dve.wait_ge(dec_t_ready, 2 * n + 2)
                v.tensor_tensor(o_n[:], PS[:, 7, :].rearrange("p (i e) -> p i e", i=4),
                                o_rs.unsqueeze(2).to_broadcast([P, 4, P]), ALU.mult)\
                    .then_inc(o_n_ready, 1)

            def branch_tile(l, at_chunk, f, x, out):
                dve.wait_ge(gate_ready, x + 1)
                dve.wait_ge(chunk_done[1], nth(l, at_chunk) + f + 1)
                v.tensor_tensor(halves(out), pair(1), halves(tmp1[:]), ALU.mult).then_inc(branch_taken, 1)

            def window_pair(l, kv, i, p, more):
                n = l * PAIRS + 2 * i + p
                sink = col[:, bass.ds(C_SINK + l * PAIRS + 2 * i + p, 1)]
                dve.wait_ge(swa_scores, n + 1)
                v.tensor_reduce(s_nm[:, 0:8], flat[:, 0:1024].rearrange("p (c k) -> p c k", c=8), AX_X,
                                ALU.max)
                v.tensor_reduce(s_nm[:, 8:10], PS[:, 2:4, 0:384], AX_X, ALU.max).then_inc(swa_row_max, 1)
                dve.wait_ge(swa_row_max, n + 1)
                v.tensor_scalar(s_nm, s_nm, sink, -1.0, ALU.max, ALU.mult).then_inc(swa_max, 1)
                dve.wait_ge(swa_exp, n + 1)
                dve.wait_ge(swa_sink_exp, n + 1)
                v.tensor_tensor(s_l, s_l, s_e, ALU.add).then_inc(swa_sum, 1)
                dve.wait_ge(swa_sum, n + 1)
                v.reciprocal(s_l, s_l).then_inc(swa_recip, 1)
                if more:
                    rotate_pair(l, i + p, 1 - p)
                dve.wait_ge(swa_recip, n + 1)
                dve.wait_ge(swa_pv, n + 1)
                v.tensor_tensor(s_o[:], flat[:, 0:ROWS].rearrange("p (u d) -> p u d", d=DH),
                                s_l.unsqueeze(2).to_broadcast([P, 10, DH]), ALU.mult)\
                    .then_inc(swa_o_ready, 1)
                dve.wait_ge(b_hi_ready, n + 1)
                for (lo, src), (hi, _) in zip(transposed_outputs(act_b[1], 2 * i + p),
                                              transposed_outputs(act_b[0].bitcast(F32), 2 * i + p)):
                    last = v.tensor_tensor(lo, src, hi, ALU.subtract)
                last.then_inc(b_lo_ready, 1)

            def rotate_pair(l, i, p):
                adds = []
                for g, parts in ((0, LOW), (1, HIGH)):
                    adds.append((zq[p][parts, :, g, :], parts,
                                 lambda t: t[:, 0:SEQ].rearrange("p (c q) -> p c q", q=CHUNK)))
                    adds.append((zs[p][parts, :, g * DH:(g + 1) * DH], parts,
                                 lambda t: t[:, SEQ:ROWS].rearrange("p (g q) -> p g q", g=2)))
                rotate(l, l * ROPES + (2 * HEADS + 1) + 2 * i + p, chunk_done[p],
                       nth(l, AT_SWA, 1) + i, QK_SCALE, adds)

            def norm(l, which):
                x0 = l * (2 * RT) + which * RT

                def stats(r):
                    for half in range(2):
                        last = v.bn_stats(ln_st[:, r, half, :], rows[:, r, half * BANK:(half + 1) * BANK])
                    last.then_inc(ln_stats, 1)
                    wait_apart(dve, ln_stats, x0 + r + 1)
                    v.bn_aggr(ln_mv[:, r, 0:2], ln_st[:, r].rearrange("p a b -> p (a b)"))\
                        .then_inc(ln_aggr, 1)

                def low(r):
                    dve.wait_ge(x_hi_ready, x0 + r + X0 + 1)
                    psum = flat[:, (r % 2) * 1024:(r % 2) * 1024 + 1024].rearrange("p (k n) -> p k n", k=KT)
                    c = slice(r * P, (r + 1) * P)
                    v.tensor_tensor(xt_lo[:, :, c], psum, xt_hi[:, :, c].bitcast(F32), ALU.subtract)\
                        .then_inc(x_lo_ready, 1)

                dve.wait_ge(row_evacuated[RT - 1], l * GROUPS + (4 if which == 0 else GROUPS))
                stats(0)
                dve.wait_ge(ln_par_loaded, 32 * (2 * l + which + 1))
                for r in range(RT):
                    y, t = rows[:, r, :], ln_x[r % 2][:]
                    if r + 1 < RT:
                        stats(r + 1)
                    dve.wait_ge(ln_rstd, x0 + r + 1)
                    dve.wait_ge(ln_rows, x0 + r)
                    v.tensor_scalar(t, y, ln_mv[:, r, 0:1], ln_mv[:, r, 3:4], ALU.subtract, ALU.mult)\
                        .then_inc(ln_normed, 1)
                    dve.wait_ge(ln_normed, x0 + r + 1)
                    v.tensor_tensor(t, t, ln_g[:], ALU.mult).then_inc(ln_scaled, 1)
                    dve.wait_ge(ln_scaled, x0 + r + 1)
                    v.tensor_tensor(y, t, ln_b[:], ALU.add).then_inc(ln_rows, 1)
                    if r > 0:
                        low(r - 1)
                low(RT - 1)

            def take_group(group, n, out, residual=None, slot=1):
                for r in range(RT):
                    if r < RT - 1:
                        dve.wait_ge(row_acc_ready, group * (RT - 1) + r + 1)
                    else:
                        dve.wait_ge(chunk_done[1], n)
                    if residual is None:
                        v.tensor_copy(out(r), PS[:, r, :]).then_inc(row_evacuated[r], 1)
                    else:
                        v.scalar_tensor_tensor(out(r), out(r), residual, PS[:, r, :], ALU.mult,
                                               ALU.add).then_inc(row_evacuated[r], 1)

            def half_rows(h):
                return lambda r: rows[:, r, bass.ts(h, BANK)]

            dve.wait_ge(consts_loaded, 16 * CONST_LOADS)
            v.tensor_copy(mask_cols[:], mask_f[:]).then_inc(masks_ready, 1)
            dve.wait_ge(masks_ready, 1)
            prod = tmp1[:, 0:2 * DEPTH * DH].rearrange("p (a l d) -> p a l d", a=2, l=DEPTH)
            for a in range(2):
                last = v.tensor_tensor(prod[:, a], lam_v[:, :, 2 * a, :], lam_v[:, :, 2 * a + 1, :],
                                       ALU.mult)
            last.then_inc(lam_link, 1)
            dve.wait_ge(lam_link, 1)
            v.tensor_reduce(lam2, prod.rearrange("p a l d -> p (a l) d"), AX_X, ALU.add)\
                .then_inc(lam_sum, 1)
            dve.wait_ge(lam_exp, 1)
            v.tensor_tensor(neg_lam[:], lam2[:, DEPTH:2 * DEPTH], lam2[:, 0:DEPTH], ALU.subtract)\
                .then_inc(lam_link, 1)
            dve.wait_ge(lam_link, 2)
            v.tensor_tensor(neg_lam[:], neg_lam[:], col[:, C_LAM_INIT:C_LAM_INIT + DEPTH], ALU.subtract)
            v.tensor_tensor(g_sub[:], col[:, C_SUBLN:C_SUBLN + DEPTH],
                            col[:, C_ONE_MINUS:C_ONE_MINUS + DEPTH], ALU.mult).then_inc(lam_link, 1)
            dve.wait_ge(lam_link, 3)
            dve.wait_ge(x0_loaded, 16)
            dve.wait_ge(x_hi_ready, X0)
            v.tensor_tensor(xt_lo[:], x_f[:], xt_hi[:].bitcast(F32), ALU.subtract).then_inc(x_lo_ready, 1)
            with dve.Fori(0, DEPTH) as l:
                dve.wait_ge(x_lo_ready, l * (2 * RT) + X0)
                for p in range(2):
                    v.memset(z_map[p][0][HIGH, :], 0.0)
                    v.memset(z_map[p][1][LOW, :], 0.0)
                v.memset(z_all[:], 0.0)
                v.memset(z_dec[:], 0.0).then_inc(z_zeroed, 1)
                wait_apart(dve, y_stored, 16 * l)
                with dve.Fori(0, 2) as half:
                    take_group(l * GROUPS + half, nth(l, AT_V) + 2 * half + 2, half_rows(half))
                dve.wait_ge(z_zeroed, l + 1)
                rotate_q(l, 0, 0)
                rotate_k(l, 0, 0, l * (HEADS // 2))
                with dve.Fori(0, HEADS // 2 - 1) as i:
                    for p in range(2):
                        head(l, 2 * i + p, p, True, l * (HEADS // 2) + i + p)
                head(l, HEADS - 2, 0, True, l * (HEADS // 2) + HEADS // 2 - 1)
                head(l, HEADS - 1, 1, False, None)
                dve.wait_ge(a_done, HEADS * (l + 1))
                wait_apart(dve, dec_done, HEADS * (l + 1))
                with dve.Fori(0, KT) as k:
                    dve.wait_ge(a_hi_ready, l * KT + k + 1)
                    v.tensor_tensor(act_b[1][:, k, :], a_t[:, k, :], act_b[0][:, k, :].bitcast(F32),
                                    ALU.subtract).then_inc(a_lo_ready, 1)
                with dve.Fori(0, KT) as f:
                    branch_tile(l, AT_BRANCH_A, f, l * 16 + f, mix_a[:, f, :])
                dve.wait_ge(a_lo_ready, KT * (l + 1))
                for p in range(2):
                    v.memset(zq[p][:], 0.0)
                    last = v.memset(zs[p][:], 0.0)
                last.then_inc(swa_zeroed, 1)
                rotate(l, l * ROPES + 2 * HEADS, chunk_done[0], nth(l, AT_SWA), 1.0,
                       [(sk_t[:], slice(0, P), lambda t: t[:])])
                dve.wait_ge(swa_zeroed, l + 1)
                rotate_pair(l, 0, 0)
                all_pairs(dve, l, window_pair)
                dve.wait_ge(swa_stored, 32 * (l + 1))
                wait_apart(dve, rope_added, l * ROPES + ROPES)
                with dve.Fori(0, KT) as f:
                    n = l * KT + f
                    dve.wait_ge(mix_ready, n)
                    branch_tile(l, AT_BRANCH_B, f, l * 16 + 8 + f, tmp2[:])
                    dve.wait_ge(branch_taken, l * 16 + 8 + f + 1)
                    v.tensor_tensor(tmp2[:], tmp2[:], mix_a[:, f, :], ALU.add).then_inc(mix_sum, 1)
                    dve.wait_ge(mix_hi_ready, n + 1)
                    v.tensor_tensor(act_a[1][:, f, :], tmp2[:], act_a[0][:, f, :].bitcast(F32),
                                    ALU.subtract).then_inc(mix_ready, 1)
                wait_apart(dve, x_rows_loaded, 16 * (l + 1))
                with dve.Fori(0, 2) as half:
                    take_group(l * GROUPS + 2 + half, nth(l, AT_O) + 2 * half + 2, half_rows(half), ALPHA)
                norm(l, 0)
                for r in range(RT):
                    last = v.tensor_scalar(rows[:, r, :], rows[:, r, :], ALPHA, None, ALU.mult)
                last.then_inc(resid_scaled, 1)
                with dve.Fori(0, FF_PARTS // 2) as i:
                    for p in range(2):
                        hidden = act_b if p == 0 else act_a
                        part = 2 * i + p
                        with dve.Fori(0, KT // 2) as u:
                            for s in range(2):
                                t = l * 32 + part * 8 + 2 * u + s
                                dve.wait_ge(relu_done[s], l * 16 + part * 4 + u + 1)
                                dve.wait_ge(h_ready, t)
                                v.tensor_tensor(tmp2[:], tmp1[:], tmp1[:], ALU.mult).then_inc(sq_done, 1)
                                dve.wait_ge(h_hi_ready, t + 1)
                                v.tensor_tensor(hidden[1][:, 2 * u + s, :], tmp2[:],
                                                hidden[0][:, 2 * u + s, :].bitcast(F32), ALU.subtract)\
                                    .then_inc(h_ready, 1)
                        wait_apart(dve, resid_scaled, l + 1)
                        with dve.Fori(0, 2) as half:
                            dve.wait_ge(row_evacuated[RT - 1], l * GROUPS + 4 + 2 * part + half)
                            take_group(l * GROUPS + 4 + 2 * part + half,
                                       nth(l, AT_FF) + 8 * part + 4 + 2 * half + 2, half_rows(half), 1.0)
                norm(l, 1)


def stream(w_in, w_a, w_b, w_o, w_up, w_down):
    import numpy as np

    def feature_tiles(w, tiles):
        t = w.reshape(KT, P, -1, P).transpose(2, 1, 0, 3).reshape(-1, P, D)
        return [t[f] for f in tiles]

    def row_form(w):
        t = w.reshape(KT // 2, 2, P, 2, BANK).transpose(3, 0, 2, 1, 4).reshape(-1, P, D)
        return list(t)

    out = []
    for l in range(DEPTH):
        q, k, v = (w_in[l][:, i * D:(i + 1) * D] for i in range(3))
        rest = w_in[l][:, 3 * D:]
        sq, sk, sv = rest[:, 0:D], rest[:, D:D + P], rest[:, D + P:D + 2 * P]
        ga, gb = rest[:, D + 2 * P:2 * D + 2 * P], rest[:, 2 * D + 2 * P:]
        out += row_form(v)
        for h in range(HEADS):
            out += feature_tiles(q, [h]) + feature_tiles(k, [h])
        for f in range(KT):
            out += feature_tiles(ga, [f]) + feature_tiles(w_a[l], [f])
        out += feature_tiles(sk, [0]) + feature_tiles(sv, [0]) + feature_tiles(sq, range(PAIRS))
        for f in range(KT):
            out += feature_tiles(gb, [f]) + feature_tiles(w_b[l], [f])
        out += row_form(w_o[l])
        for part in range(FF_PARTS):
            out += feature_tiles(w_up[l], range(part * KT, (part + 1) * KT))
            out += row_form(w_down[l][part * D:(part + 1) * D])
    return np.ascontiguousarray(np.stack(out))


def tables():
    import math

    import numpy as np

    half = DH // 2
    inv = (np.float32(10000.0) ** (-np.arange(half, dtype=np.float32) / np.float32(half))).astype(np.float32)
    pos = np.concatenate([np.arange(SEQ), np.tile(PAST + np.arange(DEC_T), DEC_B)]).astype(np.float32)
    ang = (inv[:, None] * pos[None, :]).astype(np.float32)
    cos = np.tile(np.cos(ang), (4, 1)).astype(np.float32)
    sin = np.sin(ang).astype(np.float32)
    sin = np.tile(np.concatenate([-sin, sin]), (2, 1)).astype(np.float32)
    row = np.arange(P)
    m = np.zeros((P, MASK_COLS), np.float32)
    m[0, 0:CHUNK] = 1.0
    m[0, P:2 * P] = 1.0
    for g in range(2):
        for b in range(DEC_B):
            m[b, 2 * P + g * P:2 * P + (g + 1) * P] = 4 * g + (row % 64) // DEC_T != b
    at = 4 * P
    m[0, at:at + 64] = NEG
    at += 64
    for b in range(DEC_B):
        m[b, at + b * DEC_T:at + (b + 1) * DEC_T] = NEG
    at += P
    for g in range(2):
        for b in range(4):
            m[4 * g + b, at + 256 * g + 64 * b:at + 256 * g + 64 * (b + 1)] = NEG
    lam_init = [0.8 - 0.6 * math.exp(-0.3 * l) for l in range(DEPTH)]
    return (cos, sin, np.eye(P, dtype=np.float32), np.full((P, P), 1.0 / P, np.float32),
            m, lam_init)


def kernel(x_prompt, x_sample, cache_diff_k, cache_diff_v, cache_swa_k, cache_swa_v, w_in,
           diff_lambda_q1, diff_lambda_k1, diff_lambda_q2, diff_lambda_k2, diff_subln_g, swa_sinks,
           w_branch_a, w_branch_b, w_o, ln1_g, ln1_b, w_up, w_down, ln2_g, ln2_b):
    import numpy as np
    import concourse.bacc as bacc
    from concourse.bass_utils import run_bass_kernel_spmd

    c = np.ascontiguousarray
    x = np.concatenate([x_prompt.reshape(SEQ, D), x_sample.reshape(DEC_B * DEC_T, D)])
    k = cache_diff_k.transpose(0, 3, 4, 5, 1, 2).reshape(DEPTH, HEADS, P, DEC_B * PAST)
    v = cache_diff_v.reshape(DEPTH, DEC_B, 4, P, HEADS, P).transpose(0, 4, 3, 2, 1, 5)
    sk = cache_swa_k[:, :, CHUNK:].transpose(0, 4, 3, 1, 2).reshape(DEPTH, DH, 2 * DEC_B * 64)
    sk = np.concatenate([sk, sk], axis=1)
    sv = cache_swa_v[:, :, CHUNK:].reshape(DEPTH, 4, P, P).transpose(0, 2, 1, 3)
    cos, sin, ident, ones, masks, lam_init = tables()
    cols = np.zeros((P, C_END), np.float32)
    for l in range(DEPTH):
        cols[:, C_LAM_INIT + l] = lam_init[l]
        cols[:, C_ONE_MINUS + l] = 1.0 - lam_init[l]
        cols[:, C_SUBLN + l] = diff_subln_g[l]
        for j in range(PAIRS):
            cols[0:64, C_SINK + l * PAIRS + j] = swa_sinks[l, 2 * j]
            cols[64:128, C_SINK + l * PAIRS + j] = swa_sinks[l, 2 * j + 1]
    cols[:, C_EPS] = EPS
    lam = np.stack([diff_lambda_q1, diff_lambda_k1, diff_lambda_q2, diff_lambda_k2], axis=1)
    lam = np.broadcast_to(lam.reshape(1, -1), (P, DEPTH * 4 * DH))
    ln = np.stack([ln1_g, ln1_b, ln2_g, ln2_b], axis=1).reshape(DEPTH, 2, 2, 1, D)
    ln = np.broadcast_to(ln, (DEPTH, 2, 2, P, D))
    keep = CHUNK * 2 - DEC_T
    arrays = {
        "x_t": x.T.reshape(KT, P, ROWS), "x_rows": x,
        "k_cache": k, "v_cache": v.reshape(DEPTH, HEADS, P, 4 * D),
        "swa_kc": sk, "swa_vc": sv.reshape(DEPTH, P, 4 * P),
        "swa_k_keep": cache_swa_k[:, :, DEC_T:].reshape(DEPTH * DEC_B, keep * P),
        "swa_v_keep": cache_swa_v[:, :, DEC_T:].reshape(DEPTH * DEC_B, keep * P),
        "weights": stream(w_in, w_branch_a, w_branch_b, w_o, w_up, w_down),
        "cols": cols, "lam_vec": lam, "ln_par": ln, "cos_t": cos, "sin_t": sin, "ident_d": ident,
        "ones_d": ones, "masks": masks,
    }
    arrays = {"in_" + n: c(a) for n, a in arrays.items()}
    outs = {
        "x_all": [DEPTH + 1, ROWS, D], "k_out": [DEPTH, HEADS, P, ROWS],
        "v_out": [DEPTH, P, RT, D], "swk_out": [DEPTH, P, 2 * P], "swv_out": [DEPTH, P, 2 * P],
        "swk_keep_out": [DEPTH * DEC_B, keep * P], "swv_keep_out": [DEPTH * DEC_B, keep * P],
    }
    nc = bacc.Bacc("TRN2", target_bir_lowering=False, num_devices=1)
    args = [nc.dram_tensor(n, a.shape, mybir.dt.from_np(a.dtype), kind="ExternalInput").ap()
            for n, a in arrays.items()]
    args += [nc.dram_tensor(n, s, F32, kind="ExternalOutput").ap() for n, s in outs.items()]
    build(nc, *args)
    got = run_bass_kernel_spmd(nc, [arrays], core_ids=[0]).results[0]

    y = got["x_all"][DEPTH]
    ko, vo = got["k_out"], got["v_out"].transpose(0, 2, 1, 3).reshape(DEPTH, ROWS, HEADS, P)
    ko = ko.reshape(DEPTH, HEADS, 2, DH, ROWS).transpose(0, 4, 1, 2, 3)

    def window(new, kept):
        new = new.transpose(0, 2, 1).reshape(DEPTH, 2 * P, 2, DH)
        kept = kept.reshape(DEPTH, DEC_B, keep, 2, DH)
        fresh = new[:, P:].reshape(DEPTH, DEC_B, DEC_T, 2, DH)
        return c(new[:, None, 0:P]), c(np.concatenate([kept, fresh], axis=2))

    skp, sks = window(got["swk_out"], got["swk_keep_out"])
    svp, svs = window(got["swv_out"], got["swv_keep_out"])
    return (c(y[:SEQ].reshape(1, SEQ, D)), c(y[SEQ:].reshape(DEC_B, DEC_T, D)),
            c(ko[:, None, :SEQ]), c(vo[:, None, :SEQ]), skp, svp,
            c(ko[:, SEQ:].reshape(DEPTH, DEC_B, DEC_T, HEADS, 2, DH)),
            c(vo[:, SEQ:].reshape(DEPTH, DEC_B, DEC_T, HEADS, P)), sks, svs)
```

```python
from contextlib import ExitStack

import concourse.bass as bass
from concourse import mybir

F32 = mybir.dt.float32
F32R = mybir.dt.float32r
BF16 = mybir.dt.bfloat16
ALU = mybir.AluOpType
ACT = mybir.ActivationFunctionType
AX_X = mybir.AxisListType.X

P = 128
D = 1024
KT = D // P
SEQ = 512
DEC_B = 8
DEC_T = 16
ROWS = SEQ + DEC_B * DEC_T
RT = ROWS // P
DEPTH = 2
CHUNK = 64
PAST = 512
HEADS = 8
DH = 64
PAIRS = 8
HALF = ROWS // 2
BANK = 512
FF_PARTS = 4
ALPHA = (2 * DEPTH) ** 0.25
EPS = 1e-5
QK_SCALE = DH ** -0.5
NEG = -1e30

V_CHUNKS, HEAD_CHUNKS, BRANCH_CHUNKS, O_CHUNKS = 8, 2 * HEADS, 2 * KT, 8
SWA_CHUNKS = 2 + PAIRS
FF_CHUNKS = FF_PARTS * 16
AT_HEAD_0 = 0
AT_V = AT_HEAD_0 + 2
AT_HEADS = AT_V + V_CHUNKS - 2
AT_BRANCH_A = AT_HEADS + HEAD_CHUNKS
AT_SWA = AT_BRANCH_A + BRANCH_CHUNKS
AT_BRANCH_B = AT_SWA + SWA_CHUNKS
AT_O = AT_BRANCH_B + BRANCH_CHUNKS
AT_FF = AT_O + O_CHUNKS
CHUNKS = AT_FF + FF_CHUNKS
RAW_SLOTS = 4

ROPES = 2 * HEADS + 1 + PAIRS
GROUPS = 2 + 2 + 2 * FF_PARTS

C_LAM_INIT = 0
C_ONE_MINUS = C_LAM_INIT + DEPTH
C_SUBLN = C_ONE_MINUS + DEPTH
C_ZERO = C_SUBLN + DEPTH
C_EPS = C_ZERO + 1
C_SINK = C_EPS + 1
C_END = C_SINK + DEPTH * PAIRS
MASK_COLS = 4 * P + 64 + P + 512


def build(nc, x_rows, k_cache, v_cache, swa_kc, swa_vc, swa_k_keep, swa_v_keep, weights, cols,
          lam_vec, ln_par, cos_t, sin_t, ident_d, ones_d, masks, x_all, k_out, v_out, swk_out,
          swv_out, swk_keep_out, swv_keep_out):
    ctx = ExitStack()
    with ctx:
        def sem(name):
            return ctx.enter_context(nc.semaphore(name))

        base = -(-nc.sbuf_base // 32) * 32
        total = 212480
        ctx.enter_context(nc.sbuf_tensor("arena", [P, (total + 32) // 4], F32))
        top = [base]

        def region(nbytes):
            at = top[0]
            top[0] += nbytes
            assert top[0] <= base + total
            return [at, at + nbytes]

        def at(where, name, shape, dt):
            t = nc.alloc_sbuf_tensor_at(name, [P, *shape], dt, offset=where[0])
            size = 2 if dt == BF16 else 4
            for n in shape:
                size *= n
            where[0] += -(-size // 32) * 32
            assert where[0] <= where[1], name
            return t

        WIDE = KT * ROWS * 4
        r_xt, r_a, r_b = region(2 * WIDE), region(2 * WIDE), region(2 * WIDE)
        r_rows, r_mix, r_w = region(WIDE), region(WIDE), region(32768)
        r_keep = region(base + total - top[0])

        xt_hi = at(r_xt, "xt_hi", [KT, ROWS], F32R)
        xt_lo = at(r_xt, "xt_lo", [KT, ROWS], F32R)
        rows = at(list(r_rows), "rows", [RT, D], F32)
        mix_a = at(list(r_mix), "mix_a", [KT, ROWS], F32)
        raw = at(r_w, "w_raw", [RAW_SLOTS, D], F32)
        w_hi = [at(r_w, f"w_hi{s}", [D], F32R) for s in range(2)]
        w_lo = [at(r_w, f"w_lo{s}", [D], F32R) for s in range(2)]
        cos = at(r_keep, "cos", [ROWS], F32)
        sin = at(r_keep, "sin", [ROWS], F32)
        rope_c = at(r_keep, "rope_c", [ROWS], F32)
        rope_s = at(r_keep, "rope_s", [ROWS], F32)
        ident = at(r_keep, "ident", [P], F32)
        ones = at(r_keep, "ones", [P], F32)
        mask_cols = at(r_keep, "mask_cols", [MASK_COLS], BF16)
        m_first, m_all = mask_cols[:, 0:P], mask_cols[:, P:2 * P]
        m_own = mask_cols[:, 2 * P:4 * P].rearrange("p (g n) -> p g n", g=2)
        m_neg64 = mask_cols[:, 4 * P:4 * P + 64]
        m_negnew = mask_cols[:, 4 * P + 64:5 * P + 64]
        m_negold = mask_cols[:, 5 * P + 64:MASK_COLS].rearrange("p (g n) -> p g n", g=2)
        col = at(r_keep, "col", [C_END], F32)
        neg_lam = at(r_keep, "neg_lam", [DEPTH], F32)
        g_sub = at(r_keep, "g_sub", [DEPTH], F32)
        small = at(r_keep, "small", [64], F32)
        tmp1, tmp2 = rope_c, rope_s

        ra = list(r_a)
        a_t = at(ra, "a_t", [KT, ROWS], F32)
        z_map = [[at(ra, f"z_map{p}{m}", [SEQ], F32) for m in range(2)] for p in range(2)]
        k_t = [at(ra, f"k_t{p}", [ROWS], F32) for p in range(2)]
        z_dec = at(ra, "z_dec", [DEC_B * P + 64 * 2], F32)
        d_a = at(list(ra), "d_a", [ROWS], F32)
        o_n = at(ra, "o_n", [4, P], F32)
        d_on = at(ra, "d_on", [P], F32)
        ra = list(r_a)
        sk_t = at(ra, "sk_t", [ROWS], F32)
        sk_dup = at(ra, "sk_dup", [2, ROWS], F32)
        sv_t = at(ra, "sv_t", [ROWS], F32)
        sv_rows = at(ra, "sv_rows", [8, P], F32)
        zq = [at(ra, f"zq{p}", [8, 2, 64], F32) for p in range(2)]
        zs = [at(ra, f"zs{p}", [2, P], F32) for p in range(2)]
        s_o = at(ra, "s_o", [10, DH], F32)
        ra = list(r_a)
        act_a = [at(ra, "act_a_hi", [KT, ROWS], F32R), at(ra, "act_a_lo", [KT, ROWS], F32R)]
        rb = list(r_b)
        kc = at(rb, "kc", [DEC_B, PAST], F32)
        vc = at(rb, "vc", [4, D], F32)
        d_o = at(rb, "d_o", [DEC_B, P], F32)
        d_at = at(rb, "d_at", [5, P], F32)
        v_new = at(rb, "v_new", [P], F32)
        d_out = at(rb, "d_out", [P], F32)
        d_rs = at(rb, "d_rs", [P], F32)
        rb = list(r_b)
        act_b = [at(rb, "act_b_hi", [KT, ROWS], F32R), at(rb, "act_b_lo", [KT, ROWS], F32R)]
        rm = list(r_mix)
        u_p = [at(rm, f"u_p{p}", [2, BANK], F32) for p in range(2)]
        u_a = [at(rm, f"u_a{p}", [BANK], F32) for p in range(2)]
        u_at = [at(rm, f"u_at{p}", [BANK], F32) for p in range(2)]
        d_t = at(list(rm), "d_t", [ROWS], F32)
        o_sq = at(list(rm), "o_sq", [4, P], F32)
        rm[0] += ROWS * 4
        z_all = at(rm, "z_all", [2, P], F32)
        d_sq = at(rm, "d_sq", [P], F32)
        d_p = at(list(r_mix), "d_p", [2, ROWS], F32)
        rm = list(r_mix)
        ln_g = at(rm, "ln_g", [D], F32)
        ln_b = at(rm, "ln_b", [D], F32)
        rr = list(r_rows)
        s_p = at(rr, "s_p", [8 * P + 2 * 384], F32)
        s_pt = at(rr, "s_pt", [14, P], F32)
        s_kc = at(rr, "s_kc", [2, DEC_B, 64], F32)
        s_vc = at(rr, "s_vc", [4, P], F32)
        rm = list(r_mix)
        lam_v = at(rm, "lam_v", [DEPTH, 4, DH], F32)
        mask_f = at(rm, "mask_f", [MASK_COLS], F32)
        ln_st = at(r_keep, "ln_st", [RT, 2, 6], F32)
        ln_mv = at(r_keep, "ln_mv", [RT, 4], F32)
        d_nm, d_l, d_r = small[:, 0:2], small[:, 2:4], small[:, 4:6]
        u_nm = [small[:, 6:8], small[:, 8:10]]
        u_l = [small[:, 10:12], small[:, 12:14]]
        u_r = small[:, 14:16]
        o_ms, o_rs = small[:, 16:20], small[:, 20:24]
        s_nm, s_l, s_e = small[:, 24:34], small[:, 34:44], small[:, 44:54]
        lam2 = small[:, 54:58]

        PS = ctx.enter_context(nc.psum_tensor("PS", [P, 8, BANK], F32))
        flat = PS[:].rearrange("p b n -> p (b n)")

        def pair(which):
            return PS[:, 4 + 2 * which:6 + 2 * which, 0:HALF]

        def bank_of(which, half):
            return 4 + 2 * which + half

        def halves(t):
            return t.rearrange("p (a n) -> p a n", a=2)

        raw_loaded = [sem(f"raw_loaded{j}") for j in range(RAW_SLOTS)]
        w_hi_made = sem("w_hi_made")
        w_ready = [sem(f"w_ready{s}") for s in range(2)]
        chunk_done = [sem(f"chunk_done{s}") for s in range(2)]
        chunk_half_done = [sem(f"chunk_half_done{s}") for s in range(2)]
        consts_loaded, ident_loaded, small_loaded = sem("consts_loaded"), sem("ident_loaded"), sem("small_loaded")
        x0_loaded = [sem(f"x0_loaded{r}") for r in range(RT)]
        lam_sum, lam_exp, lam_link = sem("lam_sum"), sem("lam_exp"), sem("lam_link")
        masks_ready = sem("masks_ready")
        x_hi_ready, x_lo_ready = sem("x_hi_ready"), sem("x_lo_ready")
        row_acc_ready = sem("row_acc_ready")
        row_evacuated = [sem(f"row_evacuated{r}") for r in range(RT)]
        v_stored = sem("v_stored")
        z_zeroed = sem("z_zeroed")
        rope_swapped, rope_cos_done = sem("rope_swapped"), sem("rope_cos_done")
        rope_sin_done, rope_added = sem("rope_sin_done"), sem("rope_added")
        k_stored = [sem(f"k_stored{p}") for p in range(2)]
        kc_loaded, vc_loaded = sem("kc_loaded"), sem("vc_loaded")
        dec_scores, dec_max, dec_exp = sem("dec_scores"), sem("dec_max"), sem("dec_exp")
        dec_recip, dec_r_ready = sem("dec_recip"), sem("dec_r_ready")
        dec_shifted, dec_probs = sem("dec_shifted"), sem("dec_probs")
        dec_t_ready, dec_t_copied = sem("dec_t_ready"), sem("dec_t_copied")
        dec_pv, v_new_copied = sem("dec_pv"), sem("v_new_copied")
        dec_new_ready, dec_new_copied = sem("dec_new_ready"), sem("dec_new_copied")
        dec_o_copied, dec_ot_ready, dec_summed = sem("dec_o_copied"), sem("dec_ot_ready"), sem("dec_summed")
        dec_sq_ready, dec_ms_ready = sem("dec_sq_ready"), sem("dec_ms_ready")
        dec_ln_done, dec_rs_ready, dec_done = sem("dec_ln_done"), sem("dec_rs_ready"), sem("dec_done")
        unit_scores, unit_max, unit_exp = sem("unit_scores"), sem("unit_max"), sem("unit_exp")
        unit_recip, unit_r_ready = sem("unit_recip"), sem("unit_r_ready")
        unit_second, unit_probs = sem("unit_second"), sem("unit_probs")
        unit_t_ready, unit_t_copied, unit_pv = sem("unit_t_ready"), sem("unit_t_copied"), sem("unit_pv")
        o_sq_ready, o_ms_ready, o_ln_done = sem("o_sq_ready"), sem("o_ms_ready"), sem("o_ln_done")
        o_rs_ready, o_n_ready, o_t_ready = sem("o_rs_ready"), sem("o_n_ready"), sem("o_t_ready")
        a_done, a_hi_ready, a_lo_ready = sem("a_done"), sem("a_hi_ready"), sem("a_lo_ready")
        gate_ready, branch_taken = sem("gate_ready"), sem("branch_taken")
        mix_sum, mix_hi_ready, mix_ready = sem("mix_sum"), sem("mix_hi_ready"), sem("mix_ready")
        swa_cache_loaded, swa_k_dup = sem("swa_cache_loaded"), sem("swa_k_dup")
        swa_v_copied, swa_vt_ready, swa_v_ready = sem("swa_v_copied"), sem("swa_vt_ready"), sem("swa_v_ready")
        swa_stored, swa_zeroed = sem("swa_stored"), sem("swa_zeroed")
        swa_scores, swa_row_max, swa_max = sem("swa_scores"), sem("swa_row_max"), sem("swa_max")
        swa_exp, swa_sink_exp = sem("swa_exp"), sem("swa_sink_exp")
        swa_pt_ready, swa_pt_copied, swa_pv = sem("swa_pt_ready"), sem("swa_pt_copied"), sem("swa_pv")
        swa_sum, swa_recip, swa_o_ready = sem("swa_sum"), sem("swa_recip"), sem("swa_o_ready")
        swa_ot_ready, b_hi_ready, b_lo_ready = sem("swa_ot_ready"), sem("b_hi_ready"), sem("b_lo_ready")
        x_rows_loaded, ln_par_loaded = sem("x_rows_loaded"), sem("ln_par_loaded")
        ln_stats, ln_aggr, ln_log, ln_rstd = sem("ln_stats"), sem("ln_aggr"), sem("ln_log"), sem("ln_rstd")
        ln_centred, ln_rows, ln_t_ready = sem("ln_centred"), sem("ln_rows"), sem("ln_t_ready")
        input_rows = sem("input_rows")
        relu_done = [sem(f"relu_done{s}") for s in range(2)]
        sq_done, h_hi_ready, h_ready = sem("sq_done"), sem("h_hi_ready"), sem("h_ready")
        y_stored, keep_stored = sem("y_stored"), sem("keep_stored")
        waits_passed = sem("waits_passed")
        CONST_LOADS = 3
        SMALL_LOADS = 3

        block = ctx.enter_context(nc.Block())

        def nth(l, at_chunk, i=0):
            return l * (CHUNKS // 2) + (at_chunk // 2 + i)

        def tiles_before(l, which):
            return l * (2 * RT) + which * RT

        T_BANKS = (0, 2, 6, 0, 2)

        def transposed_tile(r):
            return flat[:, T_BANKS[r] * BANK:T_BANKS[r] * BANK + D].rearrange("p (k n) -> p k n", k=KT)

        OUT_AT = 6 * BANK

        def transposed_outputs(dst, j):
            out = dst[:, j, :].rearrange("p (t u q) -> p t u q", t=RT, u=2)
            psum = flat[:, OUT_AT:OUT_AT + ROWS].rearrange("p (t g q) -> p t g q", t=RT, g=2)
            return [(out[g * DH:(g + 1) * DH, :, u, :], psum[u * DH:(u + 1) * DH, :, g, :])
                    for g in range(2) for u in range(2)]

        def all_heads(eng, l, head):
            with eng.Fori(0, HEADS // 2 - 1) as i:
                for p in range(2):
                    head(l, 2 * i + p, p, True)
            head(l, HEADS - 2, 0, True)
            head(l, HEADS - 1, 1, False)

        def all_pairs(eng, l, pair):
            with eng.Fori(0, PAIRS // 4) as i:
                for p in range(2):
                    pair(l, 0, i, p, True)
            for i in range(PAIRS // 4, PAIRS // 2):
                for p in range(2):
                    pair(l, 1, i, p, 2 * i + p < PAIRS - 1)

        def wait_apart(eng, semaphore, value):
            eng.wait_ge(semaphore, value)
            eng.sem_inc(waits_passed, 1)

        @block.sync
        def _(sp):
            def load(g, j):
                sp.dma_start(raw[:, j, :], weights[g * RAW_SLOTS + j]).then_inc(raw_loaded[j], 16)

            sp.dma_start(ident[:], ident_d).then_inc(ident_loaded, 16)
            for dst, src in ((col[:], cols), (lam_v[:].rearrange("p a b c -> p (a b c)"), lam_vec),
                             (mask_f[0:DEC_B, :], masks)):
                sp.dma_start(dst, src).then_inc(small_loaded, 16)
            for r in range(RT):
                sp.dma_start(rows[:, r, :], x_rows[r * P:(r + 1) * P, :]).then_inc(x0_loaded[r], 16)
                if r < 2:
                    load(0, r)
            loads = [(cos[:], cos_t), (sin[:], sin_t), (ones[:], ones_d)]
            assert len(loads) == CONST_LOADS
            for dst, src in loads:
                sp.dma_start(dst, src).then_inc(consts_loaded, 16)

            for j in range(2, RAW_SLOTS):
                load(0, j)
            sp.dma_start(swk_keep_out, swa_k_keep).then_inc(keep_stored, 16)
            sp.dma_start(swv_keep_out, swa_v_keep).then_inc(keep_stored, 16)
            with sp.Fori(1, DEPTH * CHUNKS // RAW_SLOTS) as g:
                for j in range(RAW_SLOTS):
                    sp.wait_ge(w_ready[j % 2], 2 * g + (j // 2 - 1))
                    load(g, j)
            sp.wait_ge(keep_stored, 32)

        @block.gpsimd
        def _(pool):
            pool.wait_ge(small_loaded, 16 * SMALL_LOADS)
            with pool.Fori(0, DEPTH * CHUNKS // RAW_SLOTS) as g:
                for j in range(RAW_SLOTS):
                    s = j % 2
                    pool.wait_ge(raw_loaded[j], 16 * (g + 1))
                    pool.wait_ge(chunk_done[s], 2 * g + j // 2)
                    nc.gpsimd.tensor_tensor(w_hi[s][:], raw[:, j, :],
                                            col[:, C_ZERO:C_ZERO + 1].to_broadcast([P, D]),
                                            ALU.add).then_inc(w_hi_made, 1)
                    pool.wait_ge(w_hi_made, 4 * g + (j + 1))
                    nc.gpsimd.tensor_tensor(w_lo[s][:], raw[:, j, :], w_hi[s][:].bitcast(F32),
                                            ALU.subtract).then_inc(w_ready[s], 1)

        @block.tensor
        def _(pe):
            mm = nc.tensor.matmul

            def feature_tile(s, n, hi, lo, which, part=None, between=None):
                for half in (0, 1) if part is None else (part,):
                    if half == 0:
                        pe.wait_ge(w_ready[s], n + 1)
                    out = PS[:, bank_of(which, half), 0:HALF]
                    c = slice(half * HALF, (half + 1) * HALF)
                    for k in range(KT):
                        if between and (half, k) in between:
                            between[half, k]()
                        wh, wl = w_hi[s][:, k * P:(k + 1) * P], w_lo[s][:, k * P:(k + 1) * P]
                        mm(out, wh, hi[:, k, c], start=(k == 0), stop=False)
                        mm(out, wh, lo[:, k, c], start=False, stop=False)
                        last = mm(out, wl, hi[:, k, c], start=False, stop=(k == KT - 1))
                    last.then_inc((chunk_half_done if half == 0 else chunk_done)[s], 1)

            def row_group(n, group, hi, lo, before_k=None):
                for k in range(KT):
                    s, k2 = (k // 2) % 2, k % 2
                    if k2 == 0:
                        pe.wait_ge(w_ready[s], n + (k // 4 + 1))
                    if before_k:
                        before_k(k)
                    wh = w_hi[s][:, k2 * BANK:(k2 + 1) * BANK]
                    wl = w_lo[s][:, k2 * BANK:(k2 + 1) * BANK]
                    for r in range(RT):
                        if k == 0:
                            pe.wait_ge(row_evacuated[r], group)
                        xh, xl = hi[:, k, r * P:(r + 1) * P], lo[:, k, r * P:(r + 1) * P]
                        mm(PS[:, r, :], xh, wh, start=(k == 0), stop=False)
                        mm(PS[:, r, :], xh, wl, start=False, stop=False)
                        last = mm(PS[:, r, :], xl, wh, start=False, stop=(k == KT - 1))
                        if r == RT - 1:
                            last.then_inc((chunk_half_done if k2 == 0 else chunk_done)[s], 1)
                        elif k == KT - 1:
                            last.then_inc(row_acc_ready, 1)

            def rope_pair_free(u):
                pe.wait_ge(rope_swapped, 2 * u)
                pe.wait_ge(rope_cos_done, 2 * u)

            def head_tile(l, h, is_k):
                rope_pair_free(l * ROPES + 2 * h + is_k)
                feature_tile(is_k, nth(l, AT_HEADS) + h, xt_hi, xt_lo, 0)

            def dec_scores_of(l, h, p):
                n = l * HEADS + h
                pe.wait_ge(rope_added, l * ROPES + 2 * h + 2)
                pe.wait_ge(kc_loaded, 16 * (n + 1))
                pe.wait_ge(unit_exp, 4 * n)
                pe.wait_ge(dec_summed, n)
                for g in range(2):
                    old, new = PS[:, 2 * g, :], PS[:, 2 * g + 1, 0:P]
                    for b in range(4):
                        zb = z_dec[:, (4 * g + b) * P:(4 * g + b + 1) * P]
                        mm(old, zb, kc[:, 4 * g + b, :], start=(b == 0), stop=(b == 3))
                    if g == 1:
                        pe.wait_ge(dec_ln_done, n)
                    mm(new, z_all[:, g, :], k_t[p][:, SEQ:ROWS], start=True, stop=False)
                    mm(new, m_own[:, g, :], m_negnew, start=False, stop=True).then_inc(dec_scores, 1)

            def output_transposes(l, h):
                n = l * HEADS + h
                pe.wait_ge(o_n_ready, n + 1)
                pe.wait_ge(unit_t_copied, 4 * n + 4)
                for i in range(4):
                    last = nc.tensor.transpose(PS[:, 6, i * P:(i + 1) * P], o_n[:, i, :], ident[:])
                last.then_inc(o_t_ready, 1)

            def dec_transposes(l, h):
                n = l * HEADS + h
                pe.wait_ge(dec_probs, 2 * n + 2)
                pe.wait_ge(a_done, n)
                pe.wait_ge(o_n_ready, n)
                for t in range(4):
                    last = nc.tensor.transpose(PS[:, 6, t * P:(t + 1) * P], d_a[:, t * P:(t + 1) * P],
                                               ident[:])
                last.then_inc(dec_t_ready, 1)
                nc.tensor.transpose(PS[:, 7, 0:P], d_a[:, SEQ:ROWS], ident[:]).then_inc(dec_t_ready, 1)

            def dec_new_product(l, h):
                n = l * HEADS + h
                pe.wait_ge(dec_t_copied, 2 * n + 2)
                pe.wait_ge(v_new_copied, n + 1)
                mm(PS[:, 7, 2 * P:3 * P], v_new[:], d_at[:, 4, :], start=True, stop=True)\
                    .then_inc(dec_new_ready, 1)

            def dec_product(l, h):
                n = l * HEADS + h
                pe.wait_ge(vc_loaded, 16 * (n + 1))
                pe.wait_ge(unit_exp, 4 * n + 3)
                for half in range(2):
                    for t in range(4):
                        last = mm(PS[:, half, :], d_at[:, t, :], vc[:, t, half * BANK:(half + 1) * BANK],
                                  start=(t == 0), stop=(t == 3))
                last.then_inc(dec_pv, 1)

            def dec_product_transposes(l, h):
                n = l * HEADS + h
                pe.wait_ge(dec_o_copied, n + 1)
                for b in range(DEC_B):
                    last = nc.tensor.transpose(flat[:, b * P:(b + 1) * P], d_o[:, b, :], ident[:])
                last.then_inc(dec_ot_ready, 1)

            def unit_score(l, h, p, i):
                n, w = l * HEADS + h, (i + 1) * P
                if i >= 2:
                    pe.wait_ge(unit_exp, 4 * n + (i - 1))
                for m in range(2):
                    out = PS[:, 2 * (i % 2) + m, :]
                    mm(out[:, 0:w], z_map[p][m][:, i * P:(i + 1) * P], k_t[p][:, 0:w],
                       start=True, stop=False)
                    last = mm(out[:, w - CHUNK:w], m_first, m_neg64, start=False, stop=True)
                last.then_inc(unit_scores, 1)

            def unit_transpose(l, h, i):
                n = 4 * (l * HEADS + h) + i
                pe.wait_ge(unit_probs, n + 1)
                pe.wait_ge(unit_t_copied, n)
                for j in range(i + 1):
                    last = nc.tensor.transpose(PS[:, 6, j * P:(j + 1) * P],
                                               u_a[i % 2][:, j * P:(j + 1) * P], ident[:])
                last.then_inc(unit_t_ready, 1)

            def unit_product(l, h, i):
                n = 4 * (l * HEADS + h) + i
                pe.wait_ge(unit_t_copied, n + 1)
                if i == 0:
                    pe.wait_ge(dec_new_copied, l * HEADS + h + 1)
                for j in range(i + 1):
                    last = mm(PS[:, 7, i * P:(i + 1) * P], u_at[i % 2][:, j * P:(j + 1) * P],
                              rows[:, j, bass.ts(h, P)], start=(j == 0), stop=(j == i))
                last.then_inc(unit_pv, 1)

            def head(l, h, p, more):
                n = l * HEADS + h
                if more:
                    head_tile(l, h + 1, 0)
                dec_transposes(l, h)
                unit_score(l, h, p, 0)
                unit_score(l, h, p, 1)
                if more:
                    head_tile(l, h + 1, 1)
                dec_new_product(l, h)
                for i in range(2):
                    unit_transpose(l, h, i)
                    unit_score(l, h, p, i + 2)
                    unit_product(l, h, i)
                dec_product(l, h)
                unit_transpose(l, h, 2)
                dec_product_transposes(l, h)
                unit_product(l, h, 2)
                unit_transpose(l, h, 3)
                pe.wait_ge(dec_sq_ready, n + 1)
                mm(PS[:, 3, 0:P], ones[:], d_sq[:], start=True, stop=True).then_inc(dec_ms_ready, 1)
                unit_product(l, h, 3)
                if more:
                    dec_scores_of(l, h + 1, 1 - p)
                output_transposes(l, h)

            def pair_scores(l, kv, j, p):
                n = l * PAIRS + j
                pe.wait_ge(rope_added, l * ROPES + (2 * HEADS + 2) + j)
                pe.wait_ge(swa_exp, 2 * n)
                for c in range(SEQ // CHUNK):
                    ws = max(0, c - 1) * CHUNK
                    out = PS[:, c // 4, (c % 4) * P:(c % 4 + 1) * P]
                    zc = zq[p][:, c].rearrange("p g q -> p (g q)")
                    last = mm(out, zc, sk_dup[:, kv, ws:ws + P], start=True, stop=(c > 0))
                    if c == 0:
                        mm(out[:, CHUNK:P], m_all, m_neg64, start=False, stop=True)
                last.then_inc(swa_scores, 1)
                for g in range(2):
                    old, new = PS[:, 2 + g, 0:256], PS[:, 2 + g, 256:384]
                    keys = s_kc[:, kv, 4 * g:4 * g + 4, :].rearrange("p b k -> p (b k)")
                    mm(old, zs[p][:, g, :], keys, start=True, stop=False)
                    mm(old, m_own[:, g, :], m_negold[:, g, :], start=False, stop=True)
                    mm(new, zs[p][:, g, :], sk_dup[:, kv, SEQ:ROWS], start=True, stop=False)
                    last = mm(new, m_own[:, g, :], m_negnew, start=False, stop=True)
                last.then_inc(swa_scores, 1)

            def probs_transposes(n, q):
                pe.wait_ge(swa_exp, 2 * n + q // 2 + 1)
                if q >= 2:
                    pe.wait_ge(swa_pt_copied, 4 * n + (q - 1))
                else:
                    pe.wait_ge(b_lo_ready, n)
                for t in range(4 * q, min(4 * q + 4, 14)):
                    last = nc.tensor.transpose(PS[:, 6 + q % 2, (t % 4) * P:(t % 4 + 1) * P],
                                               s_p[:, t * P:(t + 1) * P], ident[:])
                last.then_inc(swa_pt_ready, 1)

            def pair_output(l, kv, j):
                n = l * PAIRS + j
                pe.wait_ge(swa_pt_copied, 4 * n + 4)
                d = bass.ts(kv, DH)
                for c in range(SEQ // CHUNK):
                    window = 0 if c == 0 else c // 2 if c % 2 else 4 + c // 2 - 1
                    mm(flat[:, OUT_AT + c * DH:OUT_AT + (c + 1) * DH], s_pt[:, c, :],
                       sv_rows[:, window, d], start=True, stop=True)
                for g in range(2):
                    out = flat[:, OUT_AT + (8 + g) * DH:OUT_AT + (9 + g) * DH]
                    mm(out, s_pt[:, 8 + 3 * g, :], s_vc[:, 2 * g, d], start=True, stop=False)
                    mm(out, s_pt[:, 9 + 3 * g, :], s_vc[:, 2 * g + 1, d], start=False, stop=False)
                    last = mm(out, s_pt[:, 10 + 3 * g, :], sv_rows[:, 7, d], start=False, stop=True)
                last.then_inc(swa_pv, 1)
                pe.wait_ge(swa_o_ready, n + 1)
                for t in range(RT):
                    pair_o = s_o[:, 2 * t:2 * t + 2, :].rearrange("p u d -> p (u d)")
                    last = nc.tensor.transpose(flat[:, OUT_AT + t * P:OUT_AT + (t + 1) * P], pair_o,
                                               ident[:])
                last.then_inc(swa_ot_ready, 1)

            def pair_tile(l, i, s, between=None):
                rope_pair_free(l * ROPES + (2 * HEADS + 1) + 2 * i + s)
                feature_tile(s, nth(l, AT_SWA, 1) + i, xt_hi, xt_lo, 0, between=between)

            def window_pair(l, kv, i, p, more):
                j = 2 * i + p
                n = l * PAIRS + j

                def rounds(*qs):
                    return lambda: [probs_transposes(n, q) for q in qs]

                pair_scores(l, kv, j, p)
                if more:
                    pair_tile(l, i + p, 1 - p, {(1, 0): rounds(0, 1), (1, 4): rounds(2, 3)})
                else:
                    rounds(0, 1, 2, 3)()
                pair_output(l, kv, j)

            def x_transposes(l, which, r):
                if which == 0:
                    pe.wait_ge(input_rows, l * RT + r + 1)
                else:
                    pe.wait_ge(ln_rows, l * RT + r + 1)
                if r >= 3:
                    pe.wait_ge(x_lo_ready, tiles_before(l, which) + r - 2)
                for k in range(KT):
                    at_col = T_BANKS[r] * BANK + k * P
                    last = nc.tensor.transpose(flat[:, at_col:at_col + P], rows[:, r, k * P:(k + 1) * P],
                                               ident[:])
                last.then_inc(ln_t_ready, 1)

            def first_tiles(l, which, n):
                for r in range(3):
                    x_transposes(l, which, r)
                for half in range(2):
                    pe.wait_ge(x_hi_ready, tiles_before(l, which) + (3, 5)[half])
                    pe.wait_ge(x_lo_ready, tiles_before(l, which) + (3, 5)[half])
                    for s in range(2):
                        feature_tile(s, n, xt_hi, xt_lo, s, half, between={
                            (0, (6, 4)[s]): lambda: x_transposes(l, which, 3 + s)})

            pe.wait_ge(ident_loaded, 16)
            with pe.Fori(0, DEPTH) as l:
                first_tiles(l, 0, nth(l, AT_HEAD_0))
                pe.wait_ge(rope_swapped, 2 * (l * ROPES + 1))
                wait_apart(pe, rope_cos_done, 2 * (l * ROPES + 1))
                with pe.Fori(0, 2) as v:
                    row_group(nth(l, AT_V) + 2 * v, l * GROUPS + v, xt_hi, xt_lo)
                for r in range(RT):
                    wait_apart(pe, row_evacuated[r], l * GROUPS + 2)
                pe.wait_ge(consts_loaded, 16 * CONST_LOADS)
                pe.wait_ge(masks_ready, 2)
                dec_scores_of(l, 0, 0)
                all_heads(pe, l, head)
                pe.wait_ge(rope_swapped, 2 * (l * ROPES + 2 * HEADS))
                wait_apart(pe, rope_cos_done, 2 * (l * ROPES + 2 * HEADS))
                with pe.Fori(0, KT) as f:
                    pe.wait_ge(gate_ready, l * 16 + f)
                    feature_tile(0, nth(l, AT_BRANCH_A) + f, xt_hi, xt_lo, 0)
                    pe.wait_ge(branch_taken, l * 16 + f)
                    pe.wait_ge(a_done, l * HEADS + HEADS)
                    pe.wait_ge(a_hi_ready, l * KT + KT)
                    pe.wait_ge(a_lo_ready, l * KT + KT)
                    feature_tile(1, nth(l, AT_BRANCH_A) + f, act_b[0], act_b[1], 1)
                pe.wait_ge(gate_ready, l * 16 + 8)
                feature_tile(0, nth(l, AT_SWA), xt_hi, xt_lo, 0)
                pe.wait_ge(branch_taken, l * 16 + 8)
                feature_tile(1, nth(l, AT_SWA), xt_hi, xt_lo, 1)
                pair_tile(l, 0, 0)
                pe.wait_ge(swa_v_copied, l + 1)
                for t in range(8):
                    first = t * P if t < 4 else (t - 4) * P + CHUNK if t < 7 else SEQ
                    last = nc.tensor.transpose(flat[:, t * P:(t + 1) * P], sv_t[:, first:first + P],
                                               ident[:])
                last.then_inc(swa_vt_ready, 1)
                pe.wait_ge(swa_v_ready, l + 1)
                pe.wait_ge(swa_k_dup, l + 1)
                wait_apart(pe, swa_cache_loaded, 32 * (l + 1))
                all_pairs(pe, l, window_pair)
                with pe.Fori(0, KT) as f:
                    pe.wait_ge(gate_ready, l * 16 + 8 + f)
                    rope_pair_free(l * ROPES + ROPES)
                    feature_tile(0, nth(l, AT_BRANCH_B) + f, xt_hi, xt_lo, 0)
                    pe.wait_ge(branch_taken, l * 16 + 8 + f)
                    pe.wait_ge(b_hi_ready, l * PAIRS + PAIRS)
                    pe.wait_ge(b_lo_ready, l * PAIRS + PAIRS)
                    pe.wait_ge(swa_pt_copied, 4 * PAIRS * (l + 1))
                    feature_tile(1, nth(l, AT_BRANCH_B) + f, act_b[0], act_b[1], 1)
                pe.wait_ge(gate_ready, l * 16 + 16)
                wait_apart(pe, branch_taken, l * 16 + 16)
                with pe.Fori(0, 2) as v:
                    row_group(nth(l, AT_O) + 2 * v, l * GROUPS + 2 + v, act_a[0], act_a[1],
                              lambda k: pe.wait_ge(mix_ready, l * KT + k + 1))
                for part in range(FF_PARTS):
                    hidden = act_b if part % 2 == 0 else act_a
                    if part == 0:
                        pe.wait_ge(row_evacuated[RT - 1], l * GROUPS + 4)
                        first_tiles(l, 1, nth(l, AT_FF))
                    with pe.Fori(1 if part == 0 else 0, KT // 2) as u:
                        for s in range(2):
                            pe.wait_ge(relu_done[s], l * 16 + 4 * part + u)
                            if s == 0:
                                pe.wait_ge(row_evacuated[RT - 1], l * GROUPS + 4 + 2 * part)
                            feature_tile(s, nth(l, AT_FF) + 8 * part + u, xt_hi, xt_lo, s)
                    wait_apart(pe, relu_done[0], l * 16 + 4 * part + 4)
                    with pe.Fori(0, 2) as v:
                        row_group(nth(l, AT_FF) + 8 * part + 4 + 2 * v, l * GROUPS + 4 + 2 * part + v,
                                  hidden[0], hidden[1],
                                  lambda k: pe.wait_ge(h_ready, l * 32 + 8 * part + k + 1))

        @block.scalar
        def _(act):
            fn = nc.scalar.activation

            def swap_half(l, u, s, n, scale, half):
                act.wait_ge((chunk_half_done, chunk_done)[half][s], n + 1)
                act.wait_ge(rope_added, u)
                for a in range(0, P, DH):
                    for dst, src in ((a, a + DH // 2), (a + DH // 2, a)):
                        last = fn(rope_s[dst:dst + 32, half * HALF:(half + 1) * HALF],
                                  PS[src:src + 32, bank_of(0, half), 0:HALF], ACT.Copy, scale=scale)
                last.then_inc(rope_swapped, 1)

            def swap(l, u, s, n, scale, which=0):
                act.wait_ge(chunk_done[s], n + 1)
                act.wait_ge(rope_added, u)
                for a in range(0, P, DH):
                    for dst, src in ((a, a + DH // 2), (a + DH // 2, a)):
                        last = fn(halves(rope_s[dst:dst + 32, :]), pair(which)[src:src + 32], ACT.Copy,
                                  scale=scale)
                last.then_inc(rope_swapped, 2)

            def x_high(l, which, r):
                act.wait_ge(ln_t_ready, tiles_before(l, which) + r + 1)
                fn(xt_hi[:, :, r * P:(r + 1) * P], transposed_tile(r), ACT.Copy).then_inc(x_hi_ready, 1)

            def q_swap(l, h):
                for half in range(2):
                    swap_half(l, l * ROPES + 2 * h, 0, nth(l, AT_HEADS) + h, QK_SCALE, half)

            def k_swap(l, h):
                swap(l, l * ROPES + 2 * h + 1, 1, nth(l, AT_HEADS) + h, 1.0)

            def pair_swap(l, j, i, s, half):
                swap_half(l, l * ROPES + (2 * HEADS + 1) + j, s, nth(l, AT_SWA, 1) + i, QK_SCALE, half)

            def load_cache(kind, l, h):
                if kind == 0:
                    act.dma_start(kc[:].rearrange("p b k -> p (b k)"), k_cache[l, h]).then_inc(kc_loaded, 16)
                else:
                    act.dma_start(vc[:].rearrange("p t n -> p (t n)"), v_cache[l, h]).then_inc(vc_loaded, 16)

            def unit_exps(l, h, i):
                n, w = 4 * (l * HEADS + h) + i, (i + 1) * P
                act.wait_ge(unit_max, n + 1)
                for m in range(2):
                    last = fn(u_p[i % 2][:, m, 0:w], PS[:, 2 * (i % 2) + m, 0:w], ACT.Exp,
                              bias=u_nm[i % 2][:, m:m + 1], accum_out=u_l[i % 2][:, m:m + 1])
                last.then_inc(unit_exp, 1)

            def unit_copy(l, h, i):
                n, w = 4 * (l * HEADS + h) + i, (i + 1) * P
                act.wait_ge(unit_t_ready, n + 1)
                act.wait_ge(unit_pv, 4 * (l * HEADS + h) + max(0, i - 1))
                fn(u_at[i % 2][:, 0:w], PS[:, 6, 0:w], ACT.Copy).then_inc(unit_t_copied, 1)

            def dec_exps(l, h):
                n = l * HEADS + h
                for g in range(2):
                    act.wait_ge(dec_max, 2 * n + g + 1)
                    fn(d_p[:, g, :], flat[:, 1024 * g:1024 * g + ROWS], ACT.Exp,
                       bias=d_nm[:, g:g + 1], accum_out=d_l[:, g:g + 1]).then_inc(dec_exp, 1)

            def head(l, h, p, more):
                n = l * HEADS + h
                act.dma_start(k_out[l, h], k_t[p][:]).then_inc(k_stored[p], 16)
                if more:
                    load_cache(0, l, h + 1)
                act.wait_ge(dec_r_ready, n + 1)
                fn(d_t[0:64], d_p[64:128, 0, :], ACT.Copy, scale=d_r[64:128, 0:1])
                fn(d_t[64:128], d_p[0:64, 1, :], ACT.Copy, scale=d_r[0:64, 1:2]).then_inc(dec_shifted, 1)
                wait_apart(act, dec_new_ready, n)
                fn(v_new[:], rows[:, RT - 1, bass.ts(h, P)], ACT.Copy).then_inc(v_new_copied, 1)
                if more:
                    q_swap(l, h + 1)
                act.wait_ge(dec_t_ready, 2 * n + 1)
                fn(d_at[:, 0:4, :].rearrange("p t n -> p (t n)"), PS[:, 6, :], ACT.Copy)\
                    .then_inc(dec_t_copied, 1)
                act.wait_ge(dec_t_ready, 2 * n + 2)
                fn(d_at[:, 4, :], PS[:, 7, 0:P], ACT.Copy).then_inc(dec_t_copied, 1)
                unit_exps(l, h, 0)
                unit_exps(l, h, 1)
                act.wait_ge(dec_new_ready, n + 1)
                act.wait_ge(dec_summed, n)
                fn(d_on[:], PS[:, 7, 2 * P:3 * P], ACT.Copy).then_inc(dec_new_copied, 1)
                unit_copy(l, h, 0)
                unit_exps(l, h, 2)
                unit_copy(l, h, 1)
                if more:
                    k_swap(l, h + 1)
                unit_exps(l, h, 3)
                act.wait_ge(dec_pv, n + 1)
                if more:
                    load_cache(1, l, h + 1)
                fn(d_o[:].rearrange("p b e -> p (b e)"), flat[:, 0:DEC_B * P], ACT.Copy)\
                    .then_inc(dec_o_copied, 1)
                unit_copy(l, h, 2)
                act.wait_ge(dec_summed, n + 1)
                fn(d_sq[:], d_out[:], ACT.Square).then_inc(dec_sq_ready, 1)
                unit_copy(l, h, 3)
                act.wait_ge(unit_pv, 4 * n + 4)
                fn(o_sq[:].rearrange("p t n -> p (t n)"), PS[:, 7, :], ACT.Square).then_inc(o_sq_ready, 1)
                act.wait_ge(dec_ms_ready, n + 1)
                fn(d_rs[:], PS[:, 3, 0:P], ACT.Ln, bias=eps).then_inc(dec_ln_done, 1)
                act.wait_ge(o_ms_ready, n + 1)
                fn(o_rs, o_ms, ACT.Ln, bias=eps, scale=1.0 / P).then_inc(o_ln_done, 1)
                act.wait_ge(o_ln_done, n + 1)
                fn(o_rs, o_rs, ACT.Exp, scale=-0.5).then_inc(o_rs_ready, 1)
                act.wait_ge(dec_ln_done, n + 1)
                fn(d_rs[:], d_rs[:], ACT.Exp, scale=-0.5).then_inc(dec_rs_ready, 1)
                if more:
                    dec_exps(l, h + 1)
                wait_apart(act, o_t_ready, n + 1)
                fn(a_t[:, h, 0:SEQ], PS[:, 6, :], ACT.Copy, scale=g_sub[:, bass.ds(l, 1)])\
                    .then_inc(a_done, 1)

            def gate_tile(l, n, f, x):
                act.wait_ge(chunk_done[0], n + 1)
                act.wait_ge(branch_taken, x)
                fn(halves(tmp1[:]), pair(0), ACT.Sigmoid).then_inc(gate_ready, 1)

            def window_pair(l, kv, i, p, more):
                n = l * PAIRS + 2 * i + p
                act.wait_ge(swa_max, 2 * n + 1)
                for c in range(8):
                    last = fn(s_p[:, c * P:(c + 1) * P], flat[:, c * P:(c + 1) * P], ACT.Exp,
                              bias=s_nm[:, c:c + 1], accum_out=s_l[:, c:c + 1])
                last.then_inc(swa_exp, 1)
                act.wait_ge(swa_max, 2 * n + 2)
                for g in range(2):
                    last = fn(s_p[:, 1024 + g * 384:1024 + (g + 1) * 384], PS[:, 2 + g, 0:384], ACT.Exp,
                              bias=s_nm[:, 8 + g:9 + g], accum_out=s_l[:, 8 + g:9 + g])
                last.then_inc(swa_exp, 1)
                fn(s_e, s_nm, ACT.Exp, bias=col[:, bass.ds(C_SINK + l * PAIRS + 2 * i + p, 1)])\
                    .then_inc(swa_sink_exp, 1)
                for q in range(4):
                    act.wait_ge(swa_pt_ready, 4 * n + q + 1)
                    if q == 0:
                        act.wait_ge(swa_pv, n)
                    k = min(4 * q + 4, 14) - 4 * q
                    fn(s_pt[:, 4 * q:4 * q + k, :].rearrange("p t n -> p (t n)"),
                       PS[:, 6 + q % 2, 0:k * P], ACT.Copy).then_inc(swa_pt_copied, 1)
                    if more and q % 2:
                        pair_swap(l, 2 * i + p + 1, i + p, 1 - p, q // 2)
                wait_apart(act, swa_ot_ready, n + 1)
                for dst, src in transposed_outputs(act_b[0], 2 * i + p):
                    last = fn(dst, src, ACT.Copy)
                last.then_inc(b_hi_ready, 1)

            eps = col[:, C_EPS:C_EPS + 1]
            act.wait_ge(small_loaded, 16 * SMALL_LOADS)
            act.wait_ge(lam_sum, 1)
            fn(lam2, lam2, ACT.Exp).then_inc(lam_exp, 1)
            for r in range(RT):
                act.wait_ge(x0_loaded[r], 16)
            with act.Fori(0, DEPTH) as l:
                act.wait_ge(ln_aggr, l * (2 * RT))
                load_cache(0, l, 0)
                load_cache(1, l, 0)
                for r in range(RT):
                    x_high(l, 0, r)
                act.wait_ge(input_rows, l * RT + RT)
                act.dma_start(x_all[l].rearrange("(r p) d -> p r d", p=P), rows[:]).then_inc(y_stored, 16)
                for is_k in range(2):
                    swap(l, l * ROPES + is_k, is_k, nth(l, AT_HEAD_0),
                         1.0 if is_k else QK_SCALE, is_k)
                for r in range(RT):
                    act.wait_ge(row_evacuated[r], l * GROUPS + 2)
                act.dma_start(v_out[l], rows[:]).then_inc(v_stored, 16)
                dec_exps(l, 0)
                all_heads(act, l, head)
                act.wait_ge(v_stored, 16 * (l + 1))
                act.dma_start(s_kc[:].rearrange("p a b k -> p (a b k)"), swa_kc[l])\
                    .then_inc(swa_cache_loaded, 16)
                act.dma_start(s_vc[:].rearrange("p t n -> p (t n)"), swa_vc[l])\
                    .then_inc(swa_cache_loaded, 16)
                act.wait_ge(dec_done, HEADS * (l + 1))
                act.wait_ge(a_done, HEADS * (l + 1))
                with act.Fori(0, KT) as k:
                    fn(act_b[0][:, k, :], a_t[:, k, :], ACT.Copy).then_inc(a_hi_ready, 1)
                with act.Fori(0, KT) as f:
                    gate_tile(l, nth(l, AT_BRANCH_A) + f, f, l * 16 + f)
                act.wait_ge(branch_taken, l * 16 + 8)
                swap(l, l * ROPES + 2 * HEADS, 0, nth(l, AT_SWA), 1.0)
                act.wait_ge(chunk_done[1], nth(l, AT_SWA) + 1)
                act.wait_ge(a_lo_ready, KT * (l + 1))
                fn(halves(sv_t[:]), pair(1), ACT.Copy).then_inc(swa_v_copied, 1)
                act.wait_ge(rope_added, l * ROPES + 2 * HEADS + 1)
                for kv in range(2):
                    for half in range(2):
                        last = fn(sk_dup[half * DH:(half + 1) * DH, kv, :], sk_t[kv * DH:(kv + 1) * DH, :],
                                  ACT.Copy)
                last.then_inc(swa_k_dup, 1)
                act.wait_ge(swa_v_copied, l + 1)
                for dst, src in ((swk_out, sk_t), (swv_out, sv_t)):
                    act.dma_start(dst[l], src[:, SEQ - 2 * CHUNK:ROWS]).then_inc(swa_stored, 16)
                act.wait_ge(swa_vt_ready, l + 1)
                fn(sv_rows[:].rearrange("p t n -> p (t n)"), flat[:, 0:1024], ACT.Copy)\
                    .then_inc(swa_v_ready, 1)
                for half in range(2):
                    pair_swap(l, 0, 0, 0, half)
                all_pairs(act, l, window_pair)
                act.wait_ge(swa_pv, PAIRS * (l + 1))
                act.wait_ge(y_stored, 16 * (l + 1))
                act.dma_start(rows[:], x_all[l].rearrange("(r p) d -> p r d", p=P))\
                    .then_inc(x_rows_loaded, 16)
                act.wait_ge(swa_stored, 32 * (l + 1))
                with act.Fori(0, KT) as f:
                    gate_tile(l, nth(l, AT_BRANCH_B) + f, f, l * 16 + 8 + f)
                    wait_apart(act, mix_sum, l * KT + f + 1)
                    fn(act_a[0][:, f, :], tmp2[:], ACT.Copy).then_inc(mix_hi_ready, 1)

                def load_norm(which):
                    act.dma_start(ln_g[:], ln_par[l, which, 0]).then_inc(ln_par_loaded, 16)
                    act.dma_start(ln_b[:], ln_par[l, which, 1]).then_inc(ln_par_loaded, 16)

                def rstds(which):
                    n = 2 * l + which
                    act.wait_ge(ln_aggr, RT * (n + 1))
                    fn(ln_mv[:, :, 2], ln_mv[:, :, 1], ACT.Ln, bias=eps).then_inc(ln_log, 1)
                    act.wait_ge(ln_log, n + 1)
                    fn(ln_mv[:, :, 3], ln_mv[:, :, 2], ACT.Exp, scale=-0.5).then_inc(ln_rstd, 1)

                act.wait_ge(mix_ready, KT * (l + 1))
                load_norm(0)
                rstds(0)
                for r in range(RT):
                    x_high(l, 1, r)
                load_norm(1)
                with act.Fori(0, FF_PARTS // 2) as i:
                    for p in range(2):
                        hidden = act_b if p == 0 else act_a
                        with act.Fori(0, KT // 2) as u:
                            for s in range(2):
                                t = l * 32 + (2 * i + p) * 8 + 2 * u + s
                                act.wait_ge(chunk_done[s], nth(l, AT_FF) + (2 * i + p) * 8 + u + 1)
                                act.wait_ge(sq_done, t)
                                fn(halves(tmp1[:]), pair(s), ACT.Relu).then_inc(relu_done[s], 1)
                                wait_apart(act, sq_done, t + 1)
                                fn(hidden[0][:, 2 * u + s, :], tmp2[:], ACT.Copy).then_inc(h_hi_ready, 1)
                rstds(1)
            act.wait_ge(input_rows, (DEPTH + 1) * RT)
            act.dma_start(x_all[DEPTH].rearrange("(r p) d -> p r d", p=P), rows[:]).then_inc(y_stored, 16)
            act.wait_ge(y_stored, 16 * (DEPTH + 1))
            act.wait_ge(v_stored, 16 * DEPTH)
            act.wait_ge(swa_stored, 32 * DEPTH)
            for p in range(2):
                act.wait_ge(k_stored[p], 16 * DEPTH * HEADS // 2)

        @block.vector
        def _(dve):
            v = nc.vector

            def rotate(l, u, s, n, scale, adds, before_adds=None, which=0, apart=False):
                dve.wait_ge(rope_added, u)
                for half in range(2) if apart else (1,):
                    dve.wait_ge((chunk_half_done, chunk_done)[half][s], n + 1)
                    dve.wait_ge(rope_swapped, 2 * u + half + 1)
                    if apart:
                        c = slice(half * HALF, (half + 1) * HALF)
                        v.scalar_tensor_tensor(rope_c[:, c], PS[:, bank_of(which, half), 0:HALF], scale,
                                               cos[:, c], ALU.mult, ALU.mult).then_inc(rope_cos_done, 1)
                        v.tensor_tensor(rope_s[:, c], rope_s[:, c], sin[:, c], ALU.mult)\
                            .then_inc(rope_sin_done, 1)
                    else:
                        v.scalar_tensor_tensor(halves(rope_c[:]), pair(which), scale, halves(cos[:]),
                                               ALU.mult, ALU.mult).then_inc(rope_cos_done, 2)
                        v.tensor_tensor(rope_s[:], rope_s[:], sin[:], ALU.mult).then_inc(rope_sin_done, 2)
                if before_adds:
                    before_adds()
                dve.wait_ge(rope_cos_done, 2 * u + 2)
                dve.wait_ge(rope_sin_done, 2 * u + 2)
                for out, parts, shape_cols in adds:
                    last = v.tensor_tensor(out, shape_cols(rope_c[parts]), shape_cols(rope_s[parts]),
                                           ALU.add)
                last.then_inc(rope_added, 1)

            LOW, HIGH = slice(0, DH), slice(DH, P)

            def rotate_q(l, h, p, at_chunk=AT_HEADS):
                def samples(g, split):
                    cs = slice(SEQ + g * DH, SEQ + (g + 1) * DH)
                    if split:
                        return lambda t: t[:, cs].rearrange("p (b q) -> p b q", b=4)
                    return lambda t: t[:, cs]

                adds = [(z_map[p][0][LOW, :], LOW, lambda t: t[:, 0:SEQ]),
                        (z_map[p][1][HIGH, :], HIGH, lambda t: t[:, 0:SEQ])]
                for g in range(2):
                    for m, parts in ((0, LOW), (1, HIGH)):
                        side = (m ^ g) * DH
                        adds.append((z_all[parts, g, side:side + DH], parts, samples(g, False)))
                        first = g * 4 * P + side
                        own = z_dec[parts, first:first + 4 * (P + DEC_T)]\
                            .rearrange("p (b c) -> p b c", b=4)[:, :, 0:DEC_T]
                        adds.append((own, parts, samples(g, True)))
                rotate(l, l * ROPES + 2 * h, 0, nth(l, at_chunk) + h, QK_SCALE, adds,
                       lambda: dve.wait_ge(dec_scores, 2 * (l * HEADS + h)),
                       apart=at_chunk != AT_HEAD_0)

            def rotate_k(l, h, p, nth_use, at_chunk=AT_HEADS, which=0):
                rotate(l, l * ROPES + 2 * h + 1, 1, nth(l, at_chunk) + h, 1.0,
                       [(k_t[p][:], slice(0, P), lambda t: t[:])],
                       lambda: dve.wait_ge(k_stored[p], 16 * nth_use), which)

            def unit_maxes(l, h, i):
                n, w = 4 * (l * HEADS + h) + i, (i + 1) * P
                dve.wait_ge(unit_scores, n + 1)
                two = PS[:, 2 * (i % 2):2 * (i % 2) + 2, 0:w]
                v.tensor_reduce(u_nm[i % 2], two, AX_X, ALU.max, negate=True).then_inc(unit_max, 1)

            def unit_combine(l, h, i):
                n, w = 4 * (l * HEADS + h) + i, (i + 1) * P
                dve.wait_ge(unit_exp, n + 1)
                dve.wait_ge(unit_probs, n)
                v.reciprocal(u_r, u_l[i % 2]).then_inc(unit_recip, 1)
                dve.wait_ge(unit_recip, n + 1)
                v.tensor_tensor(u_r[:, 1:2], u_r[:, 1:2], neg_lam[:, bass.ds(l, 1)], ALU.mult)\
                    .then_inc(unit_r_ready, 1)
                dve.wait_ge(unit_r_ready, n + 1)
                v.tensor_scalar(u_p[i % 2][:, 1, 0:w], u_p[i % 2][:, 1, 0:w], u_r[:, 1:2], None, ALU.mult)\
                    .then_inc(unit_second, 1)
                dve.wait_ge(unit_second, n + 1)
                dve.wait_ge(unit_t_ready, 4 * (l * HEADS + h) + max(0, i - 1))
                v.scalar_tensor_tensor(u_a[i % 2][:, 0:w], u_p[i % 2][:, 0, 0:w], u_r[:, 0:1],
                                       u_p[i % 2][:, 1, 0:w], ALU.mult, ALU.add).then_inc(unit_probs, 1)

            def head(l, h, p, more, next_uses):
                n = l * HEADS + h
                for g in range(2):
                    dve.wait_ge(dec_scores, 2 * n + g + 1)
                    v.tensor_reduce(d_nm[:, g:g + 1], flat[:, 1024 * g:1024 * g + ROWS], AX_X, ALU.max,
                                    negate=True).then_inc(dec_max, 1)
                dve.wait_ge(dec_exp, 2 * n + 2)
                v.reciprocal(d_r, d_l).then_inc(dec_recip, 1)
                dve.wait_ge(dec_recip, n + 1)
                for g, parts in ((0, HIGH), (1, LOW)):
                    last = v.tensor_tensor(d_r[parts, g:g + 1], d_r[parts, g:g + 1],
                                           neg_lam[parts, bass.ds(l, 1)], ALU.mult)
                last.then_inc(dec_r_ready, 1)
                dve.wait_ge(dec_shifted, n + 1)
                dve.wait_ge(o_t_ready, n)
                for g, parts in ((0, LOW), (1, HIGH)):
                    v.scalar_tensor_tensor(d_a[parts], d_p[parts, g, :], d_r[parts, g:g + 1], d_t[parts],
                                           ALU.mult, ALU.add).then_inc(dec_probs, 1)
                if more:
                    rotate_q(l, h + 1, 1 - p)
                unit_maxes(l, h, 0)
                unit_maxes(l, h, 1)
                unit_combine(l, h, 0)
                unit_combine(l, h, 1)
                unit_maxes(l, h, 2)
                unit_maxes(l, h, 3)
                if more:
                    rotate_k(l, h + 1, 1 - p, next_uses)
                unit_combine(l, h, 2)
                unit_combine(l, h, 3)
                dve.wait_ge(dec_ot_ready, n + 1)
                own = flat[:, 0:DEC_B * (P + DEC_T)].rearrange("p (b c) -> p b c", b=DEC_B)[:, :, 0:DEC_T]
                v.tensor_tensor(d_out[:].rearrange("p (b t) -> p b t", b=DEC_B), own,
                                d_on[:].rearrange("p (b t) -> p b t", b=DEC_B), ALU.add)\
                    .then_inc(dec_summed, 1)
                dve.wait_ge(o_sq_ready, n + 1)
                v.tensor_reduce(o_ms, o_sq[:], AX_X, ALU.add).then_inc(o_ms_ready, 1)
                dve.wait_ge(o_rs_ready, n + 1)
                dve.wait_ge(dec_t_ready, 2 * n + 2)
                v.tensor_tensor(o_n[:], PS[:, 7, :].rearrange("p (i e) -> p i e", i=4),
                                o_rs.unsqueeze(2).to_broadcast([P, 4, P]), ALU.mult)\
                    .then_inc(o_n_ready, 1)
                dve.wait_ge(dec_rs_ready, n + 1)
                v.scalar_tensor_tensor(a_t[:, h, SEQ:ROWS], d_out[:], g_sub[:, bass.ds(l, 1)], d_rs[:],
                                       ALU.mult, ALU.mult).then_inc(dec_done, 1)

            def branch_tile(l, at_chunk, f, x, out):
                dve.wait_ge(gate_ready, x + 1)
                dve.wait_ge(chunk_done[1], nth(l, at_chunk) + f + 1)
                v.tensor_tensor(halves(out), pair(1), halves(tmp1[:]), ALU.mult).then_inc(branch_taken, 1)

            def window_pair(l, kv, i, p, more):
                n = l * PAIRS + 2 * i + p
                sink = col[:, bass.ds(C_SINK + l * PAIRS + 2 * i + p, 1)]
                for part, (units, scores) in enumerate((
                        (slice(0, 8), flat[:, 0:1024].rearrange("p (c k) -> p c k", c=8)),
                        (slice(8, 10), PS[:, 2:4, 0:384]))):
                    dve.wait_ge(swa_scores, 2 * n + part + 1)
                    v.tensor_reduce(s_nm[:, units], scores, AX_X, ALU.max).then_inc(swa_row_max, 1)
                    dve.wait_ge(swa_row_max, 2 * n + part + 1)
                    v.tensor_scalar(s_nm[:, units], s_nm[:, units], sink, -1.0, ALU.max, ALU.mult)\
                        .then_inc(swa_max, 1)
                dve.wait_ge(swa_exp, 2 * n + 2)
                dve.wait_ge(swa_sink_exp, n + 1)
                v.tensor_tensor(s_l, s_l, s_e, ALU.add).then_inc(swa_sum, 1)
                dve.wait_ge(swa_sum, n + 1)
                v.reciprocal(s_l, s_l).then_inc(swa_recip, 1)

                def normalise():
                    dve.wait_ge(swa_recip, n + 1)
                    dve.wait_ge(swa_pv, n + 1)
                    v.tensor_tensor(s_o[:], flat[:, OUT_AT:OUT_AT + ROWS].rearrange("p (u d) -> p u d", d=DH),
                                    s_l.unsqueeze(2).to_broadcast([P, 10, DH]), ALU.mult)\
                        .then_inc(swa_o_ready, 1)

                if more:
                    rotate_pair(l, i + p, 1 - p, normalise)
                else:
                    normalise()
                dve.wait_ge(b_hi_ready, n + 1)
                for (lo, src), (hi, _) in zip(transposed_outputs(act_b[1], 2 * i + p),
                                              transposed_outputs(act_b[0].bitcast(F32), 2 * i + p)):
                    last = v.tensor_tensor(lo, src, hi, ALU.subtract)
                last.then_inc(b_lo_ready, 1)

            def rotate_pair(l, i, p, before_adds=None):
                adds = []
                for g, parts in ((0, LOW), (1, HIGH)):
                    adds.append((zq[p][parts, :, g, :], parts,
                                 lambda t: t[:, 0:SEQ].rearrange("p (c q) -> p c q", q=CHUNK)))
                    adds.append((zs[p][parts, :, g * DH:(g + 1) * DH], parts,
                                 lambda t: t[:, SEQ:ROWS].rearrange("p (g q) -> p g q", g=2)))
                rotate(l, l * ROPES + (2 * HEADS + 1) + 2 * i + p, p, nth(l, AT_SWA, 1) + i, QK_SCALE, adds,
                       before_adds, apart=True)

            def x_low(l, which, r):
                n = tiles_before(l, which) + r
                dve.wait_ge(x_hi_ready, n + 1)
                c = slice(r * P, (r + 1) * P)
                v.tensor_tensor(xt_lo[:, :, c], transposed_tile(r), xt_hi[:, :, c].bitcast(F32),
                                ALU.subtract).then_inc(x_lo_ready, 1)

            def norm(l, which):
                x0 = l * (2 * RT) + which * RT
                wait_apart(dve, ln_stats, RT * (l * (GROUPS - 2) + (2 if which == 0 else GROUPS - 2)))
                for r in range(RT):
                    v.bn_aggr(ln_mv[:, r, 0:2], ln_st[:, r].rearrange("p a b -> p (a b)"))\
                        .then_inc(ln_aggr, 1)
                dve.wait_ge(ln_par_loaded, 32 * (2 * l + which + 1))

                def centre(r):
                    dve.wait_ge(ln_aggr, x0 + r + 1)
                    v.scalar_tensor_tensor(rows[:, r, :], rows[:, r, :], ln_mv[:, r, 0:1], ln_g[:],
                                           ALU.subtract, ALU.mult).then_inc(ln_centred, 1)

                def finish(r):
                    dve.wait_ge(ln_centred, x0 + r + 1)
                    dve.wait_ge(ln_rstd, 2 * l + which + 1)
                    v.scalar_tensor_tensor(rows[:, r, :], rows[:, r, :], ln_mv[:, r, 3:4], ln_b[:],
                                           ALU.mult, ALU.add).then_inc(input_rows if which else ln_rows, 1)

                for step, r in ((centre, 0), (centre, 1), (finish, 0), (finish, 1), (centre, 2), (finish, 2)):
                    step(r)
                if which == 0:
                    for r in range(3):
                        x_low(l, 1, r)
                for r in range(3, RT):
                    centre(r)
                    finish(r)
                if which == 0:
                    for r in range(3, RT):
                        x_low(l, 1, r)

            def take_group(group, n, out, residual=None, half=None):
                for r in range(RT):
                    if r < RT - 1:
                        dve.wait_ge(row_acc_ready, group * (RT - 1) + r + 1)
                    else:
                        dve.wait_ge(chunk_done[1], n)
                    if residual is None:
                        v.tensor_copy(out(r), PS[:, r, :]).then_inc(row_evacuated[r], 1)
                    else:
                        v.scalar_tensor_tensor(out(r), out(r), residual, PS[:, r, :], ALU.mult,
                                               ALU.add).then_inc(row_evacuated[r], 1)
                if residual is not None:
                    for r in range(RT):
                        wait_apart(dve, row_evacuated[r], group + 1)
                        v.bn_stats(ln_st[:, r, half, :], out(r)).then_inc(ln_stats, 1)

            def half_rows(h):
                return lambda r: rows[:, r, bass.ts(h, BANK)]

            v.memset(mask_cols[:], 0.0).then_inc(masks_ready, 1)
            dve.wait_ge(small_loaded, 16 * SMALL_LOADS)
            dve.wait_ge(masks_ready, 1)
            v.tensor_copy(mask_cols[0:DEC_B, :], mask_f[0:DEC_B, :]).then_inc(masks_ready, 1)
            prod = tmp1[:, 0:2 * DEPTH * DH].rearrange("p (a l d) -> p a l d", a=2, l=DEPTH)
            for a in range(2):
                last = v.tensor_tensor(prod[:, a], lam_v[:, :, 2 * a, :], lam_v[:, :, 2 * a + 1, :],
                                       ALU.mult)
            last.then_inc(lam_link, 1)
            dve.wait_ge(lam_link, 1)
            v.tensor_reduce(lam2, prod.rearrange("p a l d -> p (a l) d"), AX_X, ALU.add)\
                .then_inc(lam_sum, 1)
            dve.wait_ge(lam_exp, 1)
            v.tensor_tensor(neg_lam[:], lam2[:, DEPTH:2 * DEPTH], lam2[:, 0:DEPTH], ALU.subtract)\
                .then_inc(lam_link, 1)
            dve.wait_ge(lam_link, 2)
            v.tensor_tensor(neg_lam[:], neg_lam[:], col[:, C_LAM_INIT:C_LAM_INIT + DEPTH], ALU.subtract)
            v.tensor_tensor(g_sub[:], col[:, C_SUBLN:C_SUBLN + DEPTH],
                            col[:, C_ONE_MINUS:C_ONE_MINUS + DEPTH], ALU.mult).then_inc(lam_link, 1)
            dve.wait_ge(lam_link, 3)
            dve.wait_ge(masks_ready, 2)
            for r in range(RT):
                dve.wait_ge(x0_loaded[r], 16)
                dve.sem_inc(input_rows, 1)
            with dve.Fori(0, DEPTH) as l:
                for r in range(RT):
                    x_low(l, 0, r)
                dve.wait_ge(input_rows, l * RT + RT)
                for p in range(2):
                    v.memset(z_map[p][0][HIGH, :], 0.0)
                    v.memset(z_map[p][1][LOW, :], 0.0)
                v.memset(z_all[:], 0.0)
                v.memset(z_dec[:], 0.0).then_inc(z_zeroed, 1)
                dve.wait_ge(z_zeroed, l + 1)
                dve.wait_ge(consts_loaded, 16 * CONST_LOADS)
                rotate_q(l, 0, 0, AT_HEAD_0)
                rotate_k(l, 0, 0, l * (HEADS // 2), AT_HEAD_0, 1)
                wait_apart(dve, y_stored, 16 * (l + 1))
                with dve.Fori(0, 2) as half:
                    take_group(l * GROUPS + half, nth(l, AT_V) + 2 * half + 2, half_rows(half))
                with dve.Fori(0, HEADS // 2 - 1) as i:
                    for p in range(2):
                        head(l, 2 * i + p, p, True, l * (HEADS // 2) + i + p)
                head(l, HEADS - 2, 0, True, l * (HEADS // 2) + HEADS // 2 - 1)
                head(l, HEADS - 1, 1, False, None)
                dve.wait_ge(a_done, HEADS * (l + 1))
                wait_apart(dve, dec_done, HEADS * (l + 1))
                with dve.Fori(0, KT) as k:
                    dve.wait_ge(a_hi_ready, l * KT + k + 1)
                    v.tensor_tensor(act_b[1][:, k, :], a_t[:, k, :], act_b[0][:, k, :].bitcast(F32),
                                    ALU.subtract).then_inc(a_lo_ready, 1)
                with dve.Fori(0, KT) as f:
                    branch_tile(l, AT_BRANCH_A, f, l * 16 + f, mix_a[:, f, :])
                dve.wait_ge(a_lo_ready, KT * (l + 1))
                for p in range(2):
                    v.memset(zq[p][:], 0.0)
                    last = v.memset(zs[p][:], 0.0)
                last.then_inc(swa_zeroed, 1)
                rotate(l, l * ROPES + 2 * HEADS, 0, nth(l, AT_SWA), 1.0,
                       [(sk_t[:], slice(0, P), lambda t: t[:])])
                dve.wait_ge(swa_zeroed, l + 1)
                rotate_pair(l, 0, 0)
                all_pairs(dve, l, window_pair)
                dve.wait_ge(swa_stored, 32 * (l + 1))
                wait_apart(dve, rope_added, l * ROPES + ROPES)
                with dve.Fori(0, KT) as f:
                    n = l * KT + f
                    dve.wait_ge(mix_ready, n)
                    branch_tile(l, AT_BRANCH_B, f, l * 16 + 8 + f, tmp2[:])
                    dve.wait_ge(branch_taken, l * 16 + 8 + f + 1)
                    v.tensor_tensor(tmp2[:], tmp2[:], mix_a[:, f, :], ALU.add).then_inc(mix_sum, 1)
                    dve.wait_ge(mix_hi_ready, n + 1)
                    v.tensor_tensor(act_a[1][:, f, :], tmp2[:], act_a[0][:, f, :].bitcast(F32),
                                    ALU.subtract).then_inc(mix_ready, 1)
                wait_apart(dve, x_rows_loaded, 16 * (l + 1))
                with dve.Fori(0, 2) as half:
                    take_group(l * GROUPS + 2 + half, nth(l, AT_O) + 2 * half + 2, half_rows(half), ALPHA,
                               half)
                norm(l, 0)
                for part in range(FF_PARTS):
                    hidden = act_b if part % 2 == 0 else act_a
                    with dve.Fori(0, KT // 2) as u:
                        for s in range(2):
                            t = l * 32 + part * 8 + 2 * u + s
                            dve.wait_ge(relu_done[s], l * 16 + part * 4 + u + 1)
                            dve.wait_ge(h_ready, t)
                            v.tensor_tensor(tmp2[:], tmp1[:], tmp1[:], ALU.mult).then_inc(sq_done, 1)
                            dve.wait_ge(h_hi_ready, t + 1)
                            v.tensor_tensor(hidden[1][:, 2 * u + s, :], tmp2[:],
                                            hidden[0][:, 2 * u + s, :].bitcast(F32), ALU.subtract)\
                                .then_inc(h_ready, 1)
                    dve.wait_ge(ln_stats, RT * (l * (GROUPS - 2) + 2 + 2 * part))
                    wait_apart(dve, ln_rows, RT * (l + 1))
                    with dve.Fori(0, 2) as half:
                        take_group(l * GROUPS + 4 + 2 * part + half,
                                   nth(l, AT_FF) + 8 * part + 4 + 2 * half + 2, half_rows(half),
                                   ALPHA if part == 0 else 1.0, half)
                norm(l, 1)


def stream(w_in, w_a, w_b, w_o, w_up, w_down):
    import numpy as np

    def feature_tiles(w, tiles):
        t = w.reshape(KT, P, -1, P).transpose(2, 1, 0, 3).reshape(-1, P, D)
        return [t[f] for f in tiles]

    def row_form(w):
        t = w.reshape(KT // 2, 2, P, 2, BANK).transpose(3, 0, 2, 1, 4).reshape(-1, P, D)
        return list(t)

    out = []
    for l in range(DEPTH):
        q, k, v = (w_in[l][:, i * D:(i + 1) * D] for i in range(3))
        rest = w_in[l][:, 3 * D:]
        sq, sk, sv = rest[:, 0:D], rest[:, D:D + P], rest[:, D + P:D + 2 * P]
        ga, gb = rest[:, D + 2 * P:2 * D + 2 * P], rest[:, 2 * D + 2 * P:]
        for h in range(HEADS):
            out += feature_tiles(q, [h]) + feature_tiles(k, [h])
            if h == 0:
                out += row_form(v)
        for f in range(KT):
            out += feature_tiles(ga, [f]) + feature_tiles(w_a[l], [f])
        out += feature_tiles(sk, [0]) + feature_tiles(sv, [0]) + feature_tiles(sq, range(PAIRS))
        for f in range(KT):
            out += feature_tiles(gb, [f]) + feature_tiles(w_b[l], [f])
        out += row_form(w_o[l])
        for part in range(FF_PARTS):
            out += feature_tiles(w_up[l], range(part * KT, (part + 1) * KT))
            out += row_form(w_down[l][part * D:(part + 1) * D])
    return np.ascontiguousarray(np.stack(out))


def tables():
    import math

    import numpy as np

    half = DH // 2
    inv = (np.float32(10000.0) ** (-np.arange(half, dtype=np.float32) / np.float32(half))).astype(np.float32)
    pos = np.concatenate([np.arange(SEQ), np.tile(PAST + np.arange(DEC_T), DEC_B)]).astype(np.float32)
    ang = (inv[:, None] * pos[None, :]).astype(np.float32)
    cos = np.tile(np.cos(ang), (4, 1)).astype(np.float32)
    sin = np.sin(ang).astype(np.float32)
    sin = np.tile(np.concatenate([-sin, sin]), (2, 1)).astype(np.float32)
    row = np.arange(P)
    m = np.zeros((DEC_B, MASK_COLS), np.float32)
    m[0, 0:CHUNK] = 1.0
    m[0, P:2 * P] = 1.0
    for g in range(2):
        for b in range(DEC_B):
            m[b, 2 * P + g * P:2 * P + (g + 1) * P] = 4 * g + (row % 64) // DEC_T != b
    at = 4 * P
    m[0, at:at + 64] = NEG
    at += 64
    for b in range(DEC_B):
        m[b, at + b * DEC_T:at + (b + 1) * DEC_T] = NEG
    at += P
    for g in range(2):
        for b in range(4):
            m[4 * g + b, at + 256 * g + 64 * b:at + 256 * g + 64 * (b + 1)] = NEG
    lam_init = [0.8 - 0.6 * math.exp(-0.3 * l) for l in range(DEPTH)]
    return (cos, sin, np.eye(P, dtype=np.float32), np.full((P, P), 1.0 / P, np.float32),
            m, lam_init)


def kernel(x_prompt, x_sample, cache_diff_k, cache_diff_v, cache_swa_k, cache_swa_v, w_in,
           diff_lambda_q1, diff_lambda_k1, diff_lambda_q2, diff_lambda_k2, diff_subln_g, swa_sinks,
           w_branch_a, w_branch_b, w_o, ln1_g, ln1_b, w_up, w_down, ln2_g, ln2_b):
    import numpy as np
    import concourse.bacc as bacc
    from concourse.bass_utils import run_bass_kernel_spmd

    c = np.ascontiguousarray
    x = np.concatenate([x_prompt.reshape(SEQ, D), x_sample.reshape(DEC_B * DEC_T, D)])
    k = cache_diff_k.transpose(0, 3, 4, 5, 1, 2).reshape(DEPTH, HEADS, P, DEC_B * PAST)
    v = cache_diff_v.reshape(DEPTH, DEC_B, 4, P, HEADS, P).transpose(0, 4, 3, 2, 1, 5)
    sk = cache_swa_k[:, :, CHUNK:].transpose(0, 4, 3, 1, 2).reshape(DEPTH, DH, 2 * DEC_B * 64)
    sk = np.concatenate([sk, sk], axis=1)
    sv = cache_swa_v[:, :, CHUNK:].reshape(DEPTH, 4, P, P).transpose(0, 2, 1, 3)
    cos, sin, ident, ones, masks, lam_init = tables()
    cols = np.zeros((P, C_END), np.float32)
    for l in range(DEPTH):
        cols[:, C_LAM_INIT + l] = lam_init[l]
        cols[:, C_ONE_MINUS + l] = 1.0 - lam_init[l]
        cols[:, C_SUBLN + l] = diff_subln_g[l]
        for j in range(PAIRS):
            cols[0:64, C_SINK + l * PAIRS + j] = swa_sinks[l, 2 * j]
            cols[64:128, C_SINK + l * PAIRS + j] = swa_sinks[l, 2 * j + 1]
    cols[:, C_EPS] = EPS
    lam = np.stack([diff_lambda_q1, diff_lambda_k1, diff_lambda_q2, diff_lambda_k2], axis=1)
    lam = np.broadcast_to(lam.reshape(1, -1), (P, DEPTH * 4 * DH))
    ln = np.stack([ln1_g, ln1_b, ln2_g, ln2_b], axis=1).reshape(DEPTH, 2, 2, 1, D)
    ln = np.broadcast_to(ln, (DEPTH, 2, 2, P, D))
    keep = CHUNK * 2 - DEC_T
    arrays = {
        "x_rows": x,
        "k_cache": k, "v_cache": v.reshape(DEPTH, HEADS, P, 4 * D),
        "swa_kc": sk, "swa_vc": sv.reshape(DEPTH, P, 4 * P),
        "swa_k_keep": cache_swa_k[:, :, DEC_T:].reshape(DEPTH * DEC_B, keep * P),
        "swa_v_keep": cache_swa_v[:, :, DEC_T:].reshape(DEPTH * DEC_B, keep * P),
        "weights": stream(w_in, w_branch_a, w_branch_b, w_o, w_up, w_down),
        "cols": cols, "lam_vec": lam, "ln_par": ln, "cos_t": cos, "sin_t": sin, "ident_d": ident,
        "ones_d": ones, "masks": masks,
    }
    arrays = {"in_" + n: c(a) for n, a in arrays.items()}
    outs = {
        "x_all": [DEPTH + 1, ROWS, D], "k_out": [DEPTH, HEADS, P, ROWS],
        "v_out": [DEPTH, P, RT, D], "swk_out": [DEPTH, P, 2 * P], "swv_out": [DEPTH, P, 2 * P],
        "swk_keep_out": [DEPTH * DEC_B, keep * P], "swv_keep_out": [DEPTH * DEC_B, keep * P],
    }
    nc = bacc.Bacc("TRN2", target_bir_lowering=False, num_devices=1)
    args = [nc.dram_tensor(n, a.shape, mybir.dt.from_np(a.dtype), kind="ExternalInput").ap()
            for n, a in arrays.items()]
    args += [nc.dram_tensor(n, s, F32, kind="ExternalOutput").ap() for n, s in outs.items()]
    build(nc, *args)
    got = run_bass_kernel_spmd(nc, [arrays], core_ids=[0]).results[0]

    y = got["x_all"][DEPTH]
    ko, vo = got["k_out"], got["v_out"].transpose(0, 2, 1, 3).reshape(DEPTH, ROWS, HEADS, P)
    ko = ko.reshape(DEPTH, HEADS, 2, DH, ROWS).transpose(0, 4, 1, 2, 3)

    def window(new, kept):
        new = new.transpose(0, 2, 1).reshape(DEPTH, 2 * P, 2, DH)
        kept = kept.reshape(DEPTH, DEC_B, keep, 2, DH)
        fresh = new[:, P:].reshape(DEPTH, DEC_B, DEC_T, 2, DH)
        return c(new[:, None, 0:P]), c(np.concatenate([kept, fresh], axis=2))

    skp, sks = window(got["swk_out"], got["swk_keep_out"])
    svp, svs = window(got["swv_out"], got["swv_keep_out"])
    return (c(y[:SEQ].reshape(1, SEQ, D)), c(y[SEQ:].reshape(DEC_B, DEC_T, D)),
            c(ko[:, None, :SEQ]), c(vo[:, None, :SEQ]), skp, svp,
            c(ko[:, SEQ:].reshape(DEPTH, DEC_B, DEC_T, HEADS, 2, DH)),
            c(vo[:, SEQ:].reshape(DEPTH, DEC_B, DEC_T, HEADS, P)), sks, svs)
```

```python
from contextlib import ExitStack

import concourse.bass as bass
from concourse import mybir

F32 = mybir.dt.float32
F32R = mybir.dt.float32r
BF16 = mybir.dt.bfloat16
ALU = mybir.AluOpType
ACT = mybir.ActivationFunctionType
AX_X = mybir.AxisListType.X

P = 128
D = 1024
KT = D // P
SEQ = 512
DEC_B = 8
DEC_T = 16
ROWS = SEQ + DEC_B * DEC_T
RT = ROWS // P
DEPTH = 2
CHUNK = 64
PAST = 512
HEADS = 8
DH = 64
PAIRS = 8
HALF = ROWS // 2
BANK = 512
FF_PARTS = 4
ALPHA = (2 * DEPTH) ** 0.25
EPS = 1e-5
QK_SCALE = DH ** -0.5
NEG = -1e30

V_CHUNKS, HEAD_CHUNKS, BRANCH_CHUNKS, O_CHUNKS = 8, 2 * HEADS, 2 * KT, 8
SWA_CHUNKS = 2 + PAIRS
FF_CHUNKS = FF_PARTS * 16
AT_HEAD_0 = 0
AT_V = AT_HEAD_0 + 2
AT_HEADS = AT_V + V_CHUNKS - 2
AT_BRANCH_A = AT_HEADS + HEAD_CHUNKS
AT_SWA = AT_BRANCH_A + BRANCH_CHUNKS
AT_BRANCH_B = AT_SWA + SWA_CHUNKS
AT_O = AT_BRANCH_B + BRANCH_CHUNKS
AT_FF = AT_O + O_CHUNKS
CHUNKS = AT_FF + FF_CHUNKS
RAW_SLOTS = 4

ROPES = 2 * HEADS + 1 + PAIRS
GROUPS = 2 + 2 + 2 * FF_PARTS

C_LAM_INIT = 0
C_ONE_MINUS = C_LAM_INIT + DEPTH
C_SUBLN = C_ONE_MINUS + DEPTH
C_ZERO = C_SUBLN + DEPTH
C_EPS = C_ZERO + 1
C_SINK = C_EPS + 1
C_END = C_SINK + DEPTH * PAIRS
MASK_COLS = 4 * P + 64 + P + 512


def build(nc, x_rows, k_cache, v_cache, swa_kc, swa_vc, swa_k_keep, swa_v_keep, weights, cols,
          lam_vec, ln_par, cos_t, sin_t, ident_d, ones_d, masks, x_all, k_out, v_out, swk_out,
          swv_out, swk_keep_out, swv_keep_out):
    ctx = ExitStack()
    with ctx:
        def sem(name):
            return ctx.enter_context(nc.semaphore(name))

        base = -(-nc.sbuf_base // 32) * 32
        total = 212480
        ctx.enter_context(nc.sbuf_tensor("arena", [P, (total + 32) // 4], F32))
        top = [base]

        def region(nbytes):
            at = top[0]
            top[0] += nbytes
            assert top[0] <= base + total
            return [at, at + nbytes]

        def at(where, name, shape, dt):
            t = nc.alloc_sbuf_tensor_at(name, [P, *shape], dt, offset=where[0])
            size = 2 if dt == BF16 else 4
            for n in shape:
                size *= n
            where[0] += -(-size // 32) * 32
            assert where[0] <= where[1], name
            return t

        WIDE = KT * ROWS * 4
        r_xt, r_a, r_b = region(2 * WIDE), region(2 * WIDE), region(2 * WIDE)
        r_rows, r_mix, r_w = region(WIDE), region(WIDE), region(32768)
        r_keep = region(base + total - top[0])

        xt_hi = at(r_xt, "xt_hi", [KT, ROWS], F32R)
        xt_lo = at(r_xt, "xt_lo", [KT, ROWS], F32R)
        rows = at(list(r_rows), "rows", [RT, D], F32)
        mix_a = at(list(r_mix), "mix_a", [KT, ROWS], F32)
        raw = at(r_w, "w_raw", [RAW_SLOTS, D], F32)
        w_hi = [at(r_w, f"w_hi{s}", [D], F32R) for s in range(2)]
        w_lo = [at(r_w, f"w_lo{s}", [D], F32R) for s in range(2)]
        cos = at(r_keep, "cos", [ROWS], F32)
        sin = at(r_keep, "sin", [ROWS], F32)
        rope_c = at(r_keep, "rope_c", [ROWS], F32)
        rope_s = at(r_keep, "rope_s", [ROWS], F32)
        ident = at(r_keep, "ident", [P], F32)
        ones = at(r_keep, "ones", [P], F32)
        mask_cols = at(r_keep, "mask_cols", [MASK_COLS], BF16)
        m_first, m_all = mask_cols[:, 0:P], mask_cols[:, P:2 * P]
        m_own = mask_cols[:, 2 * P:4 * P].rearrange("p (g n) -> p g n", g=2)
        m_neg64 = mask_cols[:, 4 * P:4 * P + 64]
        m_negnew = mask_cols[:, 4 * P + 64:5 * P + 64]
        m_negold = mask_cols[:, 5 * P + 64:MASK_COLS].rearrange("p (g n) -> p g n", g=2)
        col = at(r_keep, "col", [C_END], F32)
        neg_lam = at(r_keep, "neg_lam", [DEPTH], F32)
        g_sub = at(r_keep, "g_sub", [DEPTH], F32)
        small = at(r_keep, "small", [64], F32)
        tmp1, tmp2 = rope_c, rope_s

        ra = list(r_a)
        a_t = at(ra, "a_t", [KT, ROWS], F32)
        z_map = [[at(ra, f"z_map{p}{m}", [SEQ], F32) for m in range(2)] for p in range(2)]
        k_t = [at(ra, f"k_t{p}", [ROWS], F32) for p in range(2)]
        z_dec = at(ra, "z_dec", [DEC_B * P + 64 * 2], F32)
        d_a = at(list(ra), "d_a", [ROWS], F32)
        o_n = at(ra, "o_n", [4, P], F32)
        d_on = at(ra, "d_on", [P], F32)
        ra = list(r_a)
        sk_t = at(ra, "sk_t", [ROWS], F32)
        sk_dup = at(ra, "sk_dup", [2, ROWS], F32)
        sv_t = at(ra, "sv_t", [ROWS], F32)
        sv_rows = at(ra, "sv_rows", [8, P], F32)
        zq = [at(ra, f"zq{p}", [8, 2, 64], F32) for p in range(2)]
        zs = [at(ra, f"zs{p}", [2, P], F32) for p in range(2)]
        ra = list(r_a)
        act_a = [at(ra, "act_a_hi", [KT, ROWS], F32R), at(ra, "act_a_lo", [KT, ROWS], F32R)]
        rb = list(r_b)
        kc = at(rb, "kc", [DEC_B, PAST], F32)
        vc = at(rb, "vc", [4, D], F32)
        d_o = at(rb, "d_o", [DEC_B, P], F32)
        d_at = at(rb, "d_at", [5, P], F32)
        v_new = at(rb, "v_new", [P], F32)
        d_out = at(rb, "d_out", [P], F32)
        d_rs = at(rb, "d_rs", [P], F32)
        rb = list(r_b)
        act_b = [at(rb, "act_b_hi", [KT, ROWS], F32R), at(rb, "act_b_lo", [KT, ROWS], F32R)]
        rm = list(r_mix)
        u_p = [at(rm, f"u_p{p}", [2, BANK], F32) for p in range(2)]
        u_a = [at(rm, f"u_a{p}", [BANK], F32) for p in range(2)]
        u_at = [at(rm, f"u_at{p}", [BANK], F32) for p in range(2)]
        d_t = at(list(rm), "d_t", [ROWS], F32)
        o_sq = at(list(rm), "o_sq", [4, P], F32)
        rm[0] += ROWS * 4
        z_all = at(rm, "z_all", [2, P], F32)
        d_sq = at(rm, "d_sq", [P], F32)
        d_p = at(list(r_mix), "d_p", [2, ROWS], F32)
        rm = list(r_mix)
        ln_g = at(rm, "ln_g", [D], F32)
        ln_b = at(rm, "ln_b", [D], F32)
        rr = list(r_rows)
        s_p = at(rr, "s_p", [8 * P + 2 * 384], F32)
        s_pt = at(rr, "s_pt", [14, P], F32)
        s_kc = at(rr, "s_kc", [2, DEC_B, 64], F32)
        s_vc = at(rr, "s_vc", [4, P], F32)
        rm = list(r_mix)
        lam_v = at(rm, "lam_v", [DEPTH, 4, DH], F32)
        mask_f = at(rm, "mask_f", [MASK_COLS], F32)
        ln_st = at(r_keep, "ln_st", [RT, 2, 6], F32)
        ln_mv = at(r_keep, "ln_mv", [RT, 4], F32)
        d_nm, d_l, d_r = small[:, 0:2], small[:, 2:4], small[:, 4:6]
        u_nm = [small[:, 6:8], small[:, 8:10]]
        u_l = [small[:, 10:12], small[:, 12:14]]
        u_r = small[:, 14:16]
        o_ms, o_rs = small[:, 16:20], small[:, 20:24]
        s_nm, s_l, s_e = small[:, 24:34], small[:, 34:44], small[:, 44:54]
        lam2 = small[:, 54:58]

        PS = ctx.enter_context(nc.psum_tensor("PS", [P, 8, BANK], F32))
        flat = PS[:].rearrange("p b n -> p (b n)")

        def pair(which):
            return PS[:, 4 + 2 * which:6 + 2 * which, 0:HALF]

        def bank_of(which, half):
            return 4 + 2 * which + half

        def halves(t):
            return t.rearrange("p (a n) -> p a n", a=2)

        raw_loaded = [sem(f"raw_loaded{j}") for j in range(RAW_SLOTS)]
        w_hi_made = sem("w_hi_made")
        w_ready = [sem(f"w_ready{s}") for s in range(2)]
        chunk_done = [sem(f"chunk_done{s}") for s in range(2)]
        chunk_half_done = [sem(f"chunk_half_done{s}") for s in range(2)]
        consts_loaded, ident_loaded, small_loaded = sem("consts_loaded"), sem("ident_loaded"), sem("small_loaded")
        x0_loaded = [sem(f"x0_loaded{r}") for r in range(RT)]
        lam_sum, lam_exp, lam_link = sem("lam_sum"), sem("lam_exp"), sem("lam_link")
        masks_ready = sem("masks_ready")
        x_hi_ready, x_lo_ready = sem("x_hi_ready"), sem("x_lo_ready")
        row_acc_ready = sem("row_acc_ready")
        row_evacuated = [sem(f"row_evacuated{r}") for r in range(RT)]
        v_stored = sem("v_stored")
        z_zeroed = sem("z_zeroed")
        rope_swapped, rope_cos_done = sem("rope_swapped"), sem("rope_cos_done")
        rope_sin_done, rope_added = sem("rope_sin_done"), sem("rope_added")
        pair_q_added = sem("pair_q_added")
        k_stored = [sem(f"k_stored{p}") for p in range(2)]
        kc_loaded, vc_loaded = sem("kc_loaded"), sem("vc_loaded")
        dec_scores, dec_max, dec_exp = sem("dec_scores"), sem("dec_max"), sem("dec_exp")
        dec_recip, dec_r_ready = sem("dec_recip"), sem("dec_r_ready")
        dec_shifted, dec_probs = sem("dec_shifted"), sem("dec_probs")
        dec_t_ready, dec_t_copied = sem("dec_t_ready"), sem("dec_t_copied")
        dec_pv, v_new_copied = sem("dec_pv"), sem("v_new_copied")
        dec_new_ready, dec_new_copied = sem("dec_new_ready"), sem("dec_new_copied")
        dec_o_copied, dec_ot_ready, dec_summed = sem("dec_o_copied"), sem("dec_ot_ready"), sem("dec_summed")
        dec_sq_ready, dec_ms_ready = sem("dec_sq_ready"), sem("dec_ms_ready")
        dec_ln_done, dec_rs_ready, dec_done = sem("dec_ln_done"), sem("dec_rs_ready"), sem("dec_done")
        unit_scores, unit_max, unit_exp = sem("unit_scores"), sem("unit_max"), sem("unit_exp")
        unit_recip, unit_r_ready = sem("unit_recip"), sem("unit_r_ready")
        unit_second, unit_probs = sem("unit_second"), sem("unit_probs")
        unit_t_ready, unit_t_copied, unit_pv = sem("unit_t_ready"), sem("unit_t_copied"), sem("unit_pv")
        o_sq_ready, o_ms_ready, o_ln_done = sem("o_sq_ready"), sem("o_ms_ready"), sem("o_ln_done")
        o_rs_ready, o_n_ready, o_t_ready = sem("o_rs_ready"), sem("o_n_ready"), sem("o_t_ready")
        a_done, a_hi_ready, a_lo_ready = sem("a_done"), sem("a_hi_ready"), sem("a_lo_ready")
        gate_ready, branch_taken = sem("gate_ready"), sem("branch_taken")
        mix_sum, mix_hi_ready, mix_ready = sem("mix_sum"), sem("mix_hi_ready"), sem("mix_ready")
        swa_cache_loaded, swa_k_dup = sem("swa_cache_loaded"), sem("swa_k_dup")
        swa_v_copied, swa_vt_ready, swa_v_ready = sem("swa_v_copied"), sem("swa_vt_ready"), sem("swa_v_ready")
        swa_stored, swa_zeroed = sem("swa_stored"), sem("swa_zeroed")
        swa_scores, swa_row_max, swa_max = sem("swa_scores"), sem("swa_row_max"), sem("swa_max")
        swa_exp, swa_sink_exp = sem("swa_exp"), sem("swa_sink_exp")
        swa_pt_ready, swa_pt_copied, swa_pv = sem("swa_pt_ready"), sem("swa_pt_copied"), sem("swa_pv")
        swa_sum, swa_recip, swa_scaled = sem("swa_sum"), sem("swa_recip"), sem("swa_scaled")
        b_hi_ready, b_lo_ready = sem("b_hi_ready"), sem("b_lo_ready")
        b_samples_hi_ready, b_samples_lo_ready = sem("b_samples_hi_ready"), sem("b_samples_lo_ready")
        x_rows_loaded, ln_par_loaded = sem("x_rows_loaded"), sem("ln_par_loaded")
        ln_stats, ln_aggr, ln_log, ln_rstd = sem("ln_stats"), sem("ln_aggr"), sem("ln_log"), sem("ln_rstd")
        ln_centred, ln_rows, ln_t_ready = sem("ln_centred"), sem("ln_rows"), sem("ln_t_ready")
        input_rows = sem("input_rows")
        relu_done = [sem(f"relu_done{s}") for s in range(2)]
        sq_done, h_hi_ready, h_ready = sem("sq_done"), sem("h_hi_ready"), sem("h_ready")
        y_stored, keep_stored = sem("y_stored"), sem("keep_stored")
        waits_passed = sem("waits_passed")
        CONST_LOADS = 3
        SMALL_LOADS = 3

        block = ctx.enter_context(nc.Block())

        def nth(l, at_chunk, i=0):
            return l * (CHUNKS // 2) + (at_chunk // 2 + i)

        def tiles_before(l, which):
            return l * (2 * RT) + which * RT

        T_BANKS = (0, 2, 6, 0, 2)

        def transposed_tile(r):
            return flat[:, T_BANKS[r] * BANK:T_BANKS[r] * BANK + D].rearrange("p (k n) -> p k n", k=KT)

        OUT_AT = 6 * BANK
        S_OUT_AT = 2 * BANK

        def window_outputs(dst, j, samples):
            c, first, units = (slice(SEQ, ROWS), S_OUT_AT, 2) if samples else (slice(0, SEQ), OUT_AT, 8)
            psum = flat[0:DH, first:first + units * P].rearrange("p (u g q) -> p u g q", u=units, g=2)
            return [(dst[g * DH:(g + 1) * DH, j, c].rearrange("p (u q) -> p u q", u=units),
                     psum[:, :, g, :]) for g in range(2)]

        def all_heads(eng, l, head):
            with eng.Fori(0, HEADS // 2 - 1) as i:
                for p in range(2):
                    head(l, 2 * i + p, p, True)
            head(l, HEADS - 2, 0, True)
            head(l, HEADS - 1, 1, False)

        def all_pairs(eng, l, pair):
            with eng.Fori(0, PAIRS // 4) as i:
                for p in range(2):
                    pair(l, 0, i, p, True)
            for i in range(PAIRS // 4, PAIRS // 2):
                for p in range(2):
                    pair(l, 1, i, p, 2 * i + p < PAIRS - 1)

        def wait_apart(eng, semaphore, value):
            eng.wait_ge(semaphore, value)
            eng.sem_inc(waits_passed, 1)

        @block.sync
        def _(sp):
            def load(g, j):
                sp.dma_start(raw[:, j, :], weights[g * RAW_SLOTS + j]).then_inc(raw_loaded[j], 16)

            sp.dma_start(ident[:], ident_d).then_inc(ident_loaded, 16)
            for dst, src in ((col[:], cols), (lam_v[:].rearrange("p a b c -> p (a b c)"), lam_vec),
                             (mask_f[0:DEC_B, :], masks)):
                sp.dma_start(dst, src).then_inc(small_loaded, 16)
            for r in range(RT):
                sp.dma_start(rows[:, r, :], x_rows[r * P:(r + 1) * P, :]).then_inc(x0_loaded[r], 16)
                if r < 2:
                    load(0, r)
            loads = [(cos[:], cos_t), (sin[:], sin_t), (ones[:], ones_d)]
            assert len(loads) == CONST_LOADS
            for dst, src in loads:
                sp.dma_start(dst, src).then_inc(consts_loaded, 16)

            for j in range(2, RAW_SLOTS):
                load(0, j)
            sp.dma_start(swk_keep_out, swa_k_keep).then_inc(keep_stored, 16)
            sp.dma_start(swv_keep_out, swa_v_keep).then_inc(keep_stored, 16)
            with sp.Fori(1, DEPTH * CHUNKS // RAW_SLOTS) as g:
                for j in range(RAW_SLOTS):
                    sp.wait_ge(w_ready[j % 2], 2 * g + (j // 2 - 1))
                    load(g, j)
            sp.wait_ge(keep_stored, 32)

        @block.gpsimd
        def _(pool):
            pool.wait_ge(small_loaded, 16 * SMALL_LOADS)
            with pool.Fori(0, DEPTH * CHUNKS // RAW_SLOTS) as g:
                for j in range(RAW_SLOTS):
                    s = j % 2
                    pool.wait_ge(raw_loaded[j], 16 * (g + 1))
                    pool.wait_ge(chunk_done[s], 2 * g + j // 2)
                    nc.gpsimd.tensor_tensor(w_hi[s][:], raw[:, j, :],
                                            col[:, C_ZERO:C_ZERO + 1].to_broadcast([P, D]),
                                            ALU.add).then_inc(w_hi_made, 1)
                    pool.wait_ge(w_hi_made, 4 * g + (j + 1))
                    nc.gpsimd.tensor_tensor(w_lo[s][:], raw[:, j, :], w_hi[s][:].bitcast(F32),
                                            ALU.subtract).then_inc(w_ready[s], 1)

        @block.tensor
        def _(pe):
            mm = nc.tensor.matmul

            def feature_tile(s, n, hi, lo, which, part=None, between=None):
                for half in (0, 1) if part is None else (part,):
                    if half == 0:
                        pe.wait_ge(w_ready[s], n + 1)
                    out = PS[:, bank_of(which, half), 0:HALF]
                    c = slice(half * HALF, (half + 1) * HALF)
                    for k in range(KT):
                        if between and (half, k) in between:
                            between[half, k]()
                        wh, wl = w_hi[s][:, k * P:(k + 1) * P], w_lo[s][:, k * P:(k + 1) * P]
                        mm(out, wh, hi[:, k, c], start=(k == 0), stop=False)
                        mm(out, wh, lo[:, k, c], start=False, stop=False)
                        last = mm(out, wl, hi[:, k, c], start=False, stop=(k == KT - 1))
                    last.then_inc((chunk_half_done if half == 0 else chunk_done)[s], 1)

            def row_group(n, group, hi, lo, before_k=None, early=False, before_bank_4=None):
                steps = [(k, r) for k in range(KT // 2 if early else KT) for r in range(RT)]
                if early:
                    for tiles, ks in ((range(3), (4, 5)), (range(3), (6, 7)), (range(3, RT), (4, 5, 6, 7))):
                        steps += [(k, r) for r in tiles for k in ks]
                for k, r in steps:
                    s, k2 = (k // 2) % 2, k % 2
                    if r == 0:
                        if k2 == 0:
                            pe.wait_ge(w_ready[s], n + (k // 4 + 1))
                        if before_k:
                            before_k(k)
                    wh = w_hi[s][:, k2 * BANK:(k2 + 1) * BANK]
                    wl = w_lo[s][:, k2 * BANK:(k2 + 1) * BANK]
                    if k == 0:
                        pe.wait_ge(row_evacuated[r], group)
                        if r == RT - 1 and before_bank_4:
                            before_bank_4()
                    xh, xl = hi[:, k, r * P:(r + 1) * P], lo[:, k, r * P:(r + 1) * P]
                    mm(PS[:, r, :], xh, wh, start=(k == 0), stop=False)
                    mm(PS[:, r, :], xh, wl, start=False, stop=False)
                    last = mm(PS[:, r, :], xl, wh, start=False, stop=(k == KT - 1))
                    if r == RT - 1:
                        last.then_inc((chunk_half_done if k2 == 0 else chunk_done)[s], 1)
                    elif k == KT - 1:
                        last.then_inc(row_acc_ready, 1)

            def rope_pair_free(u):
                pe.wait_ge(rope_swapped, 2 * u)
                pe.wait_ge(rope_cos_done, 2 * u)

            def head_tile(l, h, is_k):
                rope_pair_free(l * ROPES + 2 * h + is_k)
                feature_tile(is_k, nth(l, AT_HEADS) + h, xt_hi, xt_lo, 0)

            def dec_scores_of(l, h, p):
                n = l * HEADS + h
                pe.wait_ge(rope_added, l * ROPES + 2 * h + 2)
                pe.wait_ge(kc_loaded, 16 * (n + 1))
                pe.wait_ge(unit_exp, 4 * n)
                pe.wait_ge(dec_summed, n)
                for g in range(2):
                    old, new = PS[:, 2 * g, :], PS[:, 2 * g + 1, 0:P]
                    for b in range(4):
                        zb = z_dec[:, (4 * g + b) * P:(4 * g + b + 1) * P]
                        mm(old, zb, kc[:, 4 * g + b, :], start=(b == 0), stop=(b == 3))
                    if g == 1:
                        pe.wait_ge(dec_ln_done, n)
                    mm(new, z_all[:, g, :], k_t[p][:, SEQ:ROWS], start=True, stop=False)
                    mm(new, m_own[:, g, :], m_negnew, start=False, stop=True).then_inc(dec_scores, 1)

            def output_transposes(l, h):
                n = l * HEADS + h
                pe.wait_ge(o_n_ready, n + 1)
                pe.wait_ge(unit_t_copied, 4 * n + 4)
                for i in range(4):
                    last = nc.tensor.transpose(PS[:, 6, i * P:(i + 1) * P], o_n[:, i, :], ident[:])
                last.then_inc(o_t_ready, 1)

            def dec_transposes(l, h):
                n = l * HEADS + h
                pe.wait_ge(dec_probs, 2 * n + 2)
                pe.wait_ge(a_done, n)
                pe.wait_ge(o_n_ready, n)
                for t in range(4):
                    last = nc.tensor.transpose(PS[:, 6, t * P:(t + 1) * P], d_a[:, t * P:(t + 1) * P],
                                               ident[:])
                last.then_inc(dec_t_ready, 1)
                nc.tensor.transpose(PS[:, 7, 0:P], d_a[:, SEQ:ROWS], ident[:]).then_inc(dec_t_ready, 1)

            def dec_new_product(l, h):
                n = l * HEADS + h
                pe.wait_ge(dec_t_copied, 2 * n + 2)
                pe.wait_ge(v_new_copied, n + 1)
                mm(PS[:, 7, 2 * P:3 * P], v_new[:], d_at[:, 4, :], start=True, stop=True)\
                    .then_inc(dec_new_ready, 1)

            def dec_product(l, h):
                n = l * HEADS + h
                pe.wait_ge(vc_loaded, 16 * (n + 1))
                pe.wait_ge(unit_exp, 4 * n + 3)
                for half in range(2):
                    for t in range(4):
                        last = mm(PS[:, half, :], d_at[:, t, :], vc[:, t, half * BANK:(half + 1) * BANK],
                                  start=(t == 0), stop=(t == 3))
                    last.then_inc(dec_pv, 1)

            def dec_product_transposes(l, h):
                n = l * HEADS + h
                pe.wait_ge(dec_o_copied, 2 * n + 2)
                for b in range(DEC_B):
                    last = nc.tensor.transpose(flat[:, b * P:(b + 1) * P], d_o[:, b, :], ident[:])
                last.then_inc(dec_ot_ready, 1)

            def unit_score(l, h, p, i):
                n, w = l * HEADS + h, (i + 1) * P
                if i >= 2:
                    pe.wait_ge(unit_exp, 4 * n + (i - 1))
                for m in range(2):
                    out = PS[:, 2 * (i % 2) + m, :]
                    mm(out[:, 0:w], z_map[p][m][:, i * P:(i + 1) * P], k_t[p][:, 0:w],
                       start=True, stop=False)
                    last = mm(out[:, w - CHUNK:w], m_first, m_neg64, start=False, stop=True)
                last.then_inc(unit_scores, 1)

            def unit_transpose(l, h, i):
                n = 4 * (l * HEADS + h) + i
                pe.wait_ge(unit_probs, n + 1)
                pe.wait_ge(unit_t_copied, n)
                for j in range(i + 1):
                    last = nc.tensor.transpose(PS[:, 6, j * P:(j + 1) * P],
                                               u_a[i % 2][:, j * P:(j + 1) * P], ident[:])
                last.then_inc(unit_t_ready, 1)

            def unit_product(l, h, i):
                n = 4 * (l * HEADS + h) + i
                pe.wait_ge(unit_t_copied, n + 1)
                if i == 0:
                    pe.wait_ge(dec_new_copied, l * HEADS + h + 1)
                for j in range(i + 1):
                    last = mm(PS[:, 7, i * P:(i + 1) * P], u_at[i % 2][:, j * P:(j + 1) * P],
                              rows[:, j, bass.ts(h, P)], start=(j == 0), stop=(j == i))
                last.then_inc(unit_pv, 1)

            def head(l, h, p, more):
                n = l * HEADS + h
                if more:
                    head_tile(l, h + 1, 0)
                else:
                    rope_pair_free(l * ROPES + 2 * HEADS)
                    feature_tile(0, nth(l, AT_BRANCH_A), xt_hi, xt_lo, 0, 0)
                dec_transposes(l, h)
                unit_score(l, h, p, 0)
                unit_score(l, h, p, 1)
                if more:
                    head_tile(l, h + 1, 1)
                dec_new_product(l, h)
                for i in range(2):
                    unit_transpose(l, h, i)
                    unit_score(l, h, p, i + 2)
                    unit_product(l, h, i)
                dec_product(l, h)
                unit_transpose(l, h, 2)
                dec_product_transposes(l, h)
                unit_product(l, h, 2)
                unit_transpose(l, h, 3)
                pe.wait_ge(dec_sq_ready, n + 1)
                mm(PS[:, 3, 0:P], ones[:], d_sq[:], start=True, stop=True).then_inc(dec_ms_ready, 1)
                unit_product(l, h, 3)
                if more:
                    dec_scores_of(l, h + 1, 1 - p)
                else:
                    feature_tile(0, nth(l, AT_BRANCH_A), xt_hi, xt_lo, 0, 1)
                output_transposes(l, h)

            def pair_scores(l, kv, j, p):
                n = l * PAIRS + j
                pe.wait_ge(pair_q_added, n + 1)
                pe.wait_ge(swa_exp, 2 * n)
                for c in range(SEQ // CHUNK):
                    ws = max(0, c - 1) * CHUNK
                    out = PS[:, c // 4, (c % 4) * P:(c % 4 + 1) * P]
                    zc = zq[p][:, c].rearrange("p g q -> p (g q)")
                    last = mm(out, zc, sk_dup[:, kv, ws:ws + P], start=True, stop=(c > 0))
                    if c == 0:
                        mm(out[:, CHUNK:P], m_all, m_neg64, start=False, stop=True)
                last.then_inc(swa_scores, 1)
                pe.wait_ge(rope_added, l * ROPES + (2 * HEADS + 2) + j)
                pe.wait_ge(b_samples_lo_ready, n)
                for g in range(2):
                    old, new = PS[:, 2 + g, 0:256], PS[:, 2 + g, 256:384]
                    keys = s_kc[:, kv, 4 * g:4 * g + 4, :].rearrange("p b k -> p (b k)")
                    mm(old, zs[p][:, g, :], keys, start=True, stop=False)
                    mm(old, m_own[:, g, :], m_negold[:, g, :], start=False, stop=True)
                    mm(new, zs[p][:, g, :], sk_dup[:, kv, SEQ:ROWS], start=True, stop=False)
                    last = mm(new, m_own[:, g, :], m_negnew, start=False, stop=True)
                last.then_inc(swa_scores, 1)

            def probs_transposes(n, q):
                pe.wait_ge(swa_scaled, 2 * n + q // 2 + 1)
                if q >= 2:
                    pe.wait_ge(swa_pt_copied, 4 * n + (q - 1))
                else:
                    pe.wait_ge(b_lo_ready, n)
                for t in range(4 * q, min(4 * q + 4, 14)):
                    last = nc.tensor.transpose(PS[:, 6 + q % 2, (t % 4) * P:(t % 4 + 1) * P],
                                               s_p[:, t * P:(t + 1) * P], ident[:])
                last.then_inc(swa_pt_ready, 1)

            def pair_output(l, kv, j):
                n = l * PAIRS + j
                pe.wait_ge(swa_pt_copied, 4 * n + 4)
                d = slice(kv * DH, (kv + 1) * DH)
                for g in range(2):
                    out = flat[0:DH, S_OUT_AT + g * P:S_OUT_AT + (g + 1) * P]
                    mm(out, s_vc[:, 2 * g, d], s_pt[:, 8 + 3 * g, :], start=True, stop=False)
                    mm(out, s_vc[:, 2 * g + 1, d], s_pt[:, 9 + 3 * g, :], start=False, stop=False)
                    last = mm(out, sv_rows[:, 7, d], s_pt[:, 10 + 3 * g, :], start=False, stop=True)
                last.then_inc(swa_pv, 1)
                for c in range(SEQ // CHUNK):
                    window = 0 if c == 0 else c // 2 if c % 2 else 4 + c // 2 - 1
                    last = mm(flat[0:DH, OUT_AT + c * P:OUT_AT + (c + 1) * P], sv_rows[:, window, d],
                              s_pt[:, c, :], start=True, stop=True)
                last.then_inc(swa_pv, 1)

            def pair_tile(l, i, s, between=None):
                rope_pair_free(l * ROPES + (2 * HEADS + 1) + 2 * i + s)
                feature_tile(s, nth(l, AT_SWA, 1) + i, xt_hi, xt_lo, 0, between=between)

            def window_pair(l, kv, i, p, more):
                j = 2 * i + p
                n = l * PAIRS + j

                def rounds(*qs):
                    return lambda: [probs_transposes(n, q) for q in qs]

                pair_scores(l, kv, j, p)
                fill = {(1, 3): rounds(0, 1), (1, 6): rounds(2, 3)}
                if more:
                    pair_tile(l, i + p, 1 - p, fill)
                else:
                    rope_pair_free(l * ROPES + ROPES)
                    feature_tile(0, nth(l, AT_BRANCH_B), xt_hi, xt_lo, 0, between=fill)
                pair_output(l, kv, j)

            def x_transposes(l, which, r):
                if which == 0:
                    pe.wait_ge(input_rows, l * RT + r + 1)
                else:
                    pe.wait_ge(ln_rows, l * RT + r + 1)
                if r >= 3:
                    pe.wait_ge(x_lo_ready, tiles_before(l, which) + r - 2)
                for k in range(KT):
                    at_col = T_BANKS[r] * BANK + k * P
                    last = nc.tensor.transpose(flat[:, at_col:at_col + P], rows[:, r, k * P:(k + 1) * P],
                                               ident[:])
                last.then_inc(ln_t_ready, 1)

            def first_tiles(l, which, n, pairs):
                for r in range(3):
                    x_transposes(l, which, r)
                for half in range(2):
                    pe.wait_ge(x_hi_ready, tiles_before(l, which) + (3, 5)[half])
                    pe.wait_ge(x_lo_ready, tiles_before(l, which) + (3, 5)[half])
                    for s in range(2):
                        feature_tile(s, n, xt_hi, xt_lo, pairs[s], half, between={
                            (0, (6, 4)[s]): lambda: x_transposes(l, which, 3 + s)})

            pe.wait_ge(ident_loaded, 16)
            with pe.Fori(0, DEPTH) as l:
                first_tiles(l, 0, nth(l, AT_HEAD_0), (0, 1))
                with pe.Fori(0, 2) as v:
                    row_group(nth(l, AT_V) + 2 * v, l * GROUPS + v, xt_hi, xt_lo,
                              before_bank_4=lambda: rope_pair_free(l * ROPES + 1))
                for r in range(RT):
                    wait_apart(pe, row_evacuated[r], l * GROUPS + 2)
                pe.wait_ge(consts_loaded, 16 * CONST_LOADS)
                pe.wait_ge(masks_ready, 2)
                dec_scores_of(l, 0, 0)
                all_heads(pe, l, head)
                def product_a(f):
                    def split_k(k):
                        pe.wait_ge(a_hi_ready, l * KT + k + 1)
                        pe.wait_ge(a_lo_ready, l * KT + k + 1)

                    pe.wait_ge(branch_taken, l * 16 + f)
                    feature_tile(1, nth(l, AT_BRANCH_A) + f, act_b[0], act_b[1], 1,
                                 between={(0, k): (lambda k=k: split_k(k)) for k in range(KT)})

                wait_apart(pe, a_done, l * HEADS + HEADS)
                with pe.Fori(0, KT - 1) as f:
                    product_a(f)
                    pe.wait_ge(gate_ready, l * 16 + f + 1)
                    feature_tile(0, nth(l, AT_BRANCH_A, 1) + f, xt_hi, xt_lo, 0)
                product_a(KT - 1)
                pe.wait_ge(gate_ready, l * 16 + 8)
                feature_tile(0, nth(l, AT_SWA), xt_hi, xt_lo, 0)
                pe.wait_ge(branch_taken, l * 16 + 8)
                feature_tile(1, nth(l, AT_SWA), xt_hi, xt_lo, 1)
                rope_pair_free(l * ROPES + 2 * HEADS + 1)
                feature_tile(0, nth(l, AT_SWA, 1), xt_hi, xt_lo, 0)
                pe.wait_ge(swa_v_copied, l + 1)
                for t in range(8):
                    first = t * P if t < 4 else (t - 4) * P + CHUNK if t < 7 else SEQ
                    last = nc.tensor.transpose(flat[:, t * P:(t + 1) * P], sv_t[:, first:first + P],
                                               ident[:])
                last.then_inc(swa_vt_ready, 1)
                pe.wait_ge(swa_v_ready, l + 1)
                pe.wait_ge(swa_k_dup, l + 1)
                wait_apart(pe, swa_cache_loaded, 32 * (l + 1))
                all_pairs(pe, l, window_pair)
                def product_b(f):
                    pe.wait_ge(branch_taken, l * 16 + 8 + f)
                    feature_tile(1, nth(l, AT_BRANCH_B) + f, act_b[0], act_b[1], 1)

                pe.wait_ge(b_hi_ready, l * PAIRS + PAIRS)
                pe.wait_ge(b_lo_ready, l * PAIRS + PAIRS)
                pe.wait_ge(b_samples_hi_ready, l * PAIRS + PAIRS)
                wait_apart(pe, b_samples_lo_ready, l * PAIRS + PAIRS)
                with pe.Fori(0, KT - 1) as f:
                    product_b(f)
                    pe.wait_ge(gate_ready, l * 16 + 8 + f + 1)
                    feature_tile(0, nth(l, AT_BRANCH_B, 1) + f, xt_hi, xt_lo, 0)
                product_b(KT - 1)
                for v in range(2):
                    row_group(nth(l, AT_O) + 2 * v, l * GROUPS + 2 + v, act_a[0], act_a[1],
                              lambda k: pe.wait_ge(mix_ready, l * KT + k + 1), early=(v == 1),
                              before_bank_4=lambda: pe.wait_ge(gate_ready, l * 16 + 16))
                for part in range(FF_PARTS):
                    hidden = act_b if part % 2 == 0 else act_a
                    if part == 0:
                        pe.wait_ge(row_evacuated[RT - 1], l * GROUPS + 4)
                        first_tiles(l, 1, nth(l, AT_FF), (1, 0))
                    with pe.Fori(1 if part == 0 else 0, KT // 2) as u:
                        for s in range(2):
                            pe.wait_ge(relu_done[s], l * 16 + 4 * part + u)
                            if s == 1:
                                pe.wait_ge(row_evacuated[RT - 1], l * GROUPS + 4 + 2 * part)
                            feature_tile(s, nth(l, AT_FF) + 8 * part + u, xt_hi, xt_lo, 1 - s)
                    def down(v, early=False):
                        row_group(nth(l, AT_FF) + 8 * part + 4 + 2 * v, l * GROUPS + 4 + 2 * part + v,
                                  hidden[0], hidden[1],
                                  lambda k: pe.wait_ge(h_ready, l * 32 + 8 * part + k + 1), early,
                                  lambda: pe.wait_ge(relu_done[1], l * 16 + 4 * part + 4))

                    if part < FF_PARTS - 1:
                        with pe.Fori(0, 2) as v:
                            down(v)
                    else:
                        down(0)
                        down(1, early=True)

        @block.scalar
        def _(act):
            fn = nc.scalar.activation

            def swap_half(l, u, s, n, scale, half):
                act.wait_ge((chunk_half_done, chunk_done)[half][s], n + 1)
                act.wait_ge(rope_added, u)
                for a in range(0, P, DH):
                    for dst, src in ((a, a + DH // 2), (a + DH // 2, a)):
                        last = fn(rope_s[dst:dst + 32, half * HALF:(half + 1) * HALF],
                                  PS[src:src + 32, bank_of(0, half), 0:HALF], ACT.Copy, scale=scale)
                last.then_inc(rope_swapped, 1)

            def swap(l, u, s, n, scale, which=0):
                act.wait_ge(chunk_done[s], n + 1)
                act.wait_ge(rope_added, u)
                for a in range(0, P, DH):
                    for dst, src in ((a, a + DH // 2), (a + DH // 2, a)):
                        last = fn(halves(rope_s[dst:dst + 32, :]), pair(which)[src:src + 32], ACT.Copy,
                                  scale=scale)
                last.then_inc(rope_swapped, 2)

            def x_high(l, which, r):
                act.wait_ge(ln_t_ready, tiles_before(l, which) + r + 1)
                fn(xt_hi[:, :, r * P:(r + 1) * P], transposed_tile(r), ACT.Copy).then_inc(x_hi_ready, 1)

            def q_swap(l, h):
                for half in range(2):
                    swap_half(l, l * ROPES + 2 * h, 0, nth(l, AT_HEADS) + h, QK_SCALE, half)

            def k_swap(l, h):
                swap(l, l * ROPES + 2 * h + 1, 1, nth(l, AT_HEADS) + h, 1.0)

            def pair_swap(l, j, i, s, half):
                swap_half(l, l * ROPES + (2 * HEADS + 1) + j, s, nth(l, AT_SWA, 1) + i, QK_SCALE, half)

            def load_cache(kind, l, h):
                if kind == 0:
                    act.dma_start(kc[:].rearrange("p b k -> p (b k)"), k_cache[l, h]).then_inc(kc_loaded, 16)
                else:
                    act.dma_start(vc[:].rearrange("p t n -> p (t n)"), v_cache[l, h]).then_inc(vc_loaded, 16)

            def unit_exps(l, h, i):
                n, w = 4 * (l * HEADS + h) + i, (i + 1) * P
                act.wait_ge(unit_max, n + 1)
                for m in range(2):
                    last = fn(u_p[i % 2][:, m, 0:w], PS[:, 2 * (i % 2) + m, 0:w], ACT.Exp,
                              bias=u_nm[i % 2][:, m:m + 1], accum_out=u_l[i % 2][:, m:m + 1])
                last.then_inc(unit_exp, 1)

            def unit_copy(l, h, i):
                n, w = 4 * (l * HEADS + h) + i, (i + 1) * P
                act.wait_ge(unit_t_ready, n + 1)
                act.wait_ge(unit_pv, 4 * (l * HEADS + h) + max(0, i - 1))
                fn(u_at[i % 2][:, 0:w], PS[:, 6, 0:w], ACT.Copy).then_inc(unit_t_copied, 1)

            def dec_exps(l, h):
                n = l * HEADS + h
                for g in range(2):
                    act.wait_ge(dec_max, 2 * n + g + 1)
                    fn(d_p[:, g, :], flat[:, 1024 * g:1024 * g + ROWS], ACT.Exp,
                       bias=d_nm[:, g:g + 1], accum_out=d_l[:, g:g + 1]).then_inc(dec_exp, 1)

            def head(l, h, p, more):
                n = l * HEADS + h
                act.dma_start(k_out[l, h], k_t[p][:]).then_inc(k_stored[p], 16)
                if more:
                    load_cache(0, l, h + 1)
                act.wait_ge(dec_r_ready, n + 1)
                fn(d_t[0:64], d_p[64:128, 0, :], ACT.Copy, scale=d_r[64:128, 0:1])
                fn(d_t[64:128], d_p[0:64, 1, :], ACT.Copy, scale=d_r[0:64, 1:2]).then_inc(dec_shifted, 1)
                wait_apart(act, dec_new_ready, n)
                fn(v_new[:], rows[:, RT - 1, bass.ts(h, P)], ACT.Copy).then_inc(v_new_copied, 1)
                if more:
                    q_swap(l, h + 1)
                act.wait_ge(dec_t_ready, 2 * n + 1)
                fn(d_at[:, 0:4, :].rearrange("p t n -> p (t n)"), PS[:, 6, :], ACT.Copy)\
                    .then_inc(dec_t_copied, 1)
                act.wait_ge(dec_t_ready, 2 * n + 2)
                fn(d_at[:, 4, :], PS[:, 7, 0:P], ACT.Copy).then_inc(dec_t_copied, 1)
                unit_exps(l, h, 0)
                unit_exps(l, h, 1)
                act.wait_ge(dec_new_ready, n + 1)
                act.wait_ge(dec_summed, n)
                fn(d_on[:], PS[:, 7, 2 * P:3 * P], ACT.Copy).then_inc(dec_new_copied, 1)
                unit_copy(l, h, 0)
                unit_exps(l, h, 2)
                unit_copy(l, h, 1)
                if more:
                    k_swap(l, h + 1)
                unit_exps(l, h, 3)
                for half in range(2):
                    act.wait_ge(dec_pv, 2 * n + half + 1)
                    fn(d_o[:, 4 * half:4 * half + 4, :].rearrange("p b e -> p (b e)"), PS[:, half, :],
                       ACT.Copy).then_inc(dec_o_copied, 1)
                if more:
                    load_cache(1, l, h + 1)
                unit_copy(l, h, 2)
                act.wait_ge(dec_summed, n + 1)
                fn(d_sq[:], d_out[:], ACT.Square).then_inc(dec_sq_ready, 1)
                unit_copy(l, h, 3)
                act.wait_ge(unit_pv, 4 * n + 4)
                fn(o_sq[:].rearrange("p t n -> p (t n)"), PS[:, 7, :], ACT.Square).then_inc(o_sq_ready, 1)
                act.wait_ge(dec_ms_ready, n + 1)
                fn(d_rs[:], PS[:, 3, 0:P], ACT.Ln, bias=eps).then_inc(dec_ln_done, 1)
                act.wait_ge(o_ms_ready, n + 1)
                fn(o_rs, o_ms, ACT.Ln, bias=eps, scale=1.0 / P).then_inc(o_ln_done, 1)
                act.wait_ge(o_ln_done, n + 1)
                fn(o_rs, o_rs, ACT.Exp, scale=-0.5).then_inc(o_rs_ready, 1)
                act.wait_ge(dec_ln_done, n + 1)
                fn(d_rs[:], d_rs[:], ACT.Exp, scale=-0.5).then_inc(dec_rs_ready, 1)
                if more:
                    dec_exps(l, h + 1)
                wait_apart(act, o_t_ready, n + 1)
                fn(a_t[:, h, 0:SEQ], PS[:, 6, :], ACT.Copy, scale=g_sub[:, bass.ds(l, 1)])\
                    .then_inc(a_done, 1)

            def gate_tile(l, n, f, x):
                act.wait_ge(chunk_done[0], n + 1)
                act.wait_ge(branch_taken, x)
                fn(halves(tmp1[:]), pair(0), ACT.Sigmoid).then_inc(gate_ready, 1)

            def window_pair(l, kv, i, p, more):
                n = l * PAIRS + 2 * i + p
                act.wait_ge(swa_max, 2 * n + 1)
                for c in range(8):
                    last = fn(s_p[:, c * P:(c + 1) * P], flat[:, c * P:(c + 1) * P], ACT.Exp,
                              bias=s_nm[:, c:c + 1], accum_out=s_l[:, c:c + 1])
                last.then_inc(swa_exp, 1)
                sink = col[:, bass.ds(C_SINK + l * PAIRS + 2 * i + p, 1)]
                fn(s_e[:, 0:8], s_nm[:, 0:8], ACT.Exp, bias=sink).then_inc(swa_sink_exp, 1)
                act.wait_ge(swa_max, 2 * n + 2)
                for g in range(2):
                    last = fn(s_p[:, 1024 + g * 384:1024 + (g + 1) * 384], PS[:, 2 + g, 0:384], ACT.Exp,
                              bias=s_nm[:, 8 + g:9 + g], accum_out=s_l[:, 8 + g:9 + g])
                last.then_inc(swa_exp, 1)
                fn(s_e[:, 8:10], s_nm[:, 8:10], ACT.Exp, bias=sink).then_inc(swa_sink_exp, 1)
                for q in range(4):
                    act.wait_ge(swa_pt_ready, 4 * n + q + 1)
                    if q == 0:
                        act.wait_ge(swa_pv, 2 * n)
                    k = min(4 * q + 4, 14) - 4 * q
                    fn(s_pt[:, 4 * q:4 * q + k, :].rearrange("p t n -> p (t n)"),
                       PS[:, 6 + q % 2, 0:k * P], ACT.Copy).then_inc(swa_pt_copied, 1)
                    if more and q % 2:
                        pair_swap(l, 2 * i + p + 1, i + p, 1 - p, q // 2)
                for samples, ready in ((True, b_samples_hi_ready), (False, b_hi_ready)):
                    wait_apart(act, swa_pv, 2 * n + (1 if samples else 2))
                    for dst, src in window_outputs(act_b[0], 2 * i + p, samples):
                        last = fn(dst, src, ACT.Copy)
                    last.then_inc(ready, 1)

            eps = col[:, C_EPS:C_EPS + 1]
            act.wait_ge(small_loaded, 16 * SMALL_LOADS)
            act.wait_ge(lam_sum, 1)
            fn(lam2, lam2, ACT.Exp).then_inc(lam_exp, 1)
            for r in range(RT):
                act.wait_ge(x0_loaded[r], 16)
            with act.Fori(0, DEPTH) as l:
                act.wait_ge(ln_aggr, l * (2 * RT))
                load_cache(0, l, 0)
                load_cache(1, l, 0)
                for r in range(RT):
                    x_high(l, 0, r)
                act.wait_ge(input_rows, l * RT + RT)
                act.dma_start(x_all[l].rearrange("(r p) d -> p r d", p=P), rows[:]).then_inc(y_stored, 16)
                for is_k in range(2):
                    swap(l, l * ROPES + is_k, is_k, nth(l, AT_HEAD_0),
                         1.0 if is_k else QK_SCALE, is_k)
                for r in range(RT):
                    act.wait_ge(row_evacuated[r], l * GROUPS + 2)
                act.dma_start(v_out[l], rows[:]).then_inc(v_stored, 16)
                dec_exps(l, 0)
                all_heads(act, l, head)
                act.wait_ge(v_stored, 16 * (l + 1))
                act.dma_start(s_kc[:].rearrange("p a b k -> p (a b k)"), swa_kc[l])\
                    .then_inc(swa_cache_loaded, 16)
                act.dma_start(s_vc[:].rearrange("p t n -> p (t n)"), swa_vc[l])\
                    .then_inc(swa_cache_loaded, 16)
                act.wait_ge(dec_done, HEADS * (l + 1))
                act.wait_ge(a_done, HEADS * (l + 1))
                with act.Fori(0, KT) as k:
                    fn(act_b[0][:, k, :], a_t[:, k, :], ACT.Copy).then_inc(a_hi_ready, 1)
                with act.Fori(0, KT) as f:
                    gate_tile(l, nth(l, AT_BRANCH_A) + f, f, l * 16 + f)
                act.wait_ge(branch_taken, l * 16 + 8)
                swap(l, l * ROPES + 2 * HEADS, 0, nth(l, AT_SWA), 1.0)
                swap(l, l * ROPES + 2 * HEADS + 1, 1, nth(l, AT_SWA), QK_SCALE, 1)
                act.wait_ge(a_lo_ready, KT * (l + 1))
                for kv in range(2):
                    for half in range(2):
                        last = fn(sk_dup[half * DH:(half + 1) * DH, kv, :], sk_t[kv * DH:(kv + 1) * DH, :],
                                  ACT.Copy)
                last.then_inc(swa_k_dup, 1)
                act.wait_ge(chunk_done[0], nth(l, AT_SWA, 1) + 1)
                fn(halves(sv_t[:]), pair(0), ACT.Copy).then_inc(swa_v_copied, 1)
                act.wait_ge(swa_v_copied, l + 1)
                for dst, src in ((swk_out, sk_t), (swv_out, sv_t)):
                    act.dma_start(dst[l], src[:, SEQ - 2 * CHUNK:ROWS]).then_inc(swa_stored, 16)
                act.wait_ge(swa_vt_ready, l + 1)
                fn(sv_rows[:].rearrange("p t n -> p (t n)"), flat[:, 0:1024], ACT.Copy)\
                    .then_inc(swa_v_ready, 1)
                all_pairs(act, l, window_pair)
                act.wait_ge(swa_pv, 2 * PAIRS * (l + 1))
                act.wait_ge(y_stored, 16 * (l + 1))
                act.dma_start(rows[:], x_all[l].rearrange("(r p) d -> p r d", p=P))\
                    .then_inc(x_rows_loaded, 16)
                act.wait_ge(swa_stored, 32 * (l + 1))
                with act.Fori(0, KT) as f:
                    gate_tile(l, nth(l, AT_BRANCH_B) + f, f, l * 16 + 8 + f)
                    wait_apart(act, mix_sum, l * KT + f + 1)
                    fn(act_a[0][:, f, :], tmp2[:], ACT.Copy).then_inc(mix_hi_ready, 1)

                def load_norm(which):
                    act.dma_start(ln_g[:], ln_par[l, which, 0]).then_inc(ln_par_loaded, 16)
                    act.dma_start(ln_b[:], ln_par[l, which, 1]).then_inc(ln_par_loaded, 16)

                def rstds(which, batch):
                    n = 2 * (2 * l + which) + batch
                    tiles = slice(0, 3) if batch == 0 else slice(3, RT)
                    act.wait_ge(ln_aggr, RT * (2 * l + which) + (3, RT)[batch])
                    fn(ln_mv[:, tiles, 2], ln_mv[:, tiles, 1], ACT.Ln, bias=eps).then_inc(ln_log, 1)
                    act.wait_ge(ln_log, n + 1)
                    fn(ln_mv[:, tiles, 3], ln_mv[:, tiles, 2], ACT.Exp, scale=-0.5).then_inc(ln_rstd, 1)

                act.wait_ge(mix_ready, KT * (l + 1))
                load_norm(0)
                for batch, tiles in enumerate((range(3), range(3, RT))):
                    rstds(0, batch)
                    for r in tiles:
                        x_high(l, 1, r)
                load_norm(1)
                with act.Fori(0, FF_PARTS // 2) as i:
                    for p in range(2):
                        hidden = act_b if p == 0 else act_a
                        with act.Fori(0, KT // 2) as u:
                            for s in range(2):
                                t = l * 32 + (2 * i + p) * 8 + 2 * u + s
                                act.wait_ge(chunk_done[s], nth(l, AT_FF) + (2 * i + p) * 8 + u + 1)
                                act.wait_ge(sq_done, t)
                                fn(halves(tmp1[:]), pair(1 - s), ACT.Relu).then_inc(relu_done[s], 1)
                                wait_apart(act, sq_done, t + 1)
                                fn(hidden[0][:, 2 * u + s, :], tmp2[:], ACT.Copy).then_inc(h_hi_ready, 1)
                for batch in range(2):
                    rstds(1, batch)
            act.wait_ge(input_rows, (DEPTH + 1) * RT)
            act.dma_start(x_all[DEPTH].rearrange("(r p) d -> p r d", p=P), rows[:]).then_inc(y_stored, 16)
            act.wait_ge(y_stored, 16 * (DEPTH + 1))
            act.wait_ge(v_stored, 16 * DEPTH)
            act.wait_ge(swa_stored, 32 * DEPTH)
            for p in range(2):
                act.wait_ge(k_stored[p], 16 * DEPTH * HEADS // 2)

        @block.vector
        def _(dve):
            v = nc.vector

            def rotate(l, u, s, n, scale, adds, before_adds=None, which=0, apart=False,
                       signal_add=None):
                dve.wait_ge(rope_added, u)
                for half in range(2) if apart else (1,):
                    dve.wait_ge((chunk_half_done, chunk_done)[half][s], n + 1)
                    dve.wait_ge(rope_swapped, 2 * u + half + 1)
                    if apart:
                        c = slice(half * HALF, (half + 1) * HALF)
                        v.scalar_tensor_tensor(rope_c[:, c], PS[:, bank_of(which, half), 0:HALF], scale,
                                               cos[:, c], ALU.mult, ALU.mult).then_inc(rope_cos_done, 1)
                        v.tensor_tensor(rope_s[:, c], rope_s[:, c], sin[:, c], ALU.mult)\
                            .then_inc(rope_sin_done, 1)
                    else:
                        v.scalar_tensor_tensor(halves(rope_c[:]), pair(which), scale, halves(cos[:]),
                                               ALU.mult, ALU.mult).then_inc(rope_cos_done, 2)
                        v.tensor_tensor(rope_s[:], rope_s[:], sin[:], ALU.mult).then_inc(rope_sin_done, 2)
                if before_adds:
                    before_adds()
                dve.wait_ge(rope_cos_done, 2 * u + 2)
                dve.wait_ge(rope_sin_done, 2 * u + 2)
                for i, (out, parts, shape_cols) in enumerate(adds):
                    last = v.tensor_tensor(out, shape_cols(rope_c[parts]), shape_cols(rope_s[parts]),
                                           ALU.add)
                    if i == signal_add:
                        last.then_inc(pair_q_added, 1)
                last.then_inc(rope_added, 1)

            LOW, HIGH = slice(0, DH), slice(DH, P)

            def rotate_q(l, h, p, at_chunk=AT_HEADS):
                def samples(g, split):
                    cs = slice(SEQ + g * DH, SEQ + (g + 1) * DH)
                    if split:
                        return lambda t: t[:, cs].rearrange("p (b q) -> p b q", b=4)
                    return lambda t: t[:, cs]

                adds = [(z_map[p][0][LOW, :], LOW, lambda t: t[:, 0:SEQ]),
                        (z_map[p][1][HIGH, :], HIGH, lambda t: t[:, 0:SEQ])]
                for g in range(2):
                    for m, parts in ((0, LOW), (1, HIGH)):
                        side = (m ^ g) * DH
                        adds.append((z_all[parts, g, side:side + DH], parts, samples(g, False)))
                        first = g * 4 * P + side
                        own = z_dec[parts, first:first + 4 * (P + DEC_T)]\
                            .rearrange("p (b c) -> p b c", b=4)[:, :, 0:DEC_T]
                        adds.append((own, parts, samples(g, True)))
                rotate(l, l * ROPES + 2 * h, 0, nth(l, at_chunk) + h, QK_SCALE, adds,
                       lambda: dve.wait_ge(dec_scores, 2 * (l * HEADS + h)),
                       apart=at_chunk != AT_HEAD_0)

            def rotate_k(l, h, p, nth_use, at_chunk=AT_HEADS, which=0):
                rotate(l, l * ROPES + 2 * h + 1, 1, nth(l, at_chunk) + h, 1.0,
                       [(k_t[p][:], slice(0, P), lambda t: t[:])],
                       lambda: dve.wait_ge(k_stored[p], 16 * nth_use), which)

            def unit_maxes(l, h, i):
                n, w = 4 * (l * HEADS + h) + i, (i + 1) * P
                dve.wait_ge(unit_scores, n + 1)
                two = PS[:, 2 * (i % 2):2 * (i % 2) + 2, 0:w]
                v.tensor_reduce(u_nm[i % 2], two, AX_X, ALU.max, negate=True).then_inc(unit_max, 1)

            def unit_combine(l, h, i):
                n, w = 4 * (l * HEADS + h) + i, (i + 1) * P
                dve.wait_ge(unit_exp, n + 1)
                dve.wait_ge(unit_probs, n)
                v.reciprocal(u_r, u_l[i % 2]).then_inc(unit_recip, 1)
                dve.wait_ge(unit_recip, n + 1)
                v.tensor_tensor(u_r[:, 1:2], u_r[:, 1:2], neg_lam[:, bass.ds(l, 1)], ALU.mult)\
                    .then_inc(unit_r_ready, 1)
                dve.wait_ge(unit_r_ready, n + 1)
                v.tensor_scalar(u_p[i % 2][:, 1, 0:w], u_p[i % 2][:, 1, 0:w], u_r[:, 1:2], None, ALU.mult)\
                    .then_inc(unit_second, 1)
                dve.wait_ge(unit_second, n + 1)
                dve.wait_ge(unit_t_ready, 4 * (l * HEADS + h) + max(0, i - 1))
                v.scalar_tensor_tensor(u_a[i % 2][:, 0:w], u_p[i % 2][:, 0, 0:w], u_r[:, 0:1],
                                       u_p[i % 2][:, 1, 0:w], ALU.mult, ALU.add).then_inc(unit_probs, 1)

            def head(l, h, p, more, next_uses):
                n = l * HEADS + h
                for g in range(2):
                    dve.wait_ge(dec_scores, 2 * n + g + 1)
                    v.tensor_reduce(d_nm[:, g:g + 1], flat[:, 1024 * g:1024 * g + ROWS], AX_X, ALU.max,
                                    negate=True).then_inc(dec_max, 1)
                dve.wait_ge(dec_exp, 2 * n + 2)
                v.reciprocal(d_r, d_l).then_inc(dec_recip, 1)
                dve.wait_ge(dec_recip, n + 1)
                for g, parts in ((0, HIGH), (1, LOW)):
                    last = v.tensor_tensor(d_r[parts, g:g + 1], d_r[parts, g:g + 1],
                                           neg_lam[parts, bass.ds(l, 1)], ALU.mult)
                last.then_inc(dec_r_ready, 1)
                dve.wait_ge(dec_shifted, n + 1)
                dve.wait_ge(o_t_ready, n)
                for g, parts in ((0, LOW), (1, HIGH)):
                    v.scalar_tensor_tensor(d_a[parts], d_p[parts, g, :], d_r[parts, g:g + 1], d_t[parts],
                                           ALU.mult, ALU.add).then_inc(dec_probs, 1)
                if more:
                    rotate_q(l, h + 1, 1 - p)
                unit_maxes(l, h, 0)
                unit_maxes(l, h, 1)
                unit_combine(l, h, 0)
                unit_combine(l, h, 1)
                unit_maxes(l, h, 2)
                unit_maxes(l, h, 3)
                if more:
                    rotate_k(l, h + 1, 1 - p, next_uses)
                unit_combine(l, h, 2)
                unit_combine(l, h, 3)
                dve.wait_ge(dec_ot_ready, n + 1)
                own = flat[:, 0:DEC_B * (P + DEC_T)].rearrange("p (b c) -> p b c", b=DEC_B)[:, :, 0:DEC_T]
                v.tensor_tensor(d_out[:].rearrange("p (b t) -> p b t", b=DEC_B), own,
                                d_on[:].rearrange("p (b t) -> p b t", b=DEC_B), ALU.add)\
                    .then_inc(dec_summed, 1)
                dve.wait_ge(o_sq_ready, n + 1)
                v.tensor_reduce(o_ms, o_sq[:], AX_X, ALU.add).then_inc(o_ms_ready, 1)
                dve.wait_ge(o_rs_ready, n + 1)
                dve.wait_ge(dec_t_ready, 2 * n + 2)
                v.tensor_tensor(o_n[:], PS[:, 7, :].rearrange("p (i e) -> p i e", i=4),
                                o_rs.unsqueeze(2).to_broadcast([P, 4, P]), ALU.mult)\
                    .then_inc(o_n_ready, 1)
                dve.wait_ge(dec_rs_ready, n + 1)
                v.scalar_tensor_tensor(a_t[:, h, SEQ:ROWS], d_out[:], g_sub[:, bass.ds(l, 1)], d_rs[:],
                                       ALU.mult, ALU.mult).then_inc(dec_done, 1)

            def branch_tile(l, at_chunk, f, x, out):
                dve.wait_ge(gate_ready, x + 1)
                dve.wait_ge(chunk_done[1], nth(l, at_chunk) + f + 1)
                v.tensor_tensor(halves(out), pair(1), halves(tmp1[:]), ALU.mult).then_inc(branch_taken, 1)

            def window_pair(l, kv, i, p, more):
                n = l * PAIRS + 2 * i + p
                sink = col[:, bass.ds(C_SINK + l * PAIRS + 2 * i + p, 1)]
                for part, (units, scores) in enumerate((
                        (slice(0, 8), flat[:, 0:1024].rearrange("p (c k) -> p c k", c=8)),
                        (slice(8, 10), PS[:, 2:4, 0:384]))):
                    dve.wait_ge(swa_scores, 2 * n + part + 1)
                    v.tensor_reduce(s_nm[:, units], scores, AX_X, ALU.max).then_inc(swa_row_max, 1)
                    dve.wait_ge(swa_row_max, 2 * n + part + 1)
                    v.tensor_scalar(s_nm[:, units], s_nm[:, units], sink, -1.0, ALU.max, ALU.mult)\
                        .then_inc(swa_max, 1)
                for part, (units, probs) in enumerate((
                        (slice(0, 8), s_p[:, 0:8 * P].rearrange("p (c k) -> p c k", c=8)),
                        (slice(8, 10), s_p[:, 8 * P:].rearrange("p (g k) -> p g k", g=2)))):
                    x = 2 * n + part + 1
                    dve.wait_ge(swa_exp, x)
                    dve.wait_ge(swa_sink_exp, x)
                    v.tensor_tensor(s_l[:, units], s_l[:, units], s_e[:, units], ALU.add)\
                        .then_inc(swa_sum, 1)
                    dve.wait_ge(swa_sum, x)
                    v.reciprocal(s_l[:, units], s_l[:, units]).then_inc(swa_recip, 1)
                    dve.wait_ge(swa_recip, x)
                    v.tensor_tensor(probs, probs, s_l[:, units].unsqueeze(2).to_broadcast(probs.shape),
                                    ALU.mult).then_inc(swa_scaled, 1)
                if more:
                    rotate_pair(l, i + p, 1 - p)
                for samples, hi_ready, lo_ready in ((True, b_samples_hi_ready, b_samples_lo_ready),
                                                    (False, b_hi_ready, b_lo_ready)):
                    dve.wait_ge(hi_ready, n + 1)
                    for (lo, src), (hi, _) in zip(window_outputs(act_b[1], 2 * i + p, samples),
                                                  window_outputs(act_b[0].bitcast(F32), 2 * i + p, samples)):
                        last = v.tensor_tensor(lo, src, hi, ALU.subtract)
                    last.then_inc(lo_ready, 1)

            def rotate_pair(l, i, p, first=False):
                adds = []
                for g, parts in ((0, LOW), (1, HIGH)):
                    adds.append((zq[p][parts, :, g, :], parts,
                                 lambda t: t[:, 0:SEQ].rearrange("p (c q) -> p c q", q=CHUNK)))
                for g, parts in ((0, LOW), (1, HIGH)):
                    adds.append((zs[p][parts, :, g * DH:(g + 1) * DH], parts,
                                 lambda t: t[:, SEQ:ROWS].rearrange("p (g q) -> p g q", g=2)))
                if first:
                    rotate(l, l * ROPES + 2 * HEADS + 1, 1, nth(l, AT_SWA), QK_SCALE, adds, which=1,
                           signal_add=1)
                else:
                    rotate(l, l * ROPES + (2 * HEADS + 1) + 2 * i + p, p, nth(l, AT_SWA, 1) + i, QK_SCALE,
                           adds, apart=True, signal_add=1)

            def x_low(l, which, r):
                n = tiles_before(l, which) + r
                dve.wait_ge(x_hi_ready, n + 1)
                c = slice(r * P, (r + 1) * P)
                v.tensor_tensor(xt_lo[:, :, c], transposed_tile(r), xt_hi[:, :, c].bitcast(F32),
                                ALU.subtract).then_inc(x_lo_ready, 1)

            def take(group, n, r, out, residual=None):
                if r < RT - 1:
                    dve.wait_ge(row_acc_ready, group * (RT - 1) + r + 1)
                else:
                    dve.wait_ge(chunk_done[1], n)
                if residual is None:
                    v.tensor_copy(out, PS[:, r, :]).then_inc(row_evacuated[r], 1)
                else:
                    v.scalar_tensor_tensor(out, out, residual, PS[:, r, :], ALU.mult, ALU.add)\
                        .then_inc(row_evacuated[r], 1)

            def statistics(group, r, half, out):
                wait_apart(dve, row_evacuated[r], group + 1)
                v.bn_stats(ln_st[:, r, half, :], out).then_inc(ln_stats, 1)

            def take_group(group, n, half, residual=None):
                for r in range(RT):
                    take(group, n, r, half_rows(half)(r), residual)
                if residual is not None:
                    for r in range(RT):
                        statistics(group, r, half, half_rows(half)(r))

            def take_and_normalise(l, which, group, n, residual):
                x0 = l * (2 * RT) + which * RT
                stats0 = RT * (l * (GROUPS - 2) + (1 if which == 0 else GROUPS - 3))

                def take_tile(r):
                    take(group, n, r, half_rows(1)(r), residual)
                    statistics(group, r, 1, half_rows(1)(r))
                    wait_apart(dve, ln_stats, stats0 + r + 1)
                    v.bn_aggr(ln_mv[:, r, 0:2], ln_st[:, r].rearrange("p a b -> p (a b)"))\
                        .then_inc(ln_aggr, 1)

                def centre(r):
                    dve.wait_ge(ln_par_loaded, 32 * (2 * l + which + 1))
                    dve.wait_ge(ln_aggr, x0 + r + 1)
                    v.scalar_tensor_tensor(rows[:, r, :], rows[:, r, :], ln_mv[:, r, 0:1], ln_g[:],
                                           ALU.subtract, ALU.mult).then_inc(ln_centred, 1)

                def finish(r):
                    dve.wait_ge(ln_centred, x0 + r + 1)
                    dve.wait_ge(ln_rstd, 2 * (2 * l + which) + (1 if r < 3 else 2))
                    v.scalar_tensor_tensor(rows[:, r, :], rows[:, r, :], ln_mv[:, r, 3:4], ln_b[:],
                                           ALU.mult, ALU.add).then_inc(input_rows if which else ln_rows, 1)

                for step, r in ((take_tile, 0), (take_tile, 1), (take_tile, 2), (centre, 0), (centre, 1),
                                (take_tile, 3), (finish, 0), (finish, 1), (take_tile, 4), (centre, 2),
                                (finish, 2)):
                    step(r)
                if which == 0:
                    for r in range(3):
                        x_low(l, 1, r)
                for r in range(3, RT):
                    centre(r)
                    finish(r)
                if which == 0:
                    for r in range(3, RT):
                        x_low(l, 1, r)

            def half_rows(h):
                return lambda r: rows[:, r, bass.ts(h, BANK)]

            v.memset(mask_cols[:], 0.0).then_inc(masks_ready, 1)
            dve.wait_ge(small_loaded, 16 * SMALL_LOADS)
            dve.wait_ge(masks_ready, 1)
            v.tensor_copy(mask_cols[0:DEC_B, :], mask_f[0:DEC_B, :]).then_inc(masks_ready, 1)
            prod = tmp1[:, 0:2 * DEPTH * DH].rearrange("p (a l d) -> p a l d", a=2, l=DEPTH)
            for a in range(2):
                last = v.tensor_tensor(prod[:, a], lam_v[:, :, 2 * a, :], lam_v[:, :, 2 * a + 1, :],
                                       ALU.mult)
            last.then_inc(lam_link, 1)
            dve.wait_ge(lam_link, 1)
            v.tensor_reduce(lam2, prod.rearrange("p a l d -> p (a l) d"), AX_X, ALU.add)\
                .then_inc(lam_sum, 1)
            dve.wait_ge(lam_exp, 1)
            v.tensor_tensor(neg_lam[:], lam2[:, DEPTH:2 * DEPTH], lam2[:, 0:DEPTH], ALU.subtract)\
                .then_inc(lam_link, 1)
            dve.wait_ge(lam_link, 2)
            v.tensor_tensor(neg_lam[:], neg_lam[:], col[:, C_LAM_INIT:C_LAM_INIT + DEPTH], ALU.subtract)
            v.tensor_tensor(g_sub[:], col[:, C_SUBLN:C_SUBLN + DEPTH],
                            col[:, C_ONE_MINUS:C_ONE_MINUS + DEPTH], ALU.mult).then_inc(lam_link, 1)
            dve.wait_ge(lam_link, 3)
            dve.wait_ge(masks_ready, 2)
            for r in range(RT):
                dve.wait_ge(x0_loaded[r], 16)
                dve.sem_inc(input_rows, 1)
            with dve.Fori(0, DEPTH) as l:
                for r in range(RT):
                    x_low(l, 0, r)
                dve.wait_ge(input_rows, l * RT + RT)
                for p in range(2):
                    v.memset(z_map[p][0][HIGH, :], 0.0)
                    v.memset(z_map[p][1][LOW, :], 0.0)
                v.memset(z_all[:], 0.0)
                v.memset(z_dec[:], 0.0).then_inc(z_zeroed, 1)
                dve.wait_ge(z_zeroed, l + 1)
                dve.wait_ge(consts_loaded, 16 * CONST_LOADS)
                rotate_q(l, 0, 0, AT_HEAD_0)
                rotate_k(l, 0, 0, l * (HEADS // 2), AT_HEAD_0, 1)
                wait_apart(dve, y_stored, 16 * (l + 1))
                with dve.Fori(0, 2) as half:
                    take_group(l * GROUPS + half, nth(l, AT_V) + 2 * half + 2, half)
                with dve.Fori(0, HEADS // 2 - 1) as i:
                    for p in range(2):
                        head(l, 2 * i + p, p, True, l * (HEADS // 2) + i + p)
                head(l, HEADS - 2, 0, True, l * (HEADS // 2) + HEADS // 2 - 1)
                head(l, HEADS - 1, 1, False, None)
                dve.wait_ge(a_done, HEADS * (l + 1))
                wait_apart(dve, dec_done, HEADS * (l + 1))
                with dve.Fori(0, KT) as k:
                    dve.wait_ge(a_hi_ready, l * KT + k + 1)
                    v.tensor_tensor(act_b[1][:, k, :], a_t[:, k, :], act_b[0][:, k, :].bitcast(F32),
                                    ALU.subtract).then_inc(a_lo_ready, 1)
                with dve.Fori(0, KT) as f:
                    branch_tile(l, AT_BRANCH_A, f, l * 16 + f, mix_a[:, f, :])
                dve.wait_ge(a_lo_ready, KT * (l + 1))
                for p in range(2):
                    v.memset(zq[p][:], 0.0)
                    last = v.memset(zs[p][:], 0.0)
                last.then_inc(swa_zeroed, 1)
                rotate(l, l * ROPES + 2 * HEADS, 0, nth(l, AT_SWA), 1.0,
                       [(sk_t[:], slice(0, P), lambda t: t[:])])
                dve.wait_ge(swa_zeroed, l + 1)
                rotate_pair(l, 0, 0, True)
                all_pairs(dve, l, window_pair)
                dve.wait_ge(swa_stored, 32 * (l + 1))
                wait_apart(dve, rope_added, l * ROPES + ROPES)
                with dve.Fori(0, KT) as f:
                    n = l * KT + f
                    dve.wait_ge(mix_ready, n)
                    branch_tile(l, AT_BRANCH_B, f, l * 16 + 8 + f, tmp2[:])
                    dve.wait_ge(branch_taken, l * 16 + 8 + f + 1)
                    v.tensor_tensor(tmp2[:], tmp2[:], mix_a[:, f, :], ALU.add).then_inc(mix_sum, 1)
                    dve.wait_ge(mix_hi_ready, n + 1)
                    v.tensor_tensor(act_a[1][:, f, :], tmp2[:], act_a[0][:, f, :].bitcast(F32),
                                    ALU.subtract).then_inc(mix_ready, 1)
                wait_apart(dve, x_rows_loaded, 16 * (l + 1))
                take_group(l * GROUPS + 2, nth(l, AT_O) + 2, 0, ALPHA)
                take_and_normalise(l, 0, l * GROUPS + 3, nth(l, AT_O) + 4, ALPHA)
                for part in range(FF_PARTS):
                    hidden = act_b if part % 2 == 0 else act_a
                    with dve.Fori(0, KT // 2) as u:
                        for s in range(2):
                            t = l * 32 + part * 8 + 2 * u + s
                            dve.wait_ge(relu_done[s], l * 16 + part * 4 + u + 1)
                            dve.wait_ge(h_ready, t)
                            v.tensor_tensor(tmp2[:], tmp1[:], tmp1[:], ALU.mult).then_inc(sq_done, 1)
                            dve.wait_ge(h_hi_ready, t + 1)
                            v.tensor_tensor(hidden[1][:, 2 * u + s, :], tmp2[:],
                                            hidden[0][:, 2 * u + s, :].bitcast(F32), ALU.subtract)\
                                .then_inc(h_ready, 1)
                    dve.wait_ge(ln_stats, RT * (l * (GROUPS - 2) + 2 + 2 * part))
                    wait_apart(dve, ln_rows, RT * (l + 1))
                    group, n = l * GROUPS + 4 + 2 * part, nth(l, AT_FF) + 8 * part + 6
                    if part < FF_PARTS - 1:
                        with dve.Fori(0, 2) as half:
                            take_group(group + half, n + 2 * half, half, ALPHA if part == 0 else 1.0)
                    else:
                        take_group(group, n, 0, 1.0)
                        take_and_normalise(l, 1, group + 1, n + 2, 1.0)


def stream(w_in, w_a, w_b, w_o, w_up, w_down):
    import numpy as np

    def feature_tiles(w, tiles):
        t = w.reshape(KT, P, -1, P).transpose(2, 1, 0, 3).reshape(-1, P, D)
        return [t[f] for f in tiles]

    def row_form(w):
        t = w.reshape(KT // 2, 2, P, 2, BANK).transpose(3, 0, 2, 1, 4).reshape(-1, P, D)
        return list(t)

    out = []
    for l in range(DEPTH):
        q, k, v = (w_in[l][:, i * D:(i + 1) * D] for i in range(3))
        rest = w_in[l][:, 3 * D:]
        sq, sk, sv = rest[:, 0:D], rest[:, D:D + P], rest[:, D + P:D + 2 * P]
        ga, gb = rest[:, D + 2 * P:2 * D + 2 * P], rest[:, 2 * D + 2 * P:]
        for h in range(HEADS):
            out += feature_tiles(q, [h]) + feature_tiles(k, [h])
            if h == 0:
                out += row_form(v)
        for f in range(KT):
            out += feature_tiles(ga, [f]) + feature_tiles(w_a[l], [f])
        out += (feature_tiles(sk, [0]) + feature_tiles(sq, [0]) + feature_tiles(sv, [0])
                + feature_tiles(sq, range(1, PAIRS)))
        for f in range(KT):
            out += feature_tiles(gb, [f]) + feature_tiles(w_b[l], [f])
        out += row_form(w_o[l])
        for part in range(FF_PARTS):
            out += feature_tiles(w_up[l], range(part * KT, (part + 1) * KT))
            out += row_form(w_down[l][part * D:(part + 1) * D])
    return np.ascontiguousarray(np.stack(out))


def tables():
    import math

    import numpy as np

    half = DH // 2
    inv = (np.float32(10000.0) ** (-np.arange(half, dtype=np.float32) / np.float32(half))).astype(np.float32)
    pos = np.concatenate([np.arange(SEQ), np.tile(PAST + np.arange(DEC_T), DEC_B)]).astype(np.float32)
    ang = (inv[:, None] * pos[None, :]).astype(np.float32)
    cos = np.tile(np.cos(ang), (4, 1)).astype(np.float32)
    sin = np.sin(ang).astype(np.float32)
    sin = np.tile(np.concatenate([-sin, sin]), (2, 1)).astype(np.float32)
    row = np.arange(P)
    m = np.zeros((DEC_B, MASK_COLS), np.float32)
    m[0, 0:CHUNK] = 1.0
    m[0, P:2 * P] = 1.0
    for g in range(2):
        for b in range(DEC_B):
            m[b, 2 * P + g * P:2 * P + (g + 1) * P] = 4 * g + (row % 64) // DEC_T != b
    at = 4 * P
    m[0, at:at + 64] = NEG
    at += 64
    for b in range(DEC_B):
        m[b, at + b * DEC_T:at + (b + 1) * DEC_T] = NEG
    at += P
    for g in range(2):
        for b in range(4):
            m[4 * g + b, at + 256 * g + 64 * b:at + 256 * g + 64 * (b + 1)] = NEG
    lam_init = [0.8 - 0.6 * math.exp(-0.3 * l) for l in range(DEPTH)]
    return (cos, sin, np.eye(P, dtype=np.float32), np.full((P, P), 1.0 / P, np.float32),
            m, lam_init)


def kernel(x_prompt, x_sample, cache_diff_k, cache_diff_v, cache_swa_k, cache_swa_v, w_in,
           diff_lambda_q1, diff_lambda_k1, diff_lambda_q2, diff_lambda_k2, diff_subln_g, swa_sinks,
           w_branch_a, w_branch_b, w_o, ln1_g, ln1_b, w_up, w_down, ln2_g, ln2_b):
    import numpy as np
    import concourse.bacc as bacc
    from concourse.bass_utils import run_bass_kernel_spmd

    c = np.ascontiguousarray
    x = np.concatenate([x_prompt.reshape(SEQ, D), x_sample.reshape(DEC_B * DEC_T, D)])
    k = cache_diff_k.transpose(0, 3, 4, 5, 1, 2).reshape(DEPTH, HEADS, P, DEC_B * PAST)
    v = cache_diff_v.reshape(DEPTH, DEC_B, 4, P, HEADS, P).transpose(0, 4, 3, 2, 1, 5)
    sk = cache_swa_k[:, :, CHUNK:].transpose(0, 4, 3, 1, 2).reshape(DEPTH, DH, 2 * DEC_B * 64)
    sk = np.concatenate([sk, sk], axis=1)
    sv = cache_swa_v[:, :, CHUNK:].reshape(DEPTH, 4, P, P).transpose(0, 2, 1, 3)
    cos, sin, ident, ones, masks, lam_init = tables()
    cols = np.zeros((P, C_END), np.float32)
    for l in range(DEPTH):
        cols[:, C_LAM_INIT + l] = lam_init[l]
        cols[:, C_ONE_MINUS + l] = 1.0 - lam_init[l]
        cols[:, C_SUBLN + l] = diff_subln_g[l]
        for j in range(PAIRS):
            cols[0:64, C_SINK + l * PAIRS + j] = swa_sinks[l, 2 * j]
            cols[64:128, C_SINK + l * PAIRS + j] = swa_sinks[l, 2 * j + 1]
    cols[:, C_EPS] = EPS
    lam = np.stack([diff_lambda_q1, diff_lambda_k1, diff_lambda_q2, diff_lambda_k2], axis=1)
    lam = np.broadcast_to(lam.reshape(1, -1), (P, DEPTH * 4 * DH))
    ln = np.stack([ln1_g, ln1_b, ln2_g, ln2_b], axis=1).reshape(DEPTH, 2, 2, 1, D)
    ln = np.broadcast_to(ln, (DEPTH, 2, 2, P, D))
    keep = CHUNK * 2 - DEC_T
    arrays = {
        "x_rows": x,
        "k_cache": k, "v_cache": v.reshape(DEPTH, HEADS, P, 4 * D),
        "swa_kc": sk, "swa_vc": sv.reshape(DEPTH, P, 4 * P),
        "swa_k_keep": cache_swa_k[:, :, DEC_T:].reshape(DEPTH * DEC_B, keep * P),
        "swa_v_keep": cache_swa_v[:, :, DEC_T:].reshape(DEPTH * DEC_B, keep * P),
        "weights": stream(w_in, w_branch_a, w_branch_b, w_o, w_up, w_down),
        "cols": cols, "lam_vec": lam, "ln_par": ln, "cos_t": cos, "sin_t": sin, "ident_d": ident,
        "ones_d": ones, "masks": masks,
    }
    arrays = {"in_" + n: c(a) for n, a in arrays.items()}
    outs = {
        "x_all": [DEPTH + 1, ROWS, D], "k_out": [DEPTH, HEADS, P, ROWS],
        "v_out": [DEPTH, P, RT, D], "swk_out": [DEPTH, P, 2 * P], "swv_out": [DEPTH, P, 2 * P],
        "swk_keep_out": [DEPTH * DEC_B, keep * P], "swv_keep_out": [DEPTH * DEC_B, keep * P],
    }
    nc = bacc.Bacc("TRN2", target_bir_lowering=False, num_devices=1)
    args = [nc.dram_tensor(n, a.shape, mybir.dt.from_np(a.dtype), kind="ExternalInput").ap()
            for n, a in arrays.items()]
    args += [nc.dram_tensor(n, s, F32, kind="ExternalOutput").ap() for n, s in outs.items()]
    build(nc, *args)
    got = run_bass_kernel_spmd(nc, [arrays], core_ids=[0]).results[0]

    y = got["x_all"][DEPTH]
    ko, vo = got["k_out"], got["v_out"].transpose(0, 2, 1, 3).reshape(DEPTH, ROWS, HEADS, P)
    ko = ko.reshape(DEPTH, HEADS, 2, DH, ROWS).transpose(0, 4, 1, 2, 3)

    def window(new, kept):
        new = new.transpose(0, 2, 1).reshape(DEPTH, 2 * P, 2, DH)
        kept = kept.reshape(DEPTH, DEC_B, keep, 2, DH)
        fresh = new[:, P:].reshape(DEPTH, DEC_B, DEC_T, 2, DH)
        return c(new[:, None, 0:P]), c(np.concatenate([kept, fresh], axis=2))

    skp, sks = window(got["swk_out"], got["swk_keep_out"])
    svp, svs = window(got["swv_out"], got["swv_keep_out"])
    return (c(y[:SEQ].reshape(1, SEQ, D)), c(y[SEQ:].reshape(DEC_B, DEC_T, D)),
            c(ko[:, None, :SEQ]), c(vo[:, None, :SEQ]), skp, svp,
            c(ko[:, SEQ:].reshape(DEPTH, DEC_B, DEC_T, HEADS, 2, DH)),
            c(vo[:, SEQ:].reshape(DEPTH, DEC_B, DEC_T, HEADS, P)), sks, svs)
```
